# Optimizing a Trainium2 kernel written in Bass

```python
import jax
import jax.numpy as jnp
from jax import lax
import numpy as np

D_MODEL = 1024
BATCH = 1
SEQ = 256
DEPTH = 2

CTX_LEN = 256
GRID_W = 64
CHUNK = 128
BRANCH_W = 512
N_BRANCH = 3
N_HEADS_RWKV = 8
HEAD_DIM_RWKV = BRANCH_W // N_HEADS_RWKV
DECAY_LORA = 64
AAA_LORA = 64
MV_LORA = 32
GATE_LORA = 128
N_HEADS_RET = 4
HEAD_DIM_RET = BRANCH_W // N_HEADS_RET
N_HEADS_HGRN = 4
HEAD_DIM_HGRN = BRANCH_W // N_HEADS_HGRN
D_FF = 4 * D_MODEL
ROPE_BASE = 10000.0
NORM_EPS = 1e-6
RWKV_LN_EPS = 64e-5
L2_EPS = 1e-12

RWKV_SIZES = (BRANCH_W, BRANCH_W, BRANCH_W, DECAY_LORA, DECAY_LORA, AAA_LORA, AAA_LORA, GATE_LORA)
N_RWKV_IN = 3 * BRANCH_W + 2 * DECAY_LORA + 2 * AAA_LORA + GATE_LORA
N_RET_IN = 4 * BRANCH_W
N_HGRN_IN = 5 * BRANCH_W
N_GATE_IN = N_BRANCH * D_MODEL
N_IN = N_RWKV_IN + N_RET_IN + N_HGRN_IN + N_GATE_IN

kernel_name = 'hybrid_rwkv7_retnet_hgrn2_prefix_dit'

def split_sizes(a, sizes):
    idx, acc = [], 0
    for s in sizes[:-1]:
        acc += s
        idx.append(acc)
    return jnp.split(a, idx, axis=-1)

def rms_norm(x, w=None):
    xf = x.astype(jnp.float32)
    y = xf * lax.rsqrt(jnp.mean(xf * xf, axis=-1, keepdims=True) + NORM_EPS)
    if w is not None:
        y = y * w.astype(jnp.float32)
    return y.astype(x.dtype)

def heads(a, n_heads):
    B, N, C = a.shape
    return a.reshape(B, N, n_heads, C // n_heads).transpose(0, 2, 1, 3)

def merge_heads(a):
    B, H, N, Dh = a.shape
    return a.transpose(0, 2, 1, 3).reshape(B, N, H * Dh)

def nbr_mean_seq(p):
    pp = jnp.pad(p, ((0, 0), (1, 1), (0, 0)))
    return 0.5 * (pp[:, :-2] + pp[:, 2:])

def nbr_mean_grid(p):
    B, T, C = p.shape
    rows = T // GRID_W
    g = jnp.pad(p.reshape(B, rows, GRID_W, C), ((0, 0), (1, 1), (1, 1), (0, 0)))
    m = 0.25 * (g[:, :-2, 1:-1] + g[:, 2:, 1:-1] + g[:, 1:-1, :-2] + g[:, 1:-1, 2:])
    return m.reshape(B, T, C)

def rope(x, pos):
    half = x.shape[-1] // 2
    inv_freq = ROPE_BASE ** (-jnp.arange(half, dtype=jnp.float32) / half)
    ang = pos.astype(jnp.float32)[:, None] * inv_freq[None, :]
    cos, sin = jnp.cos(ang).astype(x.dtype), jnp.sin(ang).astype(x.dtype)
    x1, x2 = x[..., :half], x[..., half:]
    return jnp.concatenate([x1 * cos - x2 * sin, x1 * sin + x2 * cos], axis=-1)

def chunk_linear_scan(q, k, v, log_f, s0):
    dt = q.dtype
    B, H, N, _ = q.shape
    n_blocks = N // CHUNK
    f32 = jnp.float32

    def blocks(a):
        return jnp.moveaxis(a.astype(f32).reshape(B, H, n_blocks, CHUNK, a.shape[-1]), 2, 0)

    lower = jnp.tril(jnp.ones((CHUNK, CHUNK), dtype=bool))[:, :, None]

    def step(S, blk):
        qc, kc, vc, gc = blk
        G = jnp.cumsum(gc, axis=2)
        rel = jnp.where(lower, G[:, :, :, None, :] - G[:, :, None, :, :], -jnp.inf)
        if gc.shape[-1] == 1:
            A = jnp.einsum('bhtd,bhsd->bhts', qc, kc) * jnp.exp(rel[..., 0])
        else:
            A = jnp.einsum('bhtd,bhsd,bhtsd->bhts', qc, kc, jnp.exp(rel))
        o = A @ vc + (qc * jnp.exp(G)) @ S
        G_end = G[:, :, -1:, :]
        S = jnp.exp(G_end).swapaxes(-1, -2) * S + (kc * jnp.exp(G_end - G)).swapaxes(-1, -2) @ vc
        return S, o

    S, o = lax.scan(step, s0.astype(f32), (blocks(q), blocks(k), blocks(v), blocks(log_f)))
    return jnp.moveaxis(o, 0, 2).reshape(B, H, N, -1).astype(dt), S

def rwkv7_scan(r, log_w, k, v, kk, a, s0):
    dt = r.dtype
    f32 = jnp.float32

    def step(S, inp):
        r_t, lw_t, k_t, v_t, kk_t, a_t = inp
        s_kk = jnp.einsum('bhvk,bhk->bhv', S, kk_t)
        S = (S * jnp.exp(lw_t)[:, :, None, :]
             - s_kk[..., None] * (a_t * kk_t)[:, :, None, :]
             + v_t[..., None] * k_t[:, :, None, :])
        return S, jnp.einsum('bhvk,bhk->bhv', S, r_t)

    xs = tuple(jnp.moveaxis(t.astype(f32), 2, 0) for t in (r, log_w, k, v, kk, a))
    S, o = lax.scan(step, s0.astype(f32), xs)
    return jnp.moveaxis(o, 0, 2).astype(dt), S

def bidir_prefix(scan_fn, fwd, bwd, s0, n_ctx):
    cf = tuple(a[:, :, :n_ctx] for a in fwd)
    lf = tuple(a[:, :, n_ctx:] for a in fwd)
    cb = tuple(jnp.flip(a[:, :, :n_ctx], axis=2) for a in bwd)
    lb = tuple(jnp.flip(a[:, :, n_ctx:], axis=2) for a in bwd)
    o_cf, s_cf = scan_fn(*cf, s0)
    o_lf, _ = scan_fn(*lf, s_cf)
    o_cb, s_cb = scan_fn(*cb, s0)
    o_lb, _ = scan_fn(*lb, s_cb)
    return jnp.concatenate([o_cf + jnp.flip(o_cb, axis=2), o_lf + jnp.flip(o_lb, axis=2)], axis=2)

def rwkv7_mixer(p, h, v_first, vres, n_ctx, mu, w0, w_up, a0, a_up, g_up, k_k, k_a, r_k, lnx_w, lnx_b):
    B = p.shape[0]
    H = N_HEADS_RWKV
    f32 = jnp.float32
    shifted = jnp.concatenate([nbr_mean_seq(p[:, :n_ctx]), nbr_mean_grid(p[:, n_ctx:])], axis=1)
    p = p + mu * (shifted - p)
    r, k, v, wd_f, wd_b, ad_f, ad_b, gd = split_sizes(p, RWKV_SIZES)
    if vres is None:
        v_first = v
    else:
        v0, v_down, v_up = vres
        v = v + (v_first - v) * jax.nn.sigmoid(v0 + (h @ v_down) @ v_up)
    g = jax.nn.sigmoid(gd) @ g_up
    r_h, v_h = heads(r, H), heads(v, H)
    kk = heads(k * k_k, H).astype(f32)
    kk = kk * lax.rsqrt(jnp.sum(kk * kk, axis=-1, keepdims=True) + L2_EPS)
    r_k_h = r_k.reshape(H, 1, HEAD_DIM_RWKV)
    dirs = []
    for d, (wd, ad) in enumerate(((wd_f, ad_f), (wd_b, ad_b))):
        w_raw = -jax.nn.softplus(-(w0[d] + jnp.tanh(wd) @ w_up[d])) - 0.5
        a = jax.nn.sigmoid(a0[d] + ad @ a_up[d])
        k_d = heads(k * (1.0 + (a - 1.0) * k_a), H)
        dirs.append((r_h, heads(-jnp.exp(w_raw.astype(f32)), H), k_d, v_h, kk, heads(a, H)))
    s0 = jnp.zeros((B, H, HEAD_DIM_RWKV, HEAD_DIM_RWKV), f32)
    o = bidir_prefix(rwkv7_scan, dirs[0], dirs[1], s0, n_ctx).astype(f32)
    mean = jnp.mean(o, axis=-1, keepdims=True)
    var = jnp.mean(jnp.square(o - mean), axis=-1, keepdims=True)
    o = merge_heads((o - mean) * lax.rsqrt(var + RWKV_LN_EPS)) * lnx_w + lnx_b
    bonus = (jnp.sum(r_h * dirs[0][2] * r_k_h, axis=-1, keepdims=True)
             + jnp.sum(r_h * dirs[1][2] * r_k_h, axis=-1, keepdims=True)) * v_h
    y = (o + merge_heads(bonus)).astype(p.dtype) * g
    return y, v_first

def retention_mixer(p, pos, decay_param, n_ctx):
    H = N_HEADS_RET
    q, k, v, g = split_sizes(p, (BRANCH_W,) * 4)
    q_h = rope(heads(q, H), pos)
    k_h = rope(heads(k, H), pos) * (HEAD_DIM_RET ** -0.5)
    v_h = heads(v, H)
    B, _, N, _ = q_h.shape
    log_gamma = -jnp.exp(decay_param.astype(jnp.float32))
    lf = [jnp.broadcast_to(log_gamma[d][None, :, None, None], (B, H, N, 1)) for d in range(2)]
    s0 = jnp.zeros((B, H, HEAD_DIM_RET, HEAD_DIM_RET), jnp.float32)
    o = bidir_prefix(chunk_linear_scan, (q_h, k_h, v_h, lf[0]), (q_h, k_h, v_h, lf[1]), s0, n_ctx)
    o = rms_norm(o)
    return merge_heads(o) * jax.nn.silu(g)

def hgrn2_mixer(p, lb, norm_w, n_ctx):
    H = N_HEADS_HGRN
    q, f_f, f_b, i, g = split_sizes(p, (BRANCH_W,) * 5)
    q_h, i_h = heads(jax.nn.silu(q), H), heads(i, H)
    B, _, N, _ = q_h.shape
    dirs = []
    for d, f in enumerate((f_f, f_b)):
        f32f = f.astype(jnp.float32)
        forget = lb[d] + (1.0 - lb[d]) * jax.nn.sigmoid(f32f)
        inp_gate = (1.0 - lb[d]) * jax.nn.sigmoid(-f32f)
        dirs.append((q_h, heads(inp_gate, H), i_h, heads(jnp.log(forget), H)))
    s0 = jnp.zeros((B, H, HEAD_DIM_HGRN, HEAD_DIM_HGRN), jnp.float32)
    o = bidir_prefix(chunk_linear_scan, dirs[0], dirs[1], s0, n_ctx)
    o = rms_norm(o, norm_w.reshape(H, 1, HEAD_DIM_HGRN))
    return merge_heads(o) * jax.nn.silu(g)

def sq_relu_mlp(h, w1, w2):
    return jnp.square(jax.nn.relu(h @ w1)) @ w2

def setup_inputs(seed: int = 0) -> dict:
    key = jax.random.key(seed)
    ks = jax.random.split(key, 32)
    f32 = jnp.float32
    L, D = DEPTH, D_MODEL

    def nrm(i, shape, s):
        return s * jax.random.normal(ks[i], shape, f32)

    ret_base = jnp.asarray(np.log(-np.log1p(-2.0 ** (-5.0 - np.arange(N_HEADS_RET)))), f32)
    return {
        'x': nrm(0, (BATCH, SEQ, D), 1.0),
        'c': nrm(1, (BATCH, D), 1.0),
        'ctx': nrm(2, (BATCH, CTX_LEN, D), 1.0),
        'c_ctx': nrm(3, (D,), 1.0),
        'ada_w': nrm(4, (L, D, 6 * D), 0.5 * D ** -0.5),
        'ada_b': nrm(5, (L, 6 * D), 0.01),
        'norm1_w': 1.0 + nrm(6, (L, D), 0.05),
        'norm2_w': 1.0 + nrm(7, (L, D), 0.05),
        'w_in': nrm(8, (L, D, N_IN), D ** -0.5),
        'rwkv_mu': jax.random.uniform(ks[9], (L, N_RWKV_IN), f32),
        'rwkv_w0': jax.random.uniform(ks[10], (L, 2, BRANCH_W), f32, minval=-6.0, maxval=-1.0),
        'rwkv_w_up': nrm(11, (L, 2, DECAY_LORA, BRANCH_W), 0.1 * DECAY_LORA ** -0.5),
        'rwkv_a0': nrm(12, (L, 2, BRANCH_W), 0.5),
        'rwkv_a_up': nrm(13, (L, 2, AAA_LORA, BRANCH_W), 0.1 * AAA_LORA ** -0.5),
        'rwkv_g_up': nrm(14, (L, GATE_LORA, BRANCH_W), GATE_LORA ** -0.5),
        'rwkv_k_k': 0.85 + nrm(15, (L, BRANCH_W), 0.05),
        'rwkv_k_a': 1.0 + nrm(16, (L, BRANCH_W), 0.05),
        'rwkv_r_k': nrm(17, (L, BRANCH_W), 0.1),
        'rwkv_lnx_w': 1.0 + nrm(18, (L, BRANCH_W), 0.05),
        'rwkv_lnx_b': nrm(19, (L, BRANCH_W), 0.01),
        'rwkv_v0': 1.0 + nrm(20, (L - 1, BRANCH_W), 0.1),
        'rwkv_v_down': nrm(21, (L - 1, D, MV_LORA), D ** -0.5),
        'rwkv_v_up': nrm(22, (L - 1, MV_LORA, BRANCH_W), 0.1 * MV_LORA ** -0.5),
        'ret_decay': ret_base + nrm(23, (L, 2, N_HEADS_RET), 0.05),
        'hgrn_lb': nrm(24, (L, 2, BRANCH_W), 0.5),
        'hgrn_norm_w': 1.0 + nrm(25, (L, BRANCH_W), 0.05),
        'w_branch': nrm(26, (L, N_BRANCH, BRANCH_W, D), BRANCH_W ** -0.5),
        'w_out': nrm(27, (L, D, D), D ** -0.5),
        'mlp_w1': nrm(28, (L, D, D_FF), D ** -0.5),
        'mlp_w2': nrm(29, (L, D_FF, D), D_FF ** -0.5),
        'final_norm_w': 1.0 + nrm(30, (D,), 0.05),
    }

def reference(x, c, ctx, c_ctx, ada_w, ada_b, norm1_w, norm2_w, w_in, rwkv_mu, rwkv_w0, rwkv_w_up,
              rwkv_a0, rwkv_a_up, rwkv_g_up, rwkv_k_k, rwkv_k_a, rwkv_r_k, rwkv_lnx_w, rwkv_lnx_b,
              rwkv_v0, rwkv_v_down, rwkv_v_up, ret_decay, hgrn_lb, hgrn_norm_w, w_branch, w_out,
              mlp_w1, mlp_w2, final_norm_w):
    n_ctx = ctx.shape[1]
    pos = jnp.arange(n_ctx + x.shape[1])
    sm = jax.nn.softmax(hgrn_lb.astype(jnp.float32), axis=0)
    hgrn_lower = jnp.cumsum(sm, axis=0) - sm[0:1]
    x_c, x_l = ctx, x
    v_first = None
    for l in range(DEPTH):
        last = l == DEPTH - 1
        mod_l = jax.nn.silu(c) @ ada_w[l] + ada_b[l]
        mod_c = jax.nn.silu(c_ctx) @ ada_w[l] + ada_b[l]
        sh1_l, sc1_l, g1_l, sh2_l, sc2_l, g2_l = (m[:, None, :] for m in jnp.split(mod_l, 6, axis=-1))
        sh1_c, sc1_c, g1_c, sh2_c, sc2_c, g2_c = jnp.split(mod_c, 6)
        h = jnp.concatenate([rms_norm(x_c, norm1_w[l]) * (1.0 + sc1_c) + sh1_c,
                             rms_norm(x_l, norm1_w[l]) * (1.0 + sc1_l) + sh1_l], axis=1)
        p_rw, p_ret, p_hg, p_gate = split_sizes(h @ w_in[l], (N_RWKV_IN, N_RET_IN, N_HGRN_IN, N_GATE_IN))
        vres = None if l == 0 else (rwkv_v0[l - 1], rwkv_v_down[l - 1], rwkv_v_up[l - 1])
        y_rw, v_first = rwkv7_mixer(p_rw, h, v_first, vres, n_ctx, rwkv_mu[l], rwkv_w0[l], rwkv_w_up[l],
                                    rwkv_a0[l], rwkv_a_up[l], rwkv_g_up[l], rwkv_k_k[l], rwkv_k_a[l],
                                    rwkv_r_k[l], rwkv_lnx_w[l], rwkv_lnx_b[l])
        y_ret = retention_mixer(p_ret, pos, ret_decay[l], n_ctx)
        y_hg = hgrn2_mixer(p_hg, hgrn_lower[l], hgrn_norm_w[l], n_ctx)
        if last:
            y_rw, y_ret, y_hg, p_gate = (t[:, n_ctx:] for t in (y_rw, y_ret, y_hg, p_gate))
        gate_rw, gate_ret, gate_hg = jnp.split(jax.nn.sigmoid(p_gate), N_BRANCH, axis=-1)
        merged = (gate_rw * (y_rw @ w_branch[l, 0]) + gate_ret * (y_ret @ w_branch[l, 1])
                  + gate_hg * (y_hg @ w_branch[l, 2]))
        out = merged @ w_out[l]
        if last:
            x_l = x_l + g1_l * out
        else:
            x_c = x_c + g1_c * out[:, :n_ctx]
            x_l = x_l + g1_l * out[:, n_ctx:]
        x_l = x_l + g2_l * sq_relu_mlp(rms_norm(x_l, norm2_w[l]) * (1.0 + sc2_l) + sh2_l, mlp_w1[l], mlp_w2[l])
        if not last:
            x_c = x_c + g2_c * sq_relu_mlp(rms_norm(x_c, norm2_w[l]) * (1.0 + sc2_c) + sh2_c, mlp_w1[l], mlp_w2[l])
    return rms_norm(x_l, final_norm_w)


_drawn_inputs = setup_inputs


def setup_inputs(seed=0):
    import zlib

    import numpy as np

    out = dict(_drawn_inputs(seed))
    spreads = {}
    factors = {'rwkv_w_up': 8.0,
     'rwkv_a_up': 8.0,
     'rwkv_k_k': 4.011,
     'rwkv_k_a': 3.858,
     'rwkv_lnx_w': 8.0,
     'rwkv_lnx_b': 52.59,
     'rwkv_v0': 8.0,
     'rwkv_v_down': 8.0,
     'rwkv_v_up': 8.0,
     'hgrn_lb': 8.0,
     'hgrn_norm_w': 7.388}
    for name, (base, spread) in spreads.items():
        noise = np.random.default_rng([zlib.crc32(name.encode()), seed]).standard_normal(out[name].shape)
        drawn = base * np.exp(spread * noise) if base else spread * noise
        out[name] = jnp.asarray(drawn.astype(out[name].dtype))
    for name, factor in factors.items():
        out[name] = (out[name] * factor).astype(out[name].dtype)
    return out
```

```python
import numpy as np
import concourse.bass as bass
import concourse.mybir as mybir
from contextlib import ExitStack

F32 = mybir.dt.float32
U32 = mybir.dt.uint32
ALU = mybir.AluOpType
ACT = mybir.ActivationFunctionType

P = 128
D = 1024
KT = D // P
N = 512
NC = 256
L = 2
BW = 512
NT = BW // P
C = 64
M = N // C
FF = 4 * D
GRID = 64
ROWS = (N - NC) // GRID
SLOT = KT * P * 3 + NT * P * 3
RING = 3
DECAY = float(np.exp(-0.5))

K_ID, K_ONE, K_BONE, K_ROT = 0, 128, 256, 384
K_STRICT, K_INCL, K_LEV = 512, 640, 768
K_HLEV = 1152
K_SCAN = 2048
K_EPS = 3072
K_ID2 = 3076
NCONST = 3140
R_COS, R_SIN, R_LAG = 0, 512, 1024
NRC = 1024 + 6 * 384

PARTS = dict(mu=15, w0=8, a0=8, kk=4, ka=4, rk=4, lnw=4, lnb=4, v0=4, lb=8, hnw=4, n1=8, n2=8, adab=48, dec=8)
COL, NPL = {}, 0
for _n, _w in PARTS.items():
    COL[_n] = NPL
    NPL += _w
NPAR = L * NPL + 8 + 16

D_MOD, D_HMU, D_QMU, D_OMU, D_OMKA, D_WS1, D_WS2, D_LG, D_CS, D_LOW, D_OML = (
    0, 96, 111, 126, 141, 145, 161, 177, 185, 201, 217)
D_TMP = 233
NDER = 265

Y = [0, 2048, 4096]
YR, YH = 1, 2
X = 10240
TN = 24576
RT_A = 7168
RT_CS, RT_LAG, RT_STRIP = 6144, 14336, 16640
RT_QK, RT_V, RT_ROT, RT_O = 19712, 21760, 22784, 23808
RW_D = [4096, 11776]
RW_SCR, RW_KK, RW_SQ, RW_KS, RW_VT = 19456, 21504, 22016, 22528, 23040
RW_RKV, RW_SMALL, RW_W, RW_VD = 23552, 25088, 26624, 28928
(KR, BT, KTI, LT, TT, ABT, MT, AKT, RR, YK, BTT, KTT, WW) = (
    0, 1024, 1536, 2048, 2560, 3072, 3584, 4096, 4608, 5120, 6144, 6656, 7168)
HG_F, HG_Q, HG_K, HG_A, HG_V, HG_T = 6144, 10240, 14336, 18432, 24576, 26624
MG, MG_T = 14336, 18432
WORK = 29440


def schedule_slots():
    out = []
    for l in range(L):
        out += [(("ada", l, a), 4 * KT * P) for a in range(12)]
        out += [(("ret", l, c), 4 * KT * P) for c in range(NT)]
        out += [(("small", l), 3 * KT * P)]
        out += [(("rw", l, c), 3 * KT * P) for c in range(NT)]
        out += [(("hi", l), 4 * KT * P)]
        out += [(("hf", l, c), 4 * KT * P) for c in range(NT)]
        out += [(("gb", l, f), SLOT) for f in range(KT)]
        out += [(("out", l, a), 4 * KT * P) for a in range(2)]
        out += [(("m1", l, a), 4 * KT * P) for a in range(8)]
        out += [(("m2", l, f), 32 * P) for f in range(8)]
    return out


class Steps:

    def __init__(self, ctx, nc, name, log, known):
        self.sem, self.name, self.log, self.known, self.n = ctx.enter_context(nc.semaphore(name)), name, log, known, 0

    def step(self, key=None, by=1):
        self.n += by
        if key is not None:
            self.also(key)
        return by

    def also(self, key):
        assert key not in self.log, key
        self.log[key] = (self.name, self.n)

    def at(self, *key):
        if self.known is None:
            return 1
        name, n = self.known[key]
        assert name == self.name, (key, name, self.name)
        return n


class Banks:

    def __init__(self, psum, first, n, width, steps, known, loaded):
        self.psum, self.first, self.n, self.width, self.steps, self.known = psum, first, n, width, steps, known
        self.loaded, self.keys, self.where = loaded, [], {}

    def fill(self, *key):
        self.where[key] = len(self.keys) % self.n
        self.keys.append(key)
        return self.get(*key)

    def freed(self):
        i = len(self.keys) - 1 - self.n
        if i < 0 or self.known is None:
            return self.loaded.sem, 32
        name, n = self.known[("drained", *self.keys[i])]
        return self.steps[name].sem, n

    def get(self, *key):
        b = self.first + self.where[key] * self.width
        return self.psum[:, 512 * b:512 * (b + self.width)]


def build_program(nc, known, wts, wsm, vec, con, rcon, xin, xscr, out):
    log = {}
    with ExitStack() as ctx:
        def sb(name, shape, dt=F32):
            return ctx.enter_context(nc.sbuf_tensor(name, shape, dt))

        ring = sb("weight_ring", [P, RING, SLOT])
        hT = sb("normed", [P, KT, N])
        vfirst = sb("v_first", [P, NT, N])
        kc = sb("constants", [P, NCONST])
        par = sb("vectors", [P, NPAR])
        der = sb("derived", [P, NDER])
        work = sb("work", [P, WORK])
        psum = ctx.enter_context(nc.psum_tensor("psum", [P, 4096], F32))

        steps = {}

        def counter(name):
            steps[name] = Steps(ctx, nc, name, log, known)
            return steps[name]

        big_filled, wide_filled = counter("big_filled"), counter("wide_filled")
        mid_filled, out_filled = counter("mid_filled"), counter("out_filled")
        vec_cond, act_cond = counter("vec_cond"), counter("act_cond")
        vec_norm, act_norm = counter("vec_norm"), counter("act_norm")
        vec_ret, act_ret, pool_ret = counter("vec_ret"), counter("act_ret"), counter("pool_ret")
        vec_rwkv, act_rwkv, pool_rwkv = counter("vec_rwkv"), counter("act_rwkv"), counter("pool_rwkv")
        vec_hgrn, act_hgrn, pool_hgrn = counter("vec_hgrn"), counter("act_hgrn"), counter("pool_hgrn")
        vec_merge, act_merge = counter("vec_merge"), counter("act_merge")
        vec_mlp, act_mlp, pool_mlp = counter("vec_mlp"), counter("act_mlp"), counter("pool_mlp")
        weights = [counter(f"weights_{i}") for i in range(RING)]
        loaded_vectors, loaded_x = counter("loaded_vectors"), counter("loaded_x")
        loaded_ret_constants, loaded_small_weights = counter("loaded_ret_constants"), counter("loaded_small_weights")
        x_saved, x_back, stored = counter("x_saved"), counter("x_back"), counter("stored")
        block = ctx.enter_context(nc.Block())

        def banks(first, n, width=1):
            return Banks(psum, first, n, width, steps, known, loaded_vectors)

        big = banks(0, 2)
        wide = banks(2, 1, 2)
        mid = banks(4, 2)
        outb = banks(6, 2)

        slots = schedule_slots()
        slot_at = {key: i for i, (key, _) in enumerate(slots)}

        def wk(off, n=N):
            return work[:, off:off + n]

        def chunks(off, n=64, at=0, step=64):
            return work[:, off:off + M * step].rearrange("p (m t) -> p m t", t=step)[:, :, at:at + n]

        def kcol(off, n):
            return kc[:, off:off + n]

        def over_chunks(ap, n):
            return ap.rearrange("p (a t) -> p a t", a=1).broadcast_to([P, M, n])

        def pcol(l, name, i=0, n=1):
            o = l * NPL + COL[name] + i
            return par[:, o:o + n]

        def dcol(o, n=1):
            return der[:, o:o + n]

        mod = der[:, D_MOD:D_MOD + 96].rearrange("p (t s) -> p t s", s=2)
        ident = kcol(K_ID, P)
        ones = kcol(K_ONE, P)
        bones = kcol(K_BONE, P)
        eps = {"rms": kcol(K_EPS, 1), "ln": kcol(K_EPS + 1, 1), "l2": kcol(K_EPS + 2, 1)}
        segs = [(0, 0, NC), (1, NC, N)]

        def live(l):
            return [(0, 0, NC), (1, NC, N)] if l < L - 1 else [(1, NC, N)]

        def rspan(l):
            s = live(l)
            return s[0][1], s[-1][2]

        ret_order = [("P", 0), ("R", 0), ("P", 1), ("A", 0), ("R", 1), ("O", 0), ("P", 2), ("A", 1), ("N", 0), ("R", 2),
                     ("O", 1), ("P", 3), ("A", 2), ("N", 1), ("R", 3), ("O", 2), ("A", 3), ("N", 2), ("O", 3), ("N", 3)]
        scut = [(0, 0), (512, 0), (1024, NC), (1280, NC)]

        def chain_order(d):
            h = M // 2
            return list(range(M)) if d == 0 else list(range(h - 1, -1, -1)) + list(range(M - 1, h - 1, -1))

        @block.tensor
        def _(eng):
            mm = nc.tensor.matmul

            def slot(*key):
                i = slot_at[key]
                eng.wait_ge(weights[i % RING].sem, 16 * (i // RING + 1))
                return ring[:, i % RING, :]

            def tiled(s, j, k):
                return s[:, (j * KT + k) * P:(j * KT + k + 1) * P]

            def project(s, j, key, t0=0, t1=N):
                ps = big.fill(*key)
                eng.wait_ge(*big.freed())
                for k in range(KT):
                    last = mm(ps[:, 0:t1 - t0], tiled(s, j, k), hT[:, k, t0:t1], start=(k == 0), stop=(k == KT - 1))
                last.then_inc(big_filled.sem, big_filled.step(key))

            def sum_over(lhs, rhs, key, n=N):
                ps = big.fill(*key)
                eng.wait_ge(*big.freed())
                mm(ps[:, 0:n], lhs, rhs, start=True, stop=True).then_inc(big_filled.sem, big_filled.step(key))

            def per_head(ps, w, lhs, rhs, accumulate=None):
                for m in range(M):
                    for h in range(2):
                        q = slice(64 * h, 64 * h + 64)
                        last = mm(ps[q, w * m:w * m + w], lhs(q, m), rhs(q, m), start=True, stop=True)
                return last

            def norm(l, which):
                t0, t1 = (0, N) if which == 1 or l < L - 1 else (NC, N)
                if which == 3:
                    t0 = NC
                ps = big.fill("sumsq", l, which)
                eng.wait_ge(*big.freed())
                for k in range(KT):
                    eng.wait_ge(act_norm.sem, act_norm.at("square", l, which, k))
                    last = mm(ps[:, 0:t1 - t0], ones, work[:, TN + 512 * (k % 2):TN + 512 * (k % 2) + t1 - t0],
                              start=(k == 0), stop=(k == KT - 1))
                    last.then_inc(big_filled.sem, big_filled.step(("squares read", l, which, k)))

            eng.wait_ge(loaded_vectors.sem, loaded_vectors.at("vectors"))
            for l in range(L):
                if l == 0:
                    eng.wait_ge(act_cond.sem, act_cond.at("cond silu"))
                for a in range(12):
                    s = slot("ada", l, a)
                    ps = big.fill("ada", l, a)
                    eng.wait_ge(*big.freed())
                    for j in range(4):
                        for k in range(KT):
                            last = mm(ps[:, 2 * j:2 * j + 2], tiled(s, j, k), der[:, D_CS + 2 * k:D_CS + 2 * k + 2],
                                      start=(k == 0), stop=(k == KT - 1))
                    last.then_inc(big_filled.sem, big_filled.step(("ada", l, a)))
                norm(l, 1)

                eng.wait_ge(act_norm.sem, act_norm.at("h", l, 1))
                for what, c in ret_order:
                    qk = RT_QK + 1024 * (c % 2)
                    v = RT_V + 512 * (c % 2)
                    A = RT_A + 1536 * (c % 2)
                    if what == "P":
                        s = slot("ret", l, c)
                        project(s, 0, ("rq", l, c))
                        project(s, 1, ("rk", l, c))
                        ps = big.fill("rv", l, c)
                        eng.wait_ge(*big.freed())
                        for i in range(4):
                            for k in range(KT):
                                last = mm(ps[:, P * i:P * i + P], hT[:, k, P * i:P * i + P], tiled(s, 2, k),
                                          start=(k == 0), stop=(k == KT - 1))
                        last.then_inc(big_filled.sem, big_filled.step(("rv", l, c)))
                        project(s, 3, ("rg", l, c))
                    if what == "R":
                        for i, n in enumerate(("rq", "rk")):
                            eng.wait_ge(act_ret.sem, act_ret.at("drained", n, l, c))
                            sum_over(kcol(K_ROT, P), wk(qk + 512 * i), (n + " turned", l, c))
                    if what == "A":
                        eng.wait_ge(vec_ret.sem, vec_ret.at("roped", l, c))
                        for i in range(2):
                            ps = mid.fill("rA", l, c, i)
                            eng.wait_ge(*mid.freed())
                            last = mm(ps, work[:, qk + 512 + P * i:qk + 512 + P * i + P], wk(qk), start=True, stop=True)
                            last.then_inc(mid_filled.sem, mid_filled.step(("rA", l, c, i)))
                        ps = mid.fill("rA", l, c, 2)
                        eng.wait_ge(*mid.freed())
                        for i in range(2, 4):
                            last = mm(ps[:, 256 * (i - 2):256 * (i - 2) + 256],
                                      work[:, qk + 512 + P * i:qk + 512 + P * i + P],
                                      work[:, qk + NC:qk + N], start=True, stop=True)
                        last.then_inc(mid_filled.sem, mid_filled.step(("rA", l, c, 2)))
                    if what == "O":
                        eng.wait_ge(vec_ret.sem, vec_ret.at("drained", "rA", l, c, 2))
                        eng.wait_ge(act_ret.sem, act_ret.at("drained", "rv", l, c))
                        ps = outb.fill("rO", l, c)
                        eng.wait_ge(*outb.freed())
                        for i, (col, t0) in enumerate(scut):
                            last = mm(ps[:, t0:N], work[:, v + P * i:v + P * i + P],
                                      work[:, A + col:A + col + N - t0], start=(i == 0), stop=(i == 3))
                        last.then_inc(out_filled.sem, out_filled.step(("rO", l, c)))
                    if what == "N":
                        eng.wait_ge(pool_ret.sem, pool_ret.at("ret squared", l, c))
                        sum_over(ones, wk(RT_O + 512), ("rN", l, c))

                s = slot("small", l)
                for j in range(3):
                    project(s, j, ("small", l, j))
                eng.wait_ge(loaded_small_weights.sem, loaded_small_weights.at("small weights", l))
                if l > 0:
                    ps = big.fill("vd", l)
                    eng.wait_ge(*big.freed())
                    for k in range(KT):
                        last = mm(ps[0:32, :], work[:, RW_W + 1536 + 32 * k:RW_W + 1536 + 32 * k + 32], hT[:, k, :],
                                  start=(k == 0), stop=(k == KT - 1))
                    last.then_inc(big_filled.sem, big_filled.step(("vd", l)))
                eng.wait_ge(act_rwkv.sem, act_rwkv.at("small ready", l))
                for c in range(NT):
                    wcol = slice(P * c, P * c + P)
                    s = slot("rw", l, c)
                    for j in range(3):
                        project(s, j, ("rkv", l, c, j))
                    if l > 0:
                        eng.wait_ge(act_rwkv.sem, act_rwkv.at("drained", "vd", l))
                        ps = big.fill("vgate", l, c)
                        eng.wait_ge(*big.freed())
                        last = mm(ps, wsm_up(work, wcol), work[0:32, RW_VD:RW_VD + N], start=True, stop=True)
                        last.then_inc(big_filled.sem, big_filled.step(("vgate", l, c)))
                    eng.wait_ge(pool_rwkv.sem, pool_rwkv.at("kk squared", l, c))
                    sum_over(bones, wk(RW_SQ), ("kk norm", l, c))
                    for d in range(2):
                        q = slice(64 * d, 64 * d + 64)
                        for j, n in enumerate(("zw", "za")):
                            ps = big.fill(n, l, c, d)
                            eng.wait_ge(*big.freed())
                            last = mm(ps, work[q, RW_W + 512 * j + P * c:RW_W + 512 * j + P * c + P],
                                      work[q, RW_SMALL + 512 * j:RW_SMALL + 512 * j + N], start=True, stop=True)
                            last.then_inc(big_filled.sem, big_filled.step((n, l, c, d)))
                    eng.wait_ge(vec_rwkv.sem, vec_rwkv.at("v ready", l, c))
                    vsrc = (lambda q, m: vfirst[q, c, 64 * m:64 * m + 64]) if l == 0 else (
                        lambda q, m: work[q, RW_RKV + 1024 + 64 * m:RW_RKV + 1024 + 64 * m + 64])
                    idq = lambda q, m: kc[q, K_ID + q.start:K_ID + q.start + 64]
                    ps = mid.fill("vT", l, c)
                    eng.wait_ge(*mid.freed())
                    per_head(ps, 64, vsrc, idq).then_inc(mid_filled.sem, mid_filled.step(("vT", l, c)))

                    def cell(off, step=64, at=0, n=64):
                        return lambda q, m: work[q, off + step * m + at:off + step * m + at + n]

                    for d in range(2):
                        B = RW_D[d]
                        eng.wait_ge(vec_rwkv.sem, vec_rwkv.at("prepared", l, c, d))
                        ps = wide.fill("gb", l, c, d)
                        eng.wait_ge(*wide.freed())
                        per_head(ps, 128, cell(B + BT), cell(B + KR, 128, 0, 128)).then_inc(wide_filled.sem, wide_filled.step(("gb", l, c, d)))
                        ps = mid.fill("tkk", l, c, d)
                        eng.wait_ge(*mid.freed())
                        per_head(ps, 64, cell(B + KR, 128), idq).then_inc(mid_filled.sem, mid_filled.step(("tkk", l, c, d)))
                        ps = mid.fill("tb", l, c, d)
                        eng.wait_ge(*mid.freed())
                        per_head(ps, 64, cell(B + BT), idq).then_inc(mid_filled.sem, mid_filled.step(("tb", l, c, d)))
                        ps = wide.fill("gk", l, c, d)
                        eng.wait_ge(*wide.freed())
                        per_head(ps, 128, cell(B + KTI), cell(B + KR, 128, 0, 128)).then_inc(wide_filled.sem, wide_filled.step(("gk", l, c, d)))
                        ps = mid.fill("tk", l, c, d)
                        eng.wait_ge(*mid.freed())
                        per_head(ps, 64, cell(B + KTI), idq).then_inc(mid_filled.sem, mid_filled.step(("tk", l, c, d)))
                    for d in range(2):
                        B = RW_D[d]
                        eng.wait_ge(vec_rwkv.sem, vec_rwkv.at("level", l, c, d, 0))
                        ps = mid.fill("l1", l, c, d)
                        eng.wait_ge(*mid.freed())
                        per_head(ps, 64, cell(B + BT), idq).then_inc(mid_filled.sem, mid_filled.step(("l1", l, c, d)))
                        eng.wait_ge(act_rwkv.sem, act_rwkv.at("drained", "vT", l, c))
                        ps = mid.fill("mv", l, c, d)
                        eng.wait_ge(*mid.freed())
                        per_head(ps, 64, cell(B + MT), cell(RW_VT)).then_inc(mid_filled.sem, mid_filled.step(("mv", l, c, d)))
                    for j in range(1, 6):
                        for d in range(2):
                            B = RW_D[d]
                            eng.wait_ge(pool_rwkv.sem, pool_rwkv.at("level", l, c, d, j))
                            if j == 1:
                                eng.wait_ge(vec_rwkv.sem, vec_rwkv.at("drained", "l1", l, c, d))
                            else:
                                eng.wait_ge(vec_rwkv.sem, vec_rwkv.at("drained", "dT", l, c, d, j - 1))
                            ps = mid.fill("Z", l, c, d, j)
                            eng.wait_ge(*mid.freed())
                            per_head(ps, 64, cell(B + (KTI if j % 2 else BT)), cell(B + TT)).then_inc(mid_filled.sem, mid_filled.step(("Z", l, c, d, j)))
                        for d in range(2):
                            B = RW_D[d]
                            eng.wait_ge(act_rwkv.sem, act_rwkv.at("drained", "Z", l, c, d, j))
                            if j > 1:
                                eng.wait_ge(vec_rwkv.sem, vec_rwkv.at("drained", "dR", l, c, d, j - 1))
                            if j < 5:
                                ps = mid.fill("dT", l, c, d, j)
                                eng.wait_ge(*mid.freed())
                                per_head(ps, 64, cell(B + RR), cell(B + MT)).then_inc(mid_filled.sem, mid_filled.step(("dT", l, c, d, j)))
                            ps = mid.fill("dR", l, c, d, j)
                            eng.wait_ge(*mid.freed())
                            per_head(ps, 64, cell(B + MT), cell(B + RR)).then_inc(mid_filled.sem, mid_filled.step(("dR", l, c, d, j)))
                    for d in range(2):
                        B = RW_D[d]
                        eng.wait_ge(vec_rwkv.sem, vec_rwkv.at("drained", "dR", l, c, d, 5))
                        ps = wide.fill("uk", l, c, d)
                        eng.wait_ge(*wide.freed())
                        per_head(ps, 128, cell(B + RR), cell(B + YK, 128, 0, 128)).then_inc(wide_filled.sem, wide_filled.step(("uk", l, c, d)))
                    for d in range(2):
                        B = RW_D[d]
                        eng.wait_ge(act_rwkv.sem, act_rwkv.at("drained", "uk", l, c, d))
                        ps = mid.fill("rr", l, c, d)
                        eng.wait_ge(*mid.freed())
                        per_head(ps, 64, cell(B + LT, 128, 64), cell(B + ABT)).then_inc(mid_filled.sem, mid_filled.step(("rr", l, c, d)))
                        ps = mid.fill("pt", l, c, d)
                        eng.wait_ge(*mid.freed())
                        per_head(ps, 64, cell(B + LT, 128, 64), cell(B + BTT)).then_inc(mid_filled.sem, mid_filled.step(("pt", l, c, d)))
                    for d in range(2):
                        outb.fill("O", l, c, d)
                        eng.wait_ge(*outb.freed())
                    for i in range(M):
                        for d in range(2):
                            B = RW_D[d]
                            m = chain_order(d)[i]
                            if i < M - 1:
                                if i > 0:
                                    eng.wait_ge(vec_rwkv.sem, vec_rwkv.at("S", l, c, d, i))
                                if i == 1:
                                    eng.wait_ge(vec_rwkv.sem, vec_rwkv.at("drained", "pt", l, c, d))
                                ps = mid.fill("dS", l, c, d, i)
                                eng.wait_ge(*mid.freed())
                                for h in range(2):
                                    q = slice(64 * h, 64 * h + 64)
                                    ops = [(KTT, RW_VT, 64), (BTT, B + LT, 128)]
                                    for n, (a, r, rs) in enumerate(ops):
                                        last = mm(ps[q, 0:64], work[q, B + a + 64 * m:B + a + 64 * m + 64],
                                                  work[q, r + rs * m:r + rs * m + 64],
                                                  start=(n == 0), stop=(n == 1 and i == 0))
                                    if i > 0:
                                        last = mm(ps[q, 0:64], work[q, B + MT + 64 * m:B + MT + 64 * m + 64],
                                                  work[q, B + YK + 64 * i:B + YK + 64 * i + 64], start=False, stop=True)
                                last.then_inc(mid_filled.sem, mid_filled.step(("dS", l, c, d, i)))
                            if i == M - 1:
                                eng.wait_ge(vec_rwkv.sem, vec_rwkv.at("S", l, c, d, i))
                            ps = outb.get("O", l, c, d)
                            if i == 0:
                                eng.wait_ge(vec_rwkv.sem, vec_rwkv.at("drained", "rr", l, c, d))
                            for h in range(2):
                                q = slice(64 * h, 64 * h + 64)
                                o = ps[q, 64 * m:64 * m + 64]
                                mm(o, work[q, RW_VT + 64 * m:RW_VT + 64 * m + 64],
                                   work[q, B + AKT + 64 * m:B + AKT + 64 * m + 64], start=True, stop=False)
                                last = mm(o, work[q, B + LT + 128 * m:B + LT + 128 * m + 64],
                                          work[q, B + ABT + 64 * m:B + ABT + 64 * m + 64], start=False, stop=(i == 0))
                                if i > 0:
                                    last = mm(o, work[q, B + YK + 64 * i:B + YK + 64 * i + 64],
                                              work[q, B + KR + 128 * m + 64:B + KR + 128 * m + 128],
                                              start=False, stop=True)
                            if i == M - 1:
                                last.then_inc(out_filled.sem, out_filled.step(("O", l, c, d)))
                    eng.wait_ge(vec_rwkv.sem, vec_rwkv.at("o summed", l, c))
                    sum_over(bones, wk(RW_SCR), ("mean", l, c))
                    eng.wait_ge(vec_rwkv.sem, vec_rwkv.at("bonus terms", l, c))
                    sum_over(bones, wk(RW_KS), ("bonus", l, c))
                    eng.wait_ge(pool_rwkv.sem, pool_rwkv.at("centred squared", l, c))
                    sum_over(bones, wk(RW_SCR + 512), ("var", l, c))
                    sum_over(work[:, RW_W + 1024 + P * c:RW_W + 1024 + P * c + P], wk(RW_SMALL + 1024), ("gate", l, c))

                s = slot("hi", l)
                for i in range(4):
                    ps = big.fill("hi", l, i)
                    eng.wait_ge(*big.freed())
                    for k in range(KT):
                        last = mm(ps, hT[:, k, P * i:P * i + P], s[:, BW * k:BW * k + BW], start=(k == 0), stop=(k == KT - 1))
                    last.then_inc(big_filled.sem, big_filled.step(("hi", l, i)))

                def hdiag(h):
                    eng.wait_ge(vec_hgrn.sem, vec_hgrn.at("hq ready", l, h))
                    ps = mid.fill("hd", l, h)
                    eng.wait_ge(*mid.freed())
                    for i in range(4):
                        t = slice(P * i, P * i + P)
                        for dd in range(2):
                            last = mm(ps[:, t], wk(HG_K + 2048 * dd + 512 * h)[:, t], wk(HG_T + 512 * (h % 2))[:, t],
                                      start=(dd == 0), stop=(dd == 1))
                    last.then_inc(mid_filled.sem, mid_filled.step(("hd", l, h)))

                for h in range(4):
                    s = slot("hf", l, h)
                    for j in range(4):
                        project(s, j, ("hf", l, h, j))
                    if h > 0:
                        hdiag(h - 1)
                hdiag(3)
                for j in range(9):
                    for h in range(4):
                        if j > 0:
                            eng.wait_ge(vec_hgrn.sem, vec_hgrn.at("hq up", l, h, j - 1))
                            eng.wait_ge(pool_hgrn.sem, pool_hgrn.at("hk up", l, h, j - 1))
                        q_ = [wk(HG_Q_of(dd, h)) for dd in range(2)]
                        k_ = [wk(HG_K + 2048 * dd + 512 * h) for dd in range(2)]
                        ps = mid.fill("hl", l, h, j)
                        eng.wait_ge(*mid.freed())
                        if j < 7:
                            b = 1 << j
                            for i in range(4):
                                t = slice(P * i, P * i + P)
                                for dd in range(2):
                                    side = 1 - dd
                                    cols = lambda ap: ap[:, t].rearrange("p (n s b) -> p n s b", s=2, b=b)[:, :, side, :]
                                    last = mm(cols(ps), k_[dd][:, t], cols(q_[dd]), start=True, stop=True)
                        elif j == 7:
                            for i in range(4):
                                dd, o = i % 2, i ^ 1
                                last = mm(ps[:, P * i:P * i + P], k_[dd][:, P * i:P * i + P], q_[dd][:, P * o:P * o + P],
                                          start=True, stop=True)
                        else:
                            for i in range(2):
                                for dd in range(2):
                                    last = mm(ps[:, 256 * i:256 * i + 256], k_[dd][:, P * i:P * i + P], q_[dd][:, NC:N],
                                              start=(dd == 0), stop=(dd == 1))
                        last.then_inc(mid_filled.sem, mid_filled.step(("hl", l, h, j)))
                for h in range(4):
                    eng.wait_ge(act_hgrn.sem, act_hgrn.at("drained", "hl", l, h, 7))
                    eng.wait_ge(act_hgrn.sem, act_hgrn.at("drained", "hl", l, h, 8))
                    if h == 0:
                        eng.wait_ge(act_hgrn.sem, act_hgrn.at("drained", "hi", l, 3))
                    ps = outb.fill("hO", l, h)
                    eng.wait_ge(*outb.freed())
                    A = HG_A + 1536 * h
                    for i, (col, t0) in enumerate(scut):
                        last = mm(ps[:, t0:N], work[:, HG_V + 512 * i + P * h:HG_V + 512 * i + P * h + P],
                                  work[:, A + col:A + col + N - t0], start=(i == 0), stop=(i == 3))
                    last.then_inc(out_filled.sem, out_filled.step(("hO", l, h)))
                for h in range(4):
                    eng.wait_ge(pool_hgrn.sem, pool_hgrn.at("hgrn squared", l, h))
                    sum_over(ones, wk(HG_T + 512 + 512 * (h % 2)), ("hN", l, h))

                t0, t1 = rspan(l)
                eng.wait_ge(vec_hgrn.sem, vec_hgrn.at("y ready", l))
                for f in range(KT):
                    s = slot("gb", l, f)
                    for b in range(3):
                        project(s, b, ("ga", l, f, b), t0, t1)
                        ps = big.fill("br", l, f, b)
                        eng.wait_ge(*big.freed())
                        for k in range(NT):
                            w0 = 3 * KT * P + (b * NT + k) * P
                            last = mm(ps[:, 0:t1 - t0], s[:, w0:w0 + P], work[:, Y[b] + 512 * k + t0:Y[b] + 512 * k + t1],
                                      start=(k == 0), stop=(k == NT - 1))
                        last.then_inc(big_filled.sem, big_filled.step(("br", l, f, b)))
                for f in range(KT):
                    if f % 4 == 0:
                        s = slot("out", l, f // 4)
                    ps = big.fill("ot", l, f)
                    eng.wait_ge(*big.freed())
                    for k in range(KT):
                        if f == 0:
                            eng.wait_ge(vec_merge.sem, vec_merge.at("merged", l, k))
                        last = mm(ps[:, 0:t1 - t0], tiled(s, f % 4, k), work[:, MG + 512 * k + t0:MG + 512 * k + t1],
                                  start=(k == 0), stop=(k == KT - 1))
                    last.then_inc(big_filled.sem, big_filled.step(("ot", l, f)))
                norm(l, 2)
                eng.wait_ge(act_norm.sem, act_norm.at("h", l, 2))
                for f in range(32):
                    if f % 4 == 0:
                        s = slot("m1", l, f // 4)
                    project(s, f % 4, ("m1", l, f), t0, t1)
                for f in range(KT):
                    s = slot("m2", l, f)
                    ps = big.fill("m2", l, f)
                    eng.wait_ge(*big.freed())
                    for k in range(32):
                        if f == 0:
                            eng.wait_ge(pool_mlp.sem, pool_mlp.at("hidden", l, k))
                        last = mm(ps[:, 0:t1 - t0], s[:, P * k:P * k + P], work[:, hid(k) + t0:hid(k) + t1],
                                  start=(k == 0), stop=(k == 31))
                    last.then_inc(big_filled.sem, big_filled.step(("m2", l, f)))
            norm(L - 1, 3)

        @block.vector
        def _(eng):
            tt, ts, stt, cp = (nc.vector.tensor_tensor, nc.vector.tensor_scalar, nc.vector.scalar_tensor_tensor,
                               nc.vector.tensor_copy)

            def drain_diag(l, h):
                eng.wait_ge(pool_hgrn.sem, pool_hgrn.at("scores clear", l, h))
                eng.wait_ge(mid_filled.sem, mid_filled.at("hd", l, h))
                msk = kc[:, K_ID:K_ID + P].bitcast(U32).rearrange("p (a t) -> p a t", a=1).broadcast_to([P, 2, P])
                for half, diag in enumerate(scores_diag(work, h)):
                    ps = mid.get("hd", l, h)[:, 256 * half:256 * half + 256].rearrange("p (i t) -> p i t", t=P)
                    nc.vector.copy_predicated(diag, msk, ps).then_inc(
                        vec_hgrn.sem, vec_hgrn.step(("drained", "hd", l, h) if half else None))
                    eng.wait_ge(vec_hgrn.sem, vec_hgrn.n)

            def hgrn_tail(l, h):
                eng.wait_ge(act_hgrn.sem, act_hgrn.at("hgrn rms", l, h))
                o = wk(HG_T + 1536 if h % 2 else HG_T)
                y = wk(Y[YH] + 512 * h)
                stt(o, o, pcol(l, "hnw", h), wk(HG_T + 512 + 512 * (h % 2)), ALU.mult, ALU.mult).then_inc(
                    vec_hgrn.sem, vec_hgrn.step())
                eng.wait_ge(vec_hgrn.sem, vec_hgrn.n)
                tt(y, y, o, ALU.mult).then_inc(vec_hgrn.sem, vec_hgrn.step(("hgrn y", l, h)))
                eng.wait_ge(vec_hgrn.sem, vec_hgrn.n)

            def add_gated(done, ps, tile, x, parts, t0, key):
                for i, (sg, u0, u1) in enumerate(parts):
                    stt(work[:, x + u0:x + u1], ps[:, u0 - t0:u1 - t0], mod[:, tile, sg:sg + 1],
                        work[:, x + u0:x + u1], ALU.mult, ALU.add).then_inc(
                            done.sem, done.step(key if i == len(parts) - 1 else None))
                    eng.wait_ge(done.sem, done.n)

            def tail(l, which):
                t0, t1 = (0, N) if which == 1 or l < L - 1 else (NC, N)
                if which == 3:
                    t0 = NC
                eng.wait_ge(act_norm.sem, act_norm.at("rms", l, which))
                for k in range(KT):
                    o = TN + 1536 + 512 * (k % 2)
                    if which == 3:
                        stt(wk(X + 512 * k)[:, t0:t1], wk(X + 512 * k)[:, t0:t1],
                                     par[:, L * NPL + k:L * NPL + k + 1], work[:, TN + 1024:TN + 1024 + t1 - t0],
                                     ALU.mult, ALU.mult).then_inc(vec_norm.sem, vec_norm.step(("final", k)))
                        eng.wait_ge(vec_norm.sem, vec_norm.n)
                        continue
                    if k >= 2:
                        eng.wait_ge(act_norm.sem, act_norm.at("h tile", l, which, k - 2))
                    tt(work[:, o:o + t1 - t0], wk(X + 512 * k)[:, t0:t1], work[:, TN + 1024:TN + 1024 + t1 - t0],
                                ALU.mult).then_inc(vec_norm.sem, vec_norm.step(("x scaled", l, which, k)))
                    eng.wait_ge(vec_norm.sem, vec_norm.n)

            eng.wait_ge(loaded_vectors.sem, loaded_vectors.at("vectors"))
            lbs = [pcol(l, "lb", 0, 8) for l in range(L)]
            t = [dcol(D_TMP + 8 * i, 8) for i in range(4)]
            tt(t[0], lbs[0], lbs[1], ALU.max).then_inc(vec_cond.sem, vec_cond.step())
            eng.wait_ge(vec_cond.sem, vec_cond.n)
            tt(t[1], lbs[0], t[0], ALU.subtract).then_inc(vec_cond.sem, vec_cond.step())
            eng.wait_ge(vec_cond.sem, vec_cond.n)
            tt(t[2], lbs[1], t[0], ALU.subtract).then_inc(vec_cond.sem, vec_cond.step(("lb centred",)))
            eng.wait_ge(vec_cond.sem, vec_cond.n)
            eng.wait_ge(act_cond.sem, act_cond.at("lb exp"))
            tt(t[3], t[1], t[2], ALU.add).then_inc(vec_cond.sem, vec_cond.step())
            eng.wait_ge(vec_cond.sem, vec_cond.n)
            nc.vector.reciprocal(t[0], t[3]).then_inc(vec_cond.sem, vec_cond.step())
            eng.wait_ge(vec_cond.sem, vec_cond.n)
            tt(t[1], t[1], t[0], ALU.mult).then_inc(vec_cond.sem, vec_cond.step())
            eng.wait_ge(vec_cond.sem, vec_cond.n)
            tt(t[2], t[2], t[0], ALU.mult).then_inc(vec_cond.sem, vec_cond.step())
            eng.wait_ge(vec_cond.sem, vec_cond.n)
            tt(t[3], t[1], t[2], ALU.add).then_inc(vec_cond.sem, vec_cond.step())
            eng.wait_ge(vec_cond.sem, vec_cond.n)
            tt(dcol(D_LOW, 8), t[1], t[1], ALU.subtract).then_inc(vec_cond.sem, vec_cond.step())
            eng.wait_ge(vec_cond.sem, vec_cond.n)
            tt(dcol(D_LOW + 8, 8), t[3], t[1], ALU.subtract).then_inc(vec_cond.sem, vec_cond.step())
            eng.wait_ge(vec_cond.sem, vec_cond.n)
            ts(dcol(D_OML, 16), dcol(D_LOW, 16), -1.0, 1.0, ALU.mult, ALU.add).then_inc(vec_cond.sem, vec_cond.step())
            eng.wait_ge(vec_cond.sem, vec_cond.n)

            for l in range(L):
                if l > 0:
                    eng.wait_ge(big_filled.sem, big_filled.at("m2", l - 1, 7))
                for a in range(12):
                    eng.wait_ge(big_filled.sem, big_filled.at("ada", l, a))
                    ps = big.get("ada", l, a)[:, 0:8].rearrange("p (j s) -> p j s", s=2)
                    bias = pcol(l, "adab", 4 * a, 4).rearrange("p (j s) -> p j s", s=1).broadcast_to([P, 4, 2])
                    tt(mod[:, 4 * a:4 * a + 4, :], ps, bias, ALU.add).then_inc(vec_cond.sem, vec_cond.step(("drained", "ada", l, a)))
                    eng.wait_ge(vec_cond.sem, vec_cond.n)
                for dst, sc, w in ((D_WS1, 8, "n1"), (D_WS2, 32, "n2")):
                    wb = pcol(l, w, 0, 8).rearrange("p (j s) -> p j s", s=1).broadcast_to([P, 8, 2])
                    stt(dcol(dst, 16).rearrange("p (j s) -> p j s", s=2), mod[:, sc:sc + 8, :], 1.0, wb,
                                 ALU.add, ALU.mult).then_inc(vec_cond.sem, vec_cond.step())
                    eng.wait_ge(vec_cond.sem, vec_cond.n)
                ts(dcol(D_HMU, 15), pcol(l, "mu", 0, 15), 0.5, None, ALU.mult).then_inc(vec_cond.sem, vec_cond.step())
                eng.wait_ge(vec_cond.sem, vec_cond.n)
                ts(dcol(D_QMU, 15), pcol(l, "mu", 0, 15), 0.25, None, ALU.mult).then_inc(vec_cond.sem, vec_cond.step())
                eng.wait_ge(vec_cond.sem, vec_cond.n)
                ts(dcol(D_OMU, 15), pcol(l, "mu", 0, 15), -1.0, 1.0, ALU.mult, ALU.add).then_inc(vec_cond.sem, vec_cond.step())
                eng.wait_ge(vec_cond.sem, vec_cond.n)
                ts(dcol(D_OMKA, 4), pcol(l, "ka", 0, 4), -1.0, 1.0, ALU.mult, ALU.add).then_inc(vec_cond.sem, vec_cond.step())
                eng.wait_ge(vec_cond.sem, vec_cond.n)
                eng.wait_ge(act_cond.sem, act_cond.at("ret decay exp", l))
                ts(dcol(D_LG, 8), dcol(D_LG, 8), -1.0, None, ALU.mult).then_inc(vec_cond.sem, vec_cond.step(("vectors derived", l)))
                eng.wait_ge(vec_cond.sem, vec_cond.n)
                tail(l, 1)

                for h in range(4):
                    S = RT_STRIP + 768 * h
                    eng.wait_ge(act_ret.sem, act_ret.at("strip exps", l, h))
                    tt(wk(S, 384), wk(S, 384), wk(RT_LAG + 768, 384), ALU.mult).then_inc(vec_ret.sem, vec_ret.step())
                    eng.wait_ge(vec_ret.sem, vec_ret.n)
                    tt(wk(RT_A + 768 * h, 384), wk(RT_A + 768 * h, 384), wk(RT_LAG + 1152, 384), ALU.mult).then_inc(vec_ret.sem, vec_ret.step())
                    eng.wait_ge(vec_ret.sem, vec_ret.n)
                    tt(wk(S, 768), wk(S, 768), wk(RT_A + 768 * h, 768), ALU.add).then_inc(vec_ret.sem, vec_ret.step())
                    eng.wait_ge(vec_ret.sem, vec_ret.n)
                    ts(wk(S, 768), wk(S, 768), float(P) ** -0.5, None, ALU.mult).then_inc(vec_ret.sem, vec_ret.step(("strip", l, h)))
                    eng.wait_ge(vec_ret.sem, vec_ret.n)
                for what, c in ret_order:
                    qk = RT_QK + 1024 * (c % 2)
                    A = RT_A + 1536 * (c % 2)
                    if what == "R":
                        for i, n in enumerate(("rq", "rk")):
                            eng.wait_ge(big_filled.sem, big_filled.at(n + " turned", l, c))
                            tt(wk(RT_ROT), big.get(n + " turned", l, c), wk(RT_CS + 512), ALU.mult).then_inc(vec_ret.sem, vec_ret.step(("drained", n + " turned", l, c)))
                            eng.wait_ge(vec_ret.sem, vec_ret.n)
                            tt(wk(qk + 512 * i), wk(qk + 512 * i), wk(RT_CS), ALU.mult).then_inc(vec_ret.sem, vec_ret.step())
                            eng.wait_ge(vec_ret.sem, vec_ret.n)
                            tt(wk(qk + 512 * i), wk(qk + 512 * i), wk(RT_ROT), ALU.add).then_inc(vec_ret.sem, vec_ret.step(("roped", l, c) if i else None))
                            eng.wait_ge(vec_ret.sem, vec_ret.n)
                    if what == "A":
                        S = RT_STRIP + 768 * c
                        for i in range(2):
                            eng.wait_ge(mid_filled.sem, mid_filled.at("rA", l, c, i))
                            ps = mid.get("rA", l, c, i)
                            tt(wk(A + 512 * i, 256), ps[:, 0:256], wk(S + 128 - 128 * i, 256), ALU.mult).then_inc(vec_ret.sem, vec_ret.step())
                            eng.wait_ge(vec_ret.sem, vec_ret.n)
                            tt(wk(A + 512 * i + 256, 256), ps[:, 256:512], wk(S + 384 + 128 - 128 * i, 256),
                                        ALU.mult).then_inc(vec_ret.sem, vec_ret.step(("drained", "rA", l, c, i)))
                            eng.wait_ge(vec_ret.sem, vec_ret.n)
                        eng.wait_ge(mid_filled.sem, mid_filled.at("rA", l, c, 2))
                        ps = mid.get("rA", l, c, 2)
                        for i in range(2):
                            tt(wk(A + 1024 + 256 * i, 256), ps[:, 256 * i:256 * i + 256],
                                        wk(S + 128 - 128 * i, 256), ALU.mult).then_inc(vec_ret.sem, vec_ret.step(("drained", "rA", l, c, 2) if i else None))
                            eng.wait_ge(vec_ret.sem, vec_ret.n)
                    if what == "O":
                        eng.wait_ge(out_filled.sem, out_filled.at("rO", l, c))
                        cp(wk(RT_O), outb.get("rO", l, c)).then_inc(vec_ret.sem, vec_ret.step(("drained", "rO", l, c)))
                        eng.wait_ge(vec_ret.sem, vec_ret.n)
                    if what == "N":
                        eng.wait_ge(act_ret.sem, act_ret.at("ret rms", l, c))
                        tt(wk(RT_O), wk(RT_O), wk(RT_O + 1024), ALU.mult).then_inc(vec_ret.sem, vec_ret.step())
                        eng.wait_ge(vec_ret.sem, vec_ret.n)
                        eng.wait_ge(act_ret.sem, act_ret.at("drained", "rg", l, c))
                        y = wk(Y[YR] + 512 * c)
                        tt(y, y, wk(RT_O), ALU.mult).then_inc(vec_ret.sem, vec_ret.step(("ret y", l, c)))
                        eng.wait_ge(vec_ret.sem, vec_ret.n)

                def mix(i, dst, key):
                    eng.wait_ge(pool_rwkv.sem, pool_rwkv.at("neighbours", l, i))
                    raw = RW_SCR
                    ts(dst[:, 0:NC], wk(raw + 1, NC), dcol(D_OMU + i), None, ALU.mult).then_inc(vec_rwkv.sem, vec_rwkv.step())
                    eng.wait_ge(vec_rwkv.sem, vec_rwkv.n)
                    grid = wk(raw + 258, 396).rearrange("p (r t) -> p r t", t=66)[:, 1:5, 1:65]
                    dg = dst[:, NC:N].rearrange("p (r t) -> p r t", t=GRID)
                    ts(dg, grid, dcol(D_OMU + i), None, ALU.mult).then_inc(vec_rwkv.sem, vec_rwkv.step())
                    eng.wait_ge(vec_rwkv.sem, vec_rwkv.n)
                    stt(dst[:, 0:NC], wk(raw + 654, NC), dcol(D_HMU + i), dst[:, 0:NC], ALU.mult, ALU.add).then_inc(vec_rwkv.sem, vec_rwkv.step())
                    eng.wait_ge(vec_rwkv.sem, vec_rwkv.n)
                    stt(dst[:, NC:N], wk(raw + 654 + NC, NC), dcol(D_QMU + i), dst[:, NC:N], ALU.mult, ALU.add).then_inc(vec_rwkv.sem, vec_rwkv.step(key))
                    eng.wait_ge(vec_rwkv.sem, vec_rwkv.n)

                eng.wait_ge(x_saved.sem, x_saved.at("x saved", l))
                for j in range(3):
                    mix(12 + j, wk(RW_SMALL + 512 * j), ("mixed", l, 12 + j))
                for c in range(NT):
                    r, k = wk(RW_RKV), wk(RW_RKV + 512)
                    vv = vfirst[:, c, :] if l == 0 else wk(RW_RKV + 1024)
                    for j, dst in enumerate((r, k, vv)):
                        mix(4 * j + c, dst, ("mixed", l, 4 * j + c))
                    ts(wk(RW_KK), k, pcol(l, "kk", c), None, ALU.mult).then_inc(vec_rwkv.sem, vec_rwkv.step(("kk raw", l, c)))
                    eng.wait_ge(vec_rwkv.sem, vec_rwkv.n)
                    if l > 0:
                        tt(wk(RW_SCR + 512), vfirst[:, c, :], vv, ALU.subtract).then_inc(vec_rwkv.sem, vec_rwkv.step())
                        eng.wait_ge(vec_rwkv.sem, vec_rwkv.n)
                        eng.wait_ge(act_rwkv.sem, act_rwkv.at("vgate sigmoid", l, c))
                        tt(wk(RW_SCR + 512), wk(RW_SCR + 512), wk(RW_SCR), ALU.mult).then_inc(vec_rwkv.sem, vec_rwkv.step())
                        eng.wait_ge(vec_rwkv.sem, vec_rwkv.n)
                        tt(vv, vv, wk(RW_SCR + 512), ALU.add).then_inc(vec_rwkv.sem, vec_rwkv.step(("v ready", l, c)))
                        eng.wait_ge(vec_rwkv.sem, vec_rwkv.n)
                    else:
                        vec_rwkv.also(("v ready", l, c))
                    eng.wait_ge(act_rwkv.sem, act_rwkv.at("kk rms", l, c))
                    tt(wk(RW_KK), wk(RW_KK), wk(RW_SQ), ALU.mult).then_inc(vec_rwkv.sem, vec_rwkv.step(("kk ready", l, c)))
                    eng.wait_ge(vec_rwkv.sem, vec_rwkv.n)
                    for d in range(2):
                        B = RW_D[d]
                        eng.wait_ge(act_rwkv.sem, act_rwkv.at("decay sigmoid", l, c, d))
                        G, s, msk = wk(RW_SCR + 512 * d), wk(B + WW), kcol(K_SCAN + 512 * d, N)
                        if d == 1:
                            G, s, msk = G[:, ::-1], s[:, ::-1], msk[:, ::-1]
                        nc.vector.tensor_tensor_scan(G, msk, s, 0.0, ALU.mult, ALU.add).then_inc(vec_rwkv.sem, vec_rwkv.step(("decay sums", l, c, d)))
                        eng.wait_ge(vec_rwkv.sem, vec_rwkv.n)
                    for d in range(2):
                        B = RW_D[d]
                        eng.wait_ge(act_rwkv.sem, act_rwkv.at("a sigmoid", l, c, d))
                        ts(wk(B + KTI), wk(B + BT), pcol(l, "ka", c), dcol(D_OMKA + c), ALU.mult, ALU.add).then_inc(vec_rwkv.sem, vec_rwkv.step(("a read", l, c, d)))
                        eng.wait_ge(vec_rwkv.sem, vec_rwkv.n)
                        tt(wk(B + KTI), wk(B + KTI), k, ALU.mult).then_inc(vec_rwkv.sem, vec_rwkv.step())
                        eng.wait_ge(vec_rwkv.sem, vec_rwkv.n)
                    tt(wk(RW_KS), wk(RW_D[0] + KTI), wk(RW_D[1] + KTI), ALU.add).then_inc(vec_rwkv.sem, vec_rwkv.step())
                    eng.wait_ge(vec_rwkv.sem, vec_rwkv.n)
                    ts(wk(RW_KS), wk(RW_KS), pcol(l, "rk", c), None, ALU.mult).then_inc(vec_rwkv.sem, vec_rwkv.step())
                    eng.wait_ge(vec_rwkv.sem, vec_rwkv.n)
                    tt(wk(RW_KS), wk(RW_KS), r, ALU.mult).then_inc(vec_rwkv.sem, vec_rwkv.step(("bonus terms", l, c)))
                    eng.wait_ge(vec_rwkv.sem, vec_rwkv.n)
                    for d in range(2):
                        B = RW_D[d]
                        eng.wait_ge(act_rwkv.sem, act_rwkv.at("decays", l, c, d))
                        kk3, W3 = chunks(RW_KK), chunks(B + WW)
                        KR3 = chunks(B + KR, 64, 0, 128)
                        e = 0 if d == 0 else 63
                        a, b = (slice(1, 64), slice(0, 63)) if d == 0 else (slice(0, 63), slice(1, 64))
                        tt(KR3[:, :, a], kk3[:, :, a], W3[:, :, b], ALU.mult).then_inc(vec_rwkv.sem, vec_rwkv.step())
                        eng.wait_ge(vec_rwkv.sem, vec_rwkv.n)
                        cp(KR3[:, :, e:e + 1], kk3[:, :, e:e + 1]).then_inc(vec_rwkv.sem, vec_rwkv.step())
                        eng.wait_ge(vec_rwkv.sem, vec_rwkv.n)
                        tt(chunks(B + KR, 64, 64, 128), chunks(RW_RKV), W3, ALU.mult).then_inc(vec_rwkv.sem, vec_rwkv.step())
                        eng.wait_ge(vec_rwkv.sem, vec_rwkv.n)
                        eng.wait_ge(pool_rwkv.sem, pool_rwkv.at("b ready", l, c, d))
                        tt(wk(B + KTI), wk(B + KTI), wk(RW_SCR + 1024 + 512 * d), ALU.mult).then_inc(vec_rwkv.sem, vec_rwkv.step(("prepared", l, c, d)))
                        eng.wait_ge(vec_rwkv.sem, vec_rwkv.n)
                    for d in range(2):
                        B = RW_D[d]
                        eng.wait_ge(wide_filled.sem, wide_filled.at("gb", l, c, d))
                        ps = wide.get("gb", l, c, d).rearrange("p (m t) -> p m t", t=128)
                        tt(chunks(B + LT), ps[:, :, 0:64], over_chunks(kcol(K_STRICT + 64 * d, 64), 64), ALU.mult).then_inc(vec_rwkv.sem, vec_rwkv.step())
                        eng.wait_ge(vec_rwkv.sem, vec_rwkv.n)
                        tt(chunks(B + ABT), ps[:, :, 64:128], over_chunks(kcol(K_INCL + 64 * d, 64), 64), ALU.mult).then_inc(vec_rwkv.sem, vec_rwkv.step(("drained", "gb", l, c, d)))
                        eng.wait_ge(vec_rwkv.sem, vec_rwkv.n)
                        eng.wait_ge(wide_filled.sem, wide_filled.at("gk", l, c, d))
                        ps = wide.get("gk", l, c, d).rearrange("p (m t) -> p m t", t=128)
                        tt(chunks(B + MT), ps[:, :, 0:64], over_chunks(kcol(K_STRICT + 64 * d, 64), 64), ALU.mult).then_inc(vec_rwkv.sem, vec_rwkv.step())
                        eng.wait_ge(vec_rwkv.sem, vec_rwkv.n)
                        tt(chunks(B + AKT), ps[:, :, 64:128], over_chunks(kcol(K_INCL + 64 * d, 64), 64), ALU.mult).then_inc(vec_rwkv.sem, vec_rwkv.step(("drained", "gk", l, c, d)))
                        eng.wait_ge(vec_rwkv.sem, vec_rwkv.n)
                        eng.wait_ge(mid_filled.sem, mid_filled.at("tb", l, c, d))
                        tt(chunks(B + BT), chunks(B + LT), over_chunks(kcol(K_LEV, 64), 64), ALU.mult).then_inc(vec_rwkv.sem, vec_rwkv.step(("level", l, c, d, 0)))
                        eng.wait_ge(vec_rwkv.sem, vec_rwkv.n)
                        tt(chunks(B + RR), ident64(kc), chunks(B + BT), ALU.subtract).then_inc(vec_rwkv.sem, vec_rwkv.step(("R first", l, c, d)))
                        eng.wait_ge(vec_rwkv.sem, vec_rwkv.n)
                    for d in range(2):
                        B = RW_D[d]
                        eng.wait_ge(mid_filled.sem, mid_filled.at("l1", l, c, d))
                        tt(chunks(B + TT), ident64(kc), mid.get("l1", l, c, d).rearrange("p (m t) -> p m t", t=64),
                                    ALU.subtract).then_inc(vec_rwkv.sem, vec_rwkv.step(("drained", "l1", l, c, d)))
                        eng.wait_ge(vec_rwkv.sem, vec_rwkv.n)
                    for j in range(1, 6):
                        for d in range(2):
                            B = RW_D[d]
                            for n, o in (("dT", TT), ("dR", RR)):
                                if n == "dT" and j == 5:
                                    continue
                                eng.wait_ge(mid_filled.sem, mid_filled.at(n, l, c, d, j))
                                tt(wk(B + o), wk(B + o), mid.get(n, l, c, d, j), ALU.subtract).then_inc(vec_rwkv.sem, vec_rwkv.step(("drained", n, l, c, d, j)))
                                eng.wait_ge(vec_rwkv.sem, vec_rwkv.n)
                    for d in range(2):
                        B = RW_D[d]
                        eng.wait_ge(mid_filled.sem, mid_filled.at("rr", l, c, d))
                        tt(chunks(B + KR, 64, 64, 128), chunks(B + KR, 64, 64, 128),
                                    mid.get("rr", l, c, d).rearrange("p (m t) -> p m t", t=64), ALU.add).then_inc(vec_rwkv.sem, vec_rwkv.step(("drained", "rr", l, c, d)))
                        eng.wait_ge(vec_rwkv.sem, vec_rwkv.n)
                        eng.wait_ge(mid_filled.sem, mid_filled.at("pt", l, c, d))
                        tt(chunks(B + MT), ident64(kc), mid.get("pt", l, c, d).rearrange("p (m t) -> p m t", t=64),
                                    ALU.add).then_inc(vec_rwkv.sem, vec_rwkv.step(("drained", "pt", l, c, d)))
                        eng.wait_ge(vec_rwkv.sem, vec_rwkv.n)
                    for i in range(M - 1):
                        for d in range(2):
                            B = RW_D[d]
                            m = chain_order(d)[i]
                            e = 64 * m + (63 if d == 0 else 0)
                            eng.wait_ge(mid_filled.sem, mid_filled.at("dS", l, c, d, i))
                            ts(wk(B + YK + 64 * (i + 1), 64), mid.get("dS", l, c, d, i)[:, 0:64],
                                        work[:, B + WW + e:B + WW + e + 1], None, ALU.mult).then_inc(vec_rwkv.sem, vec_rwkv.step(("S", l, c, d, i + 1)))
                            eng.wait_ge(vec_rwkv.sem, vec_rwkv.n)
                            vec_rwkv.also(("drained", "dS", l, c, d, i))
                    eng.wait_ge(out_filled.sem, out_filled.at("O", l, c, 0))
                    cp(wk(RW_SCR), outb.get("O", l, c, 0)).then_inc(vec_rwkv.sem, vec_rwkv.step(("drained", "O", l, c, 0)))
                    eng.wait_ge(vec_rwkv.sem, vec_rwkv.n)
                    eng.wait_ge(out_filled.sem, out_filled.at("O", l, c, 1))
                    tt(wk(RW_SCR), wk(RW_SCR), outb.get("O", l, c, 1), ALU.add).then_inc(vec_rwkv.sem, vec_rwkv.step(("drained", "O", l, c, 1)))
                    eng.wait_ge(vec_rwkv.sem, vec_rwkv.n)
                    vec_rwkv.also(("o summed", l, c))
                    eng.wait_ge(big_filled.sem, big_filled.at("mean", l, c))
                    stt(wk(RW_SCR), big.get("mean", l, c), -1.0 / 64, wk(RW_SCR), ALU.mult, ALU.add).then_inc(vec_rwkv.sem, vec_rwkv.step(("drained", "mean", l, c)))
                    eng.wait_ge(vec_rwkv.sem, vec_rwkv.n)
                    eng.wait_ge(big_filled.sem, big_filled.at("bonus", l, c))
                    tt(wk(RW_SCR + 1536), big.get("bonus", l, c), vv, ALU.mult).then_inc(vec_rwkv.sem, vec_rwkv.step(("drained", "bonus", l, c)))
                    eng.wait_ge(vec_rwkv.sem, vec_rwkv.n)
                    eng.wait_ge(act_rwkv.sem, act_rwkv.at("rwkv rms", l, c))
                    tt(wk(RW_SCR), wk(RW_SCR), wk(RW_SCR + 1024), ALU.mult).then_inc(vec_rwkv.sem, vec_rwkv.step())
                    eng.wait_ge(vec_rwkv.sem, vec_rwkv.n)
                    ts(wk(RW_SCR), wk(RW_SCR), pcol(l, "lnw", c), pcol(l, "lnb", c), ALU.mult, ALU.add).then_inc(vec_rwkv.sem, vec_rwkv.step())
                    eng.wait_ge(vec_rwkv.sem, vec_rwkv.n)
                    tt(wk(RW_SCR), wk(RW_SCR), wk(RW_SCR + 1536), ALU.add).then_inc(vec_rwkv.sem, vec_rwkv.step())
                    eng.wait_ge(vec_rwkv.sem, vec_rwkv.n)
                    eng.wait_ge(big_filled.sem, big_filled.at("gate", l, c))
                    tt(wk(Y[0] + 512 * c), wk(RW_SCR), big.get("gate", l, c), ALU.mult).then_inc(vec_rwkv.sem, vec_rwkv.step(("drained", "gate", l, c)))
                    eng.wait_ge(vec_rwkv.sem, vec_rwkv.n)

                for h in range(4):
                    for dd in range(2):
                        F, K = wk(HG_F + 2048 * dd + 512 * h), wk(HG_K + 2048 * dd + 512 * h)
                        om, lo = dcol(D_OML + 8 * l + 4 * dd + h), dcol(D_LOW + 8 * l + 4 * dd + h)
                        eng.wait_ge(act_hgrn.sem, act_hgrn.at("forget sigmoid", l, h, dd))
                        ts(F, F, om, lo, ALU.mult, ALU.add).then_inc(vec_hgrn.sem, vec_hgrn.step())
                        eng.wait_ge(vec_hgrn.sem, vec_hgrn.n)
                        ts(K, K, om, None, ALU.mult).then_inc(vec_hgrn.sem, vec_hgrn.step())
                        eng.wait_ge(vec_hgrn.sem, vec_hgrn.n)
                    eng.wait_ge(act_hgrn.sem, act_hgrn.at("hq silu", l, h))
                    for dd in range(2):
                        tt(wk(HG_Q_of(dd, h)), wk(HG_T + 512 * (h % 2)), wk(HG_F + 2048 * dd + 512 * h), ALU.mult).then_inc(vec_hgrn.sem, vec_hgrn.step(("hq ready", l, h) if dd else None))
                        eng.wait_ge(vec_hgrn.sem, vec_hgrn.n)
                    if h > 0:
                        drain_diag(l, h - 1)
                drain_diag(l, 3)
                for j in range(9):
                    for h in range(4):
                        if j < 7:
                            eng.wait_ge(mid_filled.sem, mid_filled.at("hl", l, h, j))
                            diag = scores_diag(work, h)
                            for half in range(2):
                                msk = kc[:, K_HLEV + 128 * j:K_HLEV + 128 * j + 128].bitcast(U32) \
                                    .rearrange("p (a t) -> p a t", a=1).broadcast_to([P, 2, P])
                                nc.vector.copy_predicated(
                                    diag[half], msk,
                                    mid.get("hl", l, h, j)[:, 256 * half:256 * half + 256].rearrange("p (i t) -> p i t", t=P)).then_inc(vec_hgrn.sem, vec_hgrn.step(("drained", "hl", l, h, j) if half else None))
                                eng.wait_ge(vec_hgrn.sem, vec_hgrn.n)
                        if j < 8:
                            if j == 7:
                                eng.wait_ge(mid_filled.sem, mid_filled.at("hl", l, h, j))
                            if j > 0:
                                eng.wait_ge(pool_hgrn.sem, pool_hgrn.at("F up", l, h, j - 1))
                            b = 1 << j
                            for dd in range(2):
                                pair = lambda ap: ap.rearrange("p (n s b) -> p n s b", s=2, b=b)
                                side = 1 - dd
                                q = pair(wk(HG_Q_of(dd, h)))[:, :, side, :]
                                fe = pair(wk(HG_F + 2048 * dd + 512 * h))[:, :, 1 - side, 0:1].broadcast_to([P, N // (2 * b), b])
                                tt(q, q, fe, ALU.mult).then_inc(vec_hgrn.sem, vec_hgrn.step(("hq up", l, h, j) if dd else None))
                                eng.wait_ge(vec_hgrn.sem, vec_hgrn.n)
                for h in range(4):
                    eng.wait_ge(out_filled.sem, out_filled.at("hO", l, h))
                    o = HG_T + 1536 if h % 2 else HG_T
                    cp(wk(o), outb.get("hO", l, h)).then_inc(vec_hgrn.sem, vec_hgrn.step(("drained", "hO", l, h)))
                    eng.wait_ge(vec_hgrn.sem, vec_hgrn.n)
                    if h > 0:
                        hgrn_tail(l, h - 1)
                hgrn_tail(l, 3)
                vec_hgrn.also(("y ready", l))

                t0, t1 = rspan(l)
                n = t1 - t0
                for f in range(KT):
                    mg = wk(MG + 512 * f)[:, t0:t1]
                    for b in range(3):
                        eng.wait_ge(big_filled.sem, big_filled.at("br", l, f, b))
                        eng.wait_ge(act_merge.sem, act_merge.at("drained", "ga", l, f, b))
                        sg = work[:, MG_T + 512 * ((3 * f + b) % 3):MG_T + 512 * ((3 * f + b) % 3) + n]
                        o = mg if b == 0 else work[:, MG_T + 1536:MG_T + 1536 + n]
                        tt(o, big.get("br", l, f, b)[:, 0:n], sg, ALU.mult).then_inc(vec_merge.sem, vec_merge.step(("drained", "br", l, f, b)))
                        eng.wait_ge(vec_merge.sem, vec_merge.n)
                        if b:
                            tt(mg, mg, o, ALU.add).then_inc(vec_merge.sem, vec_merge.step(("merged", l, f) if b == 2 else None))
                            eng.wait_ge(vec_merge.sem, vec_merge.n)
                eng.wait_ge(x_back.sem, x_back.at("x back", l))
                for f in range(KT):
                    eng.wait_ge(big_filled.sem, big_filled.at("ot", l, f))
                    add_gated(vec_merge, big.get("ot", l, f), 16 + f, X + 512 * f, live(l), t0, ("drained", "ot", l, f))
                tail(l, 2)
                for f in range(KT):
                    eng.wait_ge(big_filled.sem, big_filled.at("m2", l, f))
                    add_gated(vec_mlp, big.get("m2", l, f), 40 + f, X + 512 * f, live(l), t0, ("drained", "m2", l, f))
            tail(L - 1, 3)

        @block.scalar
        def _(eng):
            act = nc.scalar.activation

            eng.dma_start(par[:, :], vec).then_inc(loaded_vectors.sem, loaded_vectors.step(None, 16))
            eng.dma_start(kc[:, :], con).then_inc(loaded_vectors.sem, loaded_vectors.step(("vectors",), 16))
            eng.dma_start(work[:, X:X + KT * N], xin).then_inc(loaded_x.sem, loaded_x.step(("x loaded",), 16))

            def rsqrt(done, dst, ps, scale, e, key, drained):
                act(dst, ps, ACT.Ln, bias=eps[e], scale=scale).then_inc(done.sem, done.step(drained))
                eng.wait_ge(done.sem, done.n)
                act(dst, dst, ACT.Exp, scale=-0.5).then_inc(done.sem, done.step(key))
                eng.wait_ge(done.sem, done.n)

            def norm(l, which):
                t0, t1 = (0, N) if which == 1 or l < L - 1 else (NC, N)
                if which == 3:
                    t0 = NC
                n = t1 - t0
                if which == 1 and l == 0:
                    eng.wait_ge(loaded_x.sem, loaded_x.at("x loaded"))
                elif which == 2:
                    eng.wait_ge(vec_merge.sem, vec_merge.at("drained", "ot", l, 7))
                else:
                    eng.wait_ge(vec_mlp.sem, vec_mlp.at("drained", "m2", l if which == 3 else l - 1, 7))
                for k in range(KT):
                    if k >= 2:
                        eng.wait_ge(big_filled.sem, big_filled.at("squares read", l, which, k - 2))
                    act(work[:, TN + 512 * (k % 2):TN + 512 * (k % 2) + n], wk(X + 512 * k)[:, t0:t1], ACT.Square).then_inc(act_norm.sem, act_norm.step(("square", l, which, k)))
                    eng.wait_ge(act_norm.sem, act_norm.n)
                eng.wait_ge(big_filled.sem, big_filled.at("squares read", l, which, 7))
                rsqrt(act_norm, work[:, TN + 1024:TN + 1024 + n], big.get("sumsq", l, which)[:, 0:n], 1.0 / D, "rms",
                      ("rms", l, which), ("drained", "sumsq", l, which))
                if which == 3:
                    return
                if which == 1:
                    eng.wait_ge(vec_cond.sem, vec_cond.at("vectors derived", l))
                ws, sh = (D_WS1, 0) if which == 1 else (D_WS2, 24)
                for k in range(KT):
                    eng.wait_ge(vec_norm.sem, vec_norm.at("x scaled", l, which, k))
                    o = TN + 1536 + 512 * (k % 2)
                    parts = [s for s in segs if s[1] >= t0]
                    for i, (sg, u0, u1) in enumerate(parts):
                        last = i == len(parts) - 1
                        act(hT[:, k, u0:u1], work[:, o + u0 - t0:o + u1 - t0], ACT.Identity,
                                     bias=mod[:, sh + k, sg:sg + 1], scale=dcol(ws + 2 * k + sg)).then_inc(act_norm.sem, act_norm.step(("h tile", l, which, k) if last else None))
                        eng.wait_ge(act_norm.sem, act_norm.n)
                act_norm.also(("h", l, which))

            eng.wait_ge(loaded_vectors.sem, loaded_vectors.at("vectors"))
            act(dcol(D_CS, 16), par[:, L * NPL + 8:L * NPL + 24], ACT.Silu).then_inc(act_cond.sem, act_cond.step(("cond silu",)))
            eng.wait_ge(act_cond.sem, act_cond.n)
            eng.wait_ge(vec_cond.sem, vec_cond.at("lb centred"))
            act(dcol(D_TMP + 8, 16), dcol(D_TMP + 8, 16), ACT.Exp).then_inc(act_cond.sem, act_cond.step(("lb exp",)))
            eng.wait_ge(act_cond.sem, act_cond.n)
            for l in range(L):
                if l > 0:
                    eng.wait_ge(big_filled.sem, big_filled.at("m2", l - 1, 7))
                act(dcol(D_LG, 8), pcol(l, "dec", 0, 8), ACT.Exp).then_inc(act_cond.sem, act_cond.step(("ret decay exp", l)))
                eng.wait_ge(act_cond.sem, act_cond.n)
                norm(l, 1)

                eng.dma_start(xscr, work[:, X:X + KT * N]).then_inc(x_saved.sem, x_saved.step(("x saved", l), 16))
                eng.wait_ge(vec_norm.sem, vec_norm.at("x scaled", l, 1, 7))
                eng.dma_start(wk(RT_CS, 1024), rcon[:, 0:1024]).then_inc(loaded_ret_constants.sem, loaded_ret_constants.step(None, 16))
                eng.dma_start(wk(RT_LAG, 2304), rcon[:, 1024:NRC]).then_inc(loaded_ret_constants.sem, loaded_ret_constants.step(("ret constants", l), 16))

                eng.wait_ge(loaded_ret_constants.sem, loaded_ret_constants.at("ret constants", l))
                lg = lambda dd, h: dcol(D_LG + 4 * dd + h)
                for h in range(4):
                    S, E = RT_STRIP + 768 * h, RT_A + 768 * h
                    act(wk(S, 384), wk(RT_LAG, 384), ACT.Exp, scale=lg(0, h)).then_inc(act_ret.sem, act_ret.step())
                    eng.wait_ge(act_ret.sem, act_ret.n)
                    act(wk(E, 384), wk(RT_LAG + 384, 384), ACT.Exp, scale=lg(1, h)).then_inc(act_ret.sem, act_ret.step())
                    eng.wait_ge(act_ret.sem, act_ret.n)
                    act(wk(S + 384, 384), wk(RT_LAG + 1536, 384), ACT.Exp, scale=lg(0, h)).then_inc(act_ret.sem, act_ret.step())
                    eng.wait_ge(act_ret.sem, act_ret.n)
                    act(wk(E + 384, 384), wk(RT_LAG + 1920, 384), ACT.Exp, scale=lg(1, h)).then_inc(act_ret.sem, act_ret.step(("strip exps", l, h)))
                    eng.wait_ge(act_ret.sem, act_ret.n)
                for what, c in ret_order:
                    qk = RT_QK + 1024 * (c % 2)
                    if what == "P":
                        for i, n in enumerate(("rq", "rk")):
                            eng.wait_ge(big_filled.sem, big_filled.at(n, l, c))
                            act(wk(qk + 512 * i), big.get(n, l, c), ACT.Copy).then_inc(act_ret.sem, act_ret.step(("drained", n, l, c)))
                            eng.wait_ge(act_ret.sem, act_ret.n)
                        eng.wait_ge(big_filled.sem, big_filled.at("rv", l, c))
                        act(wk(RT_V + 512 * (c % 2)), big.get("rv", l, c), ACT.Copy).then_inc(act_ret.sem, act_ret.step(("drained", "rv", l, c)))
                        eng.wait_ge(act_ret.sem, act_ret.n)
                        eng.wait_ge(big_filled.sem, big_filled.at("rg", l, c))
                        act(wk(Y[YR] + 512 * c), big.get("rg", l, c), ACT.Silu).then_inc(act_ret.sem, act_ret.step(("drained", "rg", l, c)))
                        eng.wait_ge(act_ret.sem, act_ret.n)
                    if what == "N":
                        eng.wait_ge(big_filled.sem, big_filled.at("rN", l, c))
                        rsqrt(act_ret, wk(RT_O + 1024), big.get("rN", l, c), 1.0 / P, "rms", ("ret rms", l, c), ("drained", "rN", l, c))

                eng.wait_ge(vec_ret.sem, vec_ret.at("ret y", l, 3))
                eng.dma_start(wk(RW_W, 2304), wsm[l]).then_inc(loaded_small_weights.sem, loaded_small_weights.step(("small weights", l), 16))

                def raw(i, ps, key):
                    if i != 12:
                        eng.wait_ge(vec_rwkv.sem, vec_rwkv.at("mixed", l, last_mixed[0]))
                    act(wk(RW_SCR + 1, NC), ps[:, 0:NC], ACT.Copy).then_inc(act_rwkv.sem, act_rwkv.step())
                    eng.wait_ge(act_rwkv.sem, act_rwkv.n)
                    grid = wk(RW_SCR + 258, 396).rearrange("p (r t) -> p r t", t=66)[:, 1:5, 1:65]
                    act(grid, ps[:, NC:N].rearrange("p (r t) -> p r t", t=GRID), ACT.Copy).then_inc(act_rwkv.sem, act_rwkv.step(key))
                    eng.wait_ge(act_rwkv.sem, act_rwkv.n)
                    act_rwkv.also(("raw", l, i))
                    last_mixed[0] = i

                last_mixed = [None]
                eng.wait_ge(pool_rwkv.sem, pool_rwkv.at("pads rwkv", l, -1))
                for j in range(3):
                    eng.wait_ge(big_filled.sem, big_filled.at("small", l, j))
                    raw(12 + j, big.get("small", l, j), ("drained", "small", l, j))
                if l > 0:
                    eng.wait_ge(big_filled.sem, big_filled.at("vd", l))
                    act(work[0:32, RW_VD:RW_VD + N], big.get("vd", l)[0:32, :], ACT.Copy).then_inc(act_rwkv.sem, act_rwkv.step(("drained", "vd", l)))
                    eng.wait_ge(act_rwkv.sem, act_rwkv.n)
                eng.wait_ge(vec_rwkv.sem, vec_rwkv.at("mixed", l, 12))
                act(wk(RW_SMALL), wk(RW_SMALL), ACT.Tanh).then_inc(act_rwkv.sem, act_rwkv.step())
                eng.wait_ge(act_rwkv.sem, act_rwkv.n)
                eng.wait_ge(vec_rwkv.sem, vec_rwkv.at("mixed", l, 14))
                act(wk(RW_SMALL + 1024), wk(RW_SMALL + 1024), ACT.Sigmoid).then_inc(act_rwkv.sem, act_rwkv.step(("small ready", l)))
                eng.wait_ge(act_rwkv.sem, act_rwkv.n)
                for c in range(NT):
                    if c > 0:
                        eng.wait_ge(pool_rwkv.sem, pool_rwkv.at("pads rwkv", l, c - 1))
                    for j in range(3):
                        eng.wait_ge(big_filled.sem, big_filled.at("rkv", l, c, j))
                        raw(4 * j + c, big.get("rkv", l, c, j), ("drained", "rkv", l, c, j))
                    eng.wait_ge(vec_rwkv.sem, vec_rwkv.at("mixed", l, 8 + c))
                    if l > 0:
                        eng.wait_ge(big_filled.sem, big_filled.at("vgate", l, c))
                        act(wk(RW_SCR), big.get("vgate", l, c), ACT.Sigmoid, bias=pcol(l, "v0", c)).then_inc(act_rwkv.sem, act_rwkv.step(("drained", "vgate", l, c)))
                        eng.wait_ge(act_rwkv.sem, act_rwkv.n)
                        act_rwkv.also(("vgate sigmoid", l, c))
                    eng.wait_ge(big_filled.sem, big_filled.at("kk norm", l, c))
                    rsqrt(act_rwkv, wk(RW_SQ), big.get("kk norm", l, c), 1.0, "l2", ("kk rms", l, c), ("drained", "kk norm", l, c))
                    for d in range(2):
                        B = RW_D[d]
                        eng.wait_ge(big_filled.sem, big_filled.at("zw", l, c, d))
                        act(wk(B + WW), big.get("zw", l, c, d), ACT.Sigmoid, bias=pcol(l, "w0", 4 * d + c)).then_inc(act_rwkv.sem, act_rwkv.step(("drained", "zw", l, c, d)))
                        eng.wait_ge(act_rwkv.sem, act_rwkv.n)
                        act_rwkv.also(("decay sigmoid", l, c, d))
                        eng.wait_ge(big_filled.sem, big_filled.at("za", l, c, d))
                        act(wk(B + BT), big.get("za", l, c, d), ACT.Sigmoid, bias=pcol(l, "a0", 4 * d + c)).then_inc(act_rwkv.sem, act_rwkv.step(("drained", "za", l, c, d)))
                        eng.wait_ge(act_rwkv.sem, act_rwkv.n)
                        act_rwkv.also(("a sigmoid", l, c, d))
                    for d in range(2):
                        B = RW_D[d]
                        eng.wait_ge(vec_rwkv.sem, vec_rwkv.at("decay sums", l, c, d))
                        act(wk(B + WW), wk(RW_SCR + 512 * d), ACT.Exp, scale=-DECAY).then_inc(act_rwkv.sem, act_rwkv.step())
                        eng.wait_ge(act_rwkv.sem, act_rwkv.n)
                        act(wk(RW_SCR + 1024 + 512 * d), wk(RW_SCR + 512 * d), ACT.Exp, scale=DECAY).then_inc(act_rwkv.sem, act_rwkv.step(("decays", l, c, d)))
                        eng.wait_ge(act_rwkv.sem, act_rwkv.n)
                    eng.wait_ge(mid_filled.sem, mid_filled.at("vT", l, c))
                    act(wk(RW_VT), mid.get("vT", l, c), ACT.Copy).then_inc(act_rwkv.sem, act_rwkv.step(("drained", "vT", l, c)))
                    eng.wait_ge(act_rwkv.sem, act_rwkv.n)
                    for d in range(2):
                        B = RW_D[d]
                        for n, dst in (("tkk", chunks(B + YK, 64, 64, 128)), ("tb", chunks(B + BTT)), ("tk", chunks(B + KTT))):
                            eng.wait_ge(mid_filled.sem, mid_filled.at(n, l, c, d))
                            act(dst, mid.get(n, l, c, d).rearrange("p (m t) -> p m t", t=64), ACT.Copy).then_inc(act_rwkv.sem, act_rwkv.step(("drained", n, l, c, d)))
                            eng.wait_ge(act_rwkv.sem, act_rwkv.n)
                    for d in range(2):
                        B = RW_D[d]
                        eng.wait_ge(mid_filled.sem, mid_filled.at("mv", l, c, d))
                        act(chunks(B + YK, 64, 0, 128), mid.get("mv", l, c, d).rearrange("p (m t) -> p m t", t=64),
                                     ACT.Copy).then_inc(act_rwkv.sem, act_rwkv.step(("drained", "mv", l, c, d)))
                        eng.wait_ge(act_rwkv.sem, act_rwkv.n)
                    for j in range(1, 6):
                        for d in range(2):
                            B = RW_D[d]
                            eng.wait_ge(mid_filled.sem, mid_filled.at("Z", l, c, d, j))
                            act(wk(B + MT), mid.get("Z", l, c, d, j), ACT.Copy).then_inc(act_rwkv.sem, act_rwkv.step(("drained", "Z", l, c, d, j)))
                            eng.wait_ge(act_rwkv.sem, act_rwkv.n)
                    for d in range(2):
                        B = RW_D[d]
                        eng.wait_ge(wide_filled.sem, wide_filled.at("uk", l, c, d))
                        act(wk(B + LT, 1024), wide.get("uk", l, c, d), ACT.Copy, scale=-1.0).then_inc(act_rwkv.sem, act_rwkv.step(("drained", "uk", l, c, d)))
                        eng.wait_ge(act_rwkv.sem, act_rwkv.n)
                    eng.wait_ge(big_filled.sem, big_filled.at("var", l, c))
                    rsqrt(act_rwkv, wk(RW_SCR + 1024), big.get("var", l, c), 1.0 / 64, "ln", ("rwkv rms", l, c),
                          ("drained", "var", l, c))

                eng.wait_ge(vec_rwkv.sem, vec_rwkv.at("drained", "gate", l, 3))
                for i in range(4):
                    eng.wait_ge(big_filled.sem, big_filled.at("hi", l, i))
                    act(wk(HG_V + 512 * i), big.get("hi", l, i), ACT.Copy).then_inc(act_hgrn.sem, act_hgrn.step(("drained", "hi", l, i)))
                    eng.wait_ge(act_hgrn.sem, act_hgrn.n)
                for h in range(4):
                    for dd in range(2):
                        eng.wait_ge(big_filled.sem, big_filled.at("hf", l, h, dd))
                        ps = big.get("hf", l, h, dd)
                        act(wk(HG_F + 2048 * dd + 512 * h), ps, ACT.Sigmoid).then_inc(act_hgrn.sem, act_hgrn.step())
                        eng.wait_ge(act_hgrn.sem, act_hgrn.n)
                        act(wk(HG_K + 2048 * dd + 512 * h), ps, ACT.Sigmoid, scale=-1.0).then_inc(act_hgrn.sem, act_hgrn.step(("drained", "hf", l, h, dd)))
                        eng.wait_ge(act_hgrn.sem, act_hgrn.n)
                        act_hgrn.also(("forget sigmoid", l, h, dd))
                    eng.wait_ge(big_filled.sem, big_filled.at("hf", l, h, 2))
                    if h >= 2:
                        eng.wait_ge(mid_filled.sem, mid_filled.at("hd", l, h - 2))
                    act(wk(HG_T + 512 * (h % 2)), big.get("hf", l, h, 2), ACT.Silu).then_inc(act_hgrn.sem, act_hgrn.step(("drained", "hf", l, h, 2)))
                    eng.wait_ge(act_hgrn.sem, act_hgrn.n)
                    act_hgrn.also(("hq silu", l, h))
                    eng.wait_ge(big_filled.sem, big_filled.at("hf", l, h, 3))
                    act(wk(Y[YH] + 512 * h), big.get("hf", l, h, 3), ACT.Silu).then_inc(act_hgrn.sem, act_hgrn.step(("drained", "hf", l, h, 3)))
                    eng.wait_ge(act_hgrn.sem, act_hgrn.n)
                for h in range(4):
                    A = HG_A + 1536 * h
                    eng.wait_ge(mid_filled.sem, mid_filled.at("hl", l, h, 7))
                    ps = mid.get("hl", l, h, 7)
                    for i, o in enumerate((128, 512, 1152, 1280)):
                        act(wk(A + o, P), ps[:, P * i:P * i + P], ACT.Copy).then_inc(act_hgrn.sem, act_hgrn.step(("drained", "hl", l, h, 7) if i == 3 else None))
                        eng.wait_ge(act_hgrn.sem, act_hgrn.n)
                for h in range(4):
                    A = HG_A + 1536 * h
                    eng.wait_ge(mid_filled.sem, mid_filled.at("hl", l, h, 8))
                    ps = mid.get("hl", l, h, 8)
                    for i in range(2):
                        act(wk(A + 512 * i + 256, 256), ps[:, 256 * i:256 * i + 256], ACT.Copy).then_inc(act_hgrn.sem, act_hgrn.step(("drained", "hl", l, h, 8) if i else None))
                        eng.wait_ge(act_hgrn.sem, act_hgrn.n)
                for h in range(4):
                    eng.wait_ge(big_filled.sem, big_filled.at("hN", l, h))
                    rsqrt(act_hgrn, wk(HG_T + 512 + 512 * (h % 2)), big.get("hN", l, h), 1.0 / P, "rms", ("hgrn rms", l, h),
                          ("drained", "hN", l, h))

                t0, t1 = rspan(l)
                n = t1 - t0
                eng.wait_ge(vec_hgrn.sem, vec_hgrn.at("y ready", l))
                eng.wait_ge(x_saved.sem, x_saved.at("x saved", l))
                eng.dma_start(work[:, X:X + KT * N], xscr).then_inc(x_back.sem, x_back.step(("x back", l), 16))
                for f in range(KT):
                    for b in range(3):
                        i = 3 * f + b
                        eng.wait_ge(big_filled.sem, big_filled.at("ga", l, f, b))
                        if i >= 3:
                            eng.wait_ge(vec_merge.sem, vec_merge.at("drained", "br", l, (i - 3) // 3, (i - 3) % 3))
                        act(work[:, MG_T + 512 * (i % 3):MG_T + 512 * (i % 3) + n],
                                     big.get("ga", l, f, b)[:, 0:n], ACT.Sigmoid).then_inc(act_merge.sem, act_merge.step(("drained", "ga", l, f, b)))
                        eng.wait_ge(act_merge.sem, act_merge.n)
                norm(l, 2)
                for f in range(32):
                    eng.wait_ge(big_filled.sem, big_filled.at("m1", l, f))
                    act(work[:, hid(f) + t0:hid(f) + t1], big.get("m1", l, f)[:, 0:n], ACT.Relu).then_inc(act_mlp.sem, act_mlp.step(("drained", "m1", l, f)))
                    eng.wait_ge(act_mlp.sem, act_mlp.n)
            norm(L - 1, 3)

        @block.gpsimd
        def _(eng):
            tt = nc.gpsimd.tensor_tensor
            for l in range(L):
                for what, c in ret_order:
                    if what == "O":
                        eng.wait_ge(vec_ret.sem, vec_ret.at("drained", "rO", l, c))
                        if c > 0:
                            eng.wait_ge(big_filled.sem, big_filled.at("rN", l, c - 1))
                        tt(wk(RT_O + 512), wk(RT_O), wk(RT_O), ALU.mult).then_inc(pool_ret.sem, pool_ret.step(("ret squared", l, c)))
                        eng.wait_ge(pool_ret.sem, pool_ret.n)
                def pads(c):
                    nc.gpsimd.memset(wk(RW_SCR, 654), 0.0).then_inc(pool_rwkv.sem, pool_rwkv.step(("pads rwkv", l, c)))
                    eng.wait_ge(pool_rwkv.sem, pool_rwkv.n)

                def neighbours(i):
                    eng.wait_ge(act_rwkv.sem, act_rwkv.at("raw", l, i))
                    S = RW_SCR + 654
                    tt(wk(S, NC), wk(RW_SCR, NC), wk(RW_SCR + 2, NC), ALU.add).then_inc(pool_rwkv.sem, pool_rwkv.step())
                    eng.wait_ge(pool_rwkv.sem, pool_rwkv.n)
                    grid = wk(RW_SCR + 258, 396).rearrange("p (r t) -> p r t", t=66)
                    s3 = wk(S + NC, NC).rearrange("p (r t) -> p r t", t=GRID)
                    tt(s3, grid[:, 0:4, 1:65], grid[:, 2:6, 1:65], ALU.add).then_inc(pool_rwkv.sem, pool_rwkv.step())
                    eng.wait_ge(pool_rwkv.sem, pool_rwkv.n)
                    tt(s3, s3, grid[:, 1:5, 0:64], ALU.add).then_inc(pool_rwkv.sem, pool_rwkv.step())
                    eng.wait_ge(pool_rwkv.sem, pool_rwkv.n)
                    tt(s3, s3, grid[:, 1:5, 2:66], ALU.add).then_inc(pool_rwkv.sem, pool_rwkv.step(("neighbours", l, i)))
                    eng.wait_ge(pool_rwkv.sem, pool_rwkv.n)

                eng.wait_ge(vec_ret.sem, vec_ret.at("ret y", l, 3))
                pads(-1)
                for j in range(3):
                    neighbours(12 + j)
                for c in range(NT):
                    for j in range(3):
                        neighbours(4 * j + c)
                    eng.wait_ge(vec_rwkv.sem, vec_rwkv.at("kk raw", l, c))
                    tt(wk(RW_SQ), wk(RW_KK), wk(RW_KK), ALU.mult).then_inc(pool_rwkv.sem, pool_rwkv.step(("kk squared", l, c)))
                    eng.wait_ge(pool_rwkv.sem, pool_rwkv.n)
                    eng.wait_ge(vec_rwkv.sem, vec_rwkv.at("kk ready", l, c))
                    for d in range(2):
                        B = RW_D[d]
                        eng.wait_ge(vec_rwkv.sem, vec_rwkv.at("a read", l, c, d))
                        tt(wk(B + BT), wk(B + BT), wk(RW_KK), ALU.mult).then_inc(pool_rwkv.sem, pool_rwkv.step())
                        eng.wait_ge(pool_rwkv.sem, pool_rwkv.n)
                    for d in range(2):
                        B = RW_D[d]
                        eng.wait_ge(act_rwkv.sem, act_rwkv.at("decays", l, c, d))
                        tt(wk(B + BT), wk(B + BT), wk(RW_SCR + 1024 + 512 * d), ALU.mult).then_inc(pool_rwkv.sem, pool_rwkv.step(("b ready", l, c, d)))
                        eng.wait_ge(pool_rwkv.sem, pool_rwkv.n)
                    for j in range(1, 6):
                        for d in range(2):
                            B = RW_D[d]
                            if j == 1:
                                eng.wait_ge(mid_filled.sem, mid_filled.at("tk", l, c, d))
                                eng.wait_ge(vec_rwkv.sem, vec_rwkv.at("level", l, c, d, 0))
                            elif j == 2:
                                eng.wait_ge(mid_filled.sem, mid_filled.at("l1", l, c, d))
                                eng.wait_ge(vec_rwkv.sem, vec_rwkv.at("R first", l, c, d))
                            else:
                                eng.wait_ge(mid_filled.sem, mid_filled.at("Z", l, c, d, j - 2))
                            tt(chunks(B + (KTI if j % 2 else BT)), chunks(B + LT),
                                        over_chunks(kcol(K_LEV + 64 * j, 64), 64), ALU.mult).then_inc(pool_rwkv.sem, pool_rwkv.step(("level", l, c, d, j)))
                            eng.wait_ge(pool_rwkv.sem, pool_rwkv.n)
                    eng.wait_ge(vec_rwkv.sem, vec_rwkv.at("drained", "mean", l, c))
                    tt(wk(RW_SCR + 512), wk(RW_SCR), wk(RW_SCR), ALU.mult).then_inc(pool_rwkv.sem, pool_rwkv.step(("centred squared", l, c)))
                    eng.wait_ge(pool_rwkv.sem, pool_rwkv.n)
                    if c < NT - 1:
                        eng.wait_ge(vec_rwkv.sem, vec_rwkv.at("drained", "gate", l, c))
                        pads(c)
                eng.wait_ge(vec_rwkv.sem, vec_rwkv.at("drained", "gate", l, 3))
                for h in range(4):
                    nc.gpsimd.memset(wk(HG_A + 1536 * h, 1536), 0.0).then_inc(pool_hgrn.sem, pool_hgrn.step(("scores clear", l, h)))
                    eng.wait_ge(pool_hgrn.sem, pool_hgrn.n)
                for j in range(8):
                    for h in range(4):
                        eng.wait_ge(mid_filled.sem, mid_filled.at("hl", l, h, j))
                        b = 1 << j
                        for dd in range(2):
                            pair = lambda ap: ap.rearrange("p (n s b) -> p n s b", s=2, b=b)
                            side = dd
                            k = pair(wk(HG_K + 2048 * dd + 512 * h))[:, :, side, :]
                            fe = pair(wk(HG_F + 2048 * dd + 512 * h))[:, :, 1 - side, 0:1].broadcast_to([P, N // (2 * b), b])
                            tt(k, k, fe, ALU.mult).then_inc(pool_hgrn.sem, pool_hgrn.step(("hk up", l, h, j) if dd else None))
                            eng.wait_ge(pool_hgrn.sem, pool_hgrn.n)
                        eng.wait_ge(vec_hgrn.sem, vec_hgrn.at("hq up", l, h, j))
                        if j < 7:
                            for dd in range(2):
                                f = pair(wk(HG_F + 2048 * dd + 512 * h))
                                tt(f[:, :, 0, 0:1], f[:, :, 0, 0:1], f[:, :, 1, 0:1], ALU.mult).then_inc(pool_hgrn.sem, pool_hgrn.step(("F up", l, h, j) if dd else None))
                                eng.wait_ge(pool_hgrn.sem, pool_hgrn.n)
                for h in range(4):
                    eng.wait_ge(vec_hgrn.sem, vec_hgrn.at("drained", "hO", l, h))
                    if h >= 2:
                        eng.wait_ge(vec_hgrn.sem, vec_hgrn.at("hgrn y", l, h - 2))
                    o = HG_T + 1536 if h % 2 else HG_T
                    tt(wk(HG_T + 512 + 512 * (h % 2)), wk(o), wk(o), ALU.mult).then_inc(pool_hgrn.sem, pool_hgrn.step(("hgrn squared", l, h)))
                    eng.wait_ge(pool_hgrn.sem, pool_hgrn.n)
                t0, t1 = rspan(l)
                for f in range(32):
                    eng.wait_ge(act_mlp.sem, act_mlp.at("drained", "m1", l, f))
                    h_ = work[:, hid(f) + t0:hid(f) + t1]
                    tt(h_, h_, h_, ALU.mult).then_inc(pool_mlp.sem, pool_mlp.step(("hidden", l, f)))
                    eng.wait_ge(pool_mlp.sem, pool_mlp.n)

        @block.sync
        def _(eng):
            for i, (key, n) in enumerate(slots):
                if i >= RING:
                    eng.wait_ge(big_filled.sem, big_filled.at(*last_use(slots[i - RING][0])))
                eng.dma_start(ring[:, i % RING, 0:n], wts[i][:, 0:n]).then_inc(weights[i % RING].sem, weights[i % RING].step(None, 16))
            for k in range(KT):
                eng.wait_ge(vec_norm.sem, vec_norm.at("final", k))
                eng.dma_start(out[P * k:P * k + P, :], work[:, X + 512 * k + NC:X + 512 * k + N]).then_inc(stored.sem, stored.step(None, 16))
            eng.wait_ge(stored.sem, stored.n)
            eng.wait_ge(x_saved.sem, 16 * L)
    return log


def last_use(key):
    kind, l, *i = key
    return {"ada": lambda: ("ada", l, *i), "ret": lambda: ("rg", l, *i), "small": lambda: ("small", l, 2),
            "rw": lambda: ("rkv", l, *i, 2), "hi": lambda: ("hi", l, 3), "hf": lambda: ("hf", l, *i, 3),
            "gb": lambda: ("br", l, *i, 2), "out": lambda: ("ot", l, 4 * i[0] + 3),
            "m1": lambda: ("m1", l, 4 * i[0] + 3), "m2": lambda: ("m2", l, *i)}[kind]()


def hid(f):
    return 512 * f if f < 12 else 14336 + 512 * (f - 12)


def wsm_up(work, wcol):
    return work[0:32, RW_W + 1792 + wcol.start:RW_W + 1792 + wcol.stop]


def HG_Q_of(dd, h):
    return HG_Q + 2048 * dd + 512 * h


def ident64(kc):
    return kc[:, K_ID2:K_ID2 + C].rearrange("p (a t) -> p a t", a=1).broadcast_to([P, M, C])


def scores_diag(work, h):
    A = HG_A + 1536 * h
    ctx = work[:, A:A + 1280].rearrange("p (i t) -> p i t", t=640)[:, :, 0:P]
    lat = work[:, A + 1024:A + 1024 + 768].rearrange("p (i t) -> p i t", t=384)[:, :, 0:P]
    return ctx, lat


def constants():
    k = np.zeros((P, NCONST), np.float32)
    p = np.arange(P)
    k[:, K_ID:K_ID + P] = np.eye(P)
    k[:, K_ONE:K_ONE + P] = 1
    k[:, K_BONE:K_BONE + P] = p[:, None] // 64 == p[None] // 64
    k[:, K_ROT:K_ROT + P] = 1.0 * (p[:, None] == p[None] - 64) - 1.0 * (p[:, None] == p[None] + 64)
    s, t = (p % 64)[:, None], np.arange(64)[None]
    k[:, K_STRICT:K_STRICT + 64], k[:, K_STRICT + 64:K_STRICT + 128] = s < t, s > t
    k[:, K_INCL:K_INCL + 64], k[:, K_INCL + 64:K_INCL + 128] = s <= t, s >= t
    for j in range(6):
        k[:, K_LEV + 64 * j:K_LEV + 64 * j + 64] = (s ^ t) >> j == 1
    for j in range(7):
        k[:, K_HLEV + P * j:K_HLEV + P * j + P] = (p[:, None] ^ p[None]) >> j == 1
    t = np.arange(N)
    k[:, K_SCAN:K_SCAN + N], k[:, K_SCAN + N:K_SCAN + 2 * N] = t % C != 0, t % C != C - 1
    k[:, K_EPS], k[:, K_EPS + 1], k[:, K_EPS + 2] = 1e-6, 64e-5, 1e-12
    k[:, K_ID2:K_ID2 + 64] = (p % 64)[:, None] == np.arange(64)[None]

    r = np.zeros((P, NRC), np.float32)
    half = P // 2
    inv = np.float32(10000.0) ** (-np.arange(half, dtype=np.float32) / np.float32(half))
    ang = np.arange(N, dtype=np.float32)[None] * inv[:, None]
    r[:, R_COS:R_COS + N] = np.tile(np.cos(ang), (2, 1))
    r[:, R_SIN:R_SIN + N] = np.tile(np.sin(ang), (2, 1))
    lag = np.arange(384)[None] - P - p[:, None]
    cross = lag + 2 * P
    for i, a in enumerate((np.maximum(lag, 0), np.maximum(-lag, 0), lag >= 0, lag <= 0, cross, N - cross)):
        r[:, R_LAG + 384 * i:R_LAG + 384 * i + 384] = a
    return k, r


def lay_out(inp):
    slots = schedule_slots()
    w = np.zeros((len(slots), P, SLOT), np.float32)

    def tiles(m):
        return m.reshape(m.shape[0] // P, P, m.shape[1] // P, P).transpose(1, 2, 0, 3)

    rw = np.cumsum([0, BW, BW, BW, 128, 128, 128])
    ret0 = int(rw[-1])
    hg0 = ret0 + 4 * BW
    ga0 = hg0 + 5 * BW
    for i, ((kind, l, *a), n) in enumerate(slots):
        wi = inp["w_in"][l]
        cut = lambda o: wi[:, o:o + P]
        if kind == "ada":
            m = tiles(inp["ada_w"][l][:, 4 * P * a[0]:4 * P * a[0] + 4 * P])
        elif kind == "ret":
            m = tiles(np.concatenate([cut(ret0 + BW * j + P * a[0]) for j in range(4)], 1))
        elif kind == "small":
            m = tiles(wi[:, 3 * BW:3 * BW + 3 * P])
        elif kind == "rw":
            m = tiles(np.concatenate([cut(BW * j + P * a[0]) for j in range(3)], 1))
        elif kind == "hi":
            m = wi[:, hg0 + 3 * BW:hg0 + 4 * BW].reshape(KT, P, BW).transpose(1, 0, 2)
        elif kind == "hf":
            m = tiles(np.concatenate([cut(hg0 + BW * j + P * a[0]) for j in (1, 2, 0, 4)], 1))
        elif kind == "gb":
            gates = tiles(np.concatenate([cut(ga0 + D * b + P * a[0]) for b in range(3)], 1)).reshape(P, -1)
            outs = [tiles(inp["w_branch"][l, b][:, P * a[0]:P * a[0] + P]).reshape(P, -1) for b in range(3)]
            m = np.concatenate([gates] + outs, 1)
        elif kind == "out":
            m = tiles(inp["w_out"][l][:, 4 * P * a[0]:4 * P * a[0] + 4 * P])
        elif kind == "m1":
            m = tiles(inp["mlp_w1"][l][:, 4 * P * a[0]:4 * P * a[0] + 4 * P])
        else:
            m = tiles(inp["mlp_w2"][l][:, P * a[0]:P * a[0] + P])
        w[i, :, :n] = m.reshape(P, n)

    small = np.zeros((L, P, 2304), np.float32)
    for l in range(L):
        small[l, :, 0:512] = inp["rwkv_w_up"][l].reshape(P, BW)
        small[l, :, 512:1024] = inp["rwkv_a_up"][l].reshape(P, BW)
        small[l, :, 1024:1536] = inp["rwkv_g_up"][l]
        if l:
            small[l, :, 1536:1792] = inp["rwkv_v_down"][l - 1].reshape(KT, P, 32).transpose(1, 0, 2).reshape(P, 256)
            small[l, 0:32, 1792:2304] = inp["rwkv_v_up"][l - 1]

    vec = np.zeros((P, NPAR), np.float32)
    col = lambda a: np.asarray(a).reshape(-1, P).T
    for l in range(L):
        got = dict(mu=inp["rwkv_mu"][l], w0=inp["rwkv_w0"][l], a0=inp["rwkv_a0"][l], kk=inp["rwkv_k_k"][l],
                   ka=inp["rwkv_k_a"][l], rk=inp["rwkv_r_k"][l], lnw=inp["rwkv_lnx_w"][l], lnb=inp["rwkv_lnx_b"][l],
                   lb=inp["hgrn_lb"][l], hnw=inp["hgrn_norm_w"][l], n1=inp["norm1_w"][l], n2=inp["norm2_w"][l],
                   adab=inp["ada_b"][l])
        if l:
            got["v0"] = inp["rwkv_v0"][l - 1]
        for name, a in got.items():
            vec[:, l * NPL + COL[name]:l * NPL + COL[name] + PARTS[name]] = col(a)
        vec[:, l * NPL + COL["dec"]:l * NPL + COL["dec"] + 8] = inp["ret_decay"][l].reshape(1, 8)
    vec[:, L * NPL:L * NPL + 8] = col(inp["final_norm_w"])
    cond = np.stack([inp["c_ctx"], inp["c"][0]])
    vec[:, L * NPL + 8:] = cond.reshape(2, KT, P).transpose(2, 1, 0).reshape(P, 16)
    x = np.concatenate([inp["ctx"][0], inp["x"][0]], 0)
    x = x.T.reshape(KT, P, N).transpose(1, 0, 2).reshape(P, KT * N)
    con, rcon = constants()
    return dict(weights=w, small_weights=small, vectors=vec, constants=con, ret_constants=rcon,
                x=np.ascontiguousarray(x))


def kernel(**inputs):
    import concourse.bacc as bacc
    from concourse.bass_utils import run_bass_kernel_spmd

    inp = {k: np.asarray(v) for k, v in inputs.items()}
    arrays = lay_out(inp)

    def program(known):
        nc = bacc.Bacc("TRN2", target_bir_lowering=False, num_devices=1)
        a = {k: nc.dram_tensor(f"in_{k}", v.shape, F32, kind="ExternalInput").ap() for k, v in arrays.items()}
        xscr = nc.dram_tensor("x_scratch", (P, KT * N), F32, kind="Internal").ap()
        out = nc.dram_tensor("out", (D, N - NC), F32, kind="ExternalOutput").ap()
        marks = build_program(nc, known, a["weights"], a["small_weights"], a["vectors"], a["constants"],
                              a["ret_constants"], a["x"], xscr, out)
        return nc, marks

    _, marks = program(None)
    nc, _ = program(marks)
    r = run_bass_kernel_spmd(nc, [{f"in_{k}": v for k, v in arrays.items()}], core_ids=[0])
    return np.ascontiguousarray(r.results[0]["out"].T)[None]
```

```python
import numpy as np
import concourse.bass as bass
import concourse.mybir as mybir
from contextlib import ExitStack

F32 = mybir.dt.float32
U32 = mybir.dt.uint32
ALU = mybir.AluOpType
ACT = mybir.ActivationFunctionType

P = 128
D = 1024
KT = D // P
N = 512
NC = 256
L = 2
BW = 512
NT = BW // P
C = 64
M = N // C
FF = 4 * D
GRID = 64
ROWS = (N - NC) // GRID
SLOT = KT * P * 3 + NT * P * 3
RING = 3
DECAY = float(np.exp(-0.5))

K_ID, K_ONE, K_BONE, K_ROT = 0, 128, 256, 384
K_STRICT, K_INCL, K_LEV = 512, 640, 768
K_HLEV = 1152
K_SCAN = 2048
K_EPS = 3072
K_ID2 = 3076
NCONST = 3140
R_COS, R_SIN, R_LAG = 0, 512, 1024
NRC = 1024 + 6 * 384

PARTS = dict(mu=15, w0=8, a0=8, kk=4, ka=4, rk=4, lnw=4, lnb=4, v0=4, lb=8, hnw=4, n1=8, n2=8, adab=48, dec=8)
COL, NPL = {}, 0
for _n, _w in PARTS.items():
    COL[_n] = NPL
    NPL += _w
NPAR = L * NPL + 8 + 16

D_MOD, D_HMU, D_QMU, D_OMU, D_OMKA, D_WS1, D_WS2, D_LG, D_CS, D_LOW, D_OML = (
    0, 96, 111, 126, 141, 145, 161, 177, 185, 201, 217)
D_TMP = 233
NDER = 265

Y = [0, 2048, 4096]
YR, YH = 1, 2
X = 10240
TN = 24576
RT_A = 7168
RT_CS, RT_LAG, RT_STRIP = 6144, 14336, 16640
RT_QK, RT_V, RT_ROT, RT_O = 19712, 21760, 22784, 23808
RW_D = [4096, 11776]
RW_SCR, RW_KK, RW_SQ, RW_KS, RW_VT = 19456, 21504, 22016, 22528, 23040
RW_RKV, RW_SMALL, RW_W, RW_VD = 23552, 25088, 26624, 28928
(KR, BT, KTI, LT, TT, ABT, MT, AKT, RR, YK, BTT, KTT, WW) = (
    0, 1024, 1536, 2048, 2560, 3072, 3584, 4096, 4608, 5120, 6144, 6656, 7168)
HG_F, HG_Q, HG_K, HG_A, HG_V, HG_T = 6144, 10240, 14336, 18432, 24576, 26624
MG, MG_T = 14336, 18432
WORK = 29440
ROWS2 = 28928


ADA_AT = {
    ("start", 0): [(0, 0), (0, 1), (0, 2), (0, 3), None], ("norm1", 0): [(0, 4), (0, 5)], ("strips", 0): [(0, 6)],
    ("small", 0): [(0, 7)],
    ("kk", 0, 0): [(0, 8)], ("kk", 0, 1): [(0, 9)], ("kk", 0, 2): [(0, 10)], ("kk", 0, 3): [(1, 3)],
    ("keys", 0, 0): [(1, 0)], ("keys", 0, 1): [(1, 1)], ("keys", 0, 2): [(1, 2)],
    ("out", 0): [(0, 11)], ("norm2", 0): [(1, 4), (1, 5)],
    ("norm1", 1): [(1, 6), (1, 7)], ("strips", 1): [(1, 8)], ("small", 1): [(1, 9)],
    ("kk", 1, 0): [(1, 10)], ("kk", 1, 1): [(1, 11)], ("kk", 1, 2): [None],
}


def schedule_slots():
    out = []

    def ada(*place):
        for what in ADA_AT.get(place, ()):
            if what is not None:
                out.append((("ada", *what), 4 * KT * P))

    for l in range(L):
        ada("start", l)
        ada("norm1", l)
        for c in range(NT):
            out += [(("ret", l, c), 4 * KT * P)]
            if c == 0:
                ada("strips", l)
        out += [(("small", l), 3 * KT * P)]
        ada("small", l)
        for c in range(NT):
            out += [(("rw", l, c), 3 * KT * P)]
            ada("kk", l, c)
            ada("keys", l, c)
        out += [(("hi", l), 4 * KT * P)]
        out += [(("hf", l, c), 4 * KT * P) for c in range(NT)]
        ada("out", l)
        out += [(("gb", l, f), SLOT) for f in range(KT)]
        out += [(("out", l, a), 4 * KT * P) for a in range(2)]
        ada("norm2", l)
        out += [(("m1", l, a), 4 * KT * P) for a in range(8)]
        out += [(("m2", l, f), 32 * P) for f in range(8)]
    return out


class Steps:

    def __init__(self, ctx, nc, name, log, known):
        self.sem, self.name, self.log, self.known, self.n = ctx.enter_context(nc.semaphore(name)), name, log, known, 0

    def step(self, key=None, by=1):
        self.n += by
        if key is not None:
            self.also(key)
        return by

    def also(self, key):
        assert key not in self.log, key
        self.log[key] = (self.name, self.n)

    def at(self, *key):
        if self.known is None:
            return 1
        name, n = self.known[key]
        assert name == self.name, (key, name, self.name)
        return n


class Banks:

    def __init__(self, psum, first, n, width, steps, known, loaded):
        self.psum, self.first, self.n, self.width, self.steps, self.known = psum, first, n, width, steps, known
        self.loaded, self.keys, self.where = loaded, [], {}

    def fill(self, *key):
        self.where[key] = len(self.keys) % self.n
        self.keys.append(key)
        return self.get(*key)

    def freed(self):
        i = len(self.keys) - 1 - self.n
        if i < 0 or self.known is None:
            return self.loaded.sem, 32
        name, n = self.known[("drained", *self.keys[i])]
        return self.steps[name].sem, n

    def get(self, *key):
        b = self.first + self.where[key] * self.width
        return self.psum[:, 512 * b:512 * (b + self.width)]


def build_program(nc, known, wts, wsm, vec, con, rcon, xin, xscr, out):
    log = {}
    with ExitStack() as ctx:
        def sb(name, shape, dt=F32):
            return ctx.enter_context(nc.sbuf_tensor(name, shape, dt))

        ring = sb("weight_ring", [P, RING, SLOT])
        hT = sb("normed", [P, KT, N])
        vfirst = sb("v_first", [P, NT, N])
        kc = sb("constants", [P, NCONST])
        par = sb("vectors", [P, NPAR])
        der = sb("derived", [P, NDER])
        work = sb("work", [P, WORK])
        psum = ctx.enter_context(nc.psum_tensor("psum", [P, 4096], F32))

        steps = {}

        def counter(name):
            steps[name] = Steps(ctx, nc, name, log, known)
            return steps[name]

        big_filled, wide_filled = counter("big_filled"), counter("wide_filled")
        mid_filled, out_filled = counter("mid_filled"), counter("out_filled")
        vec_cond, act_cond = counter("vec_cond"), counter("act_cond")
        vec_norm, act_norm = counter("vec_norm"), counter("act_norm")
        vec_ret, act_ret, pool_ret = counter("vec_ret"), counter("act_ret"), counter("pool_ret")
        vec_rwkv, act_rwkv, pool_rwkv = counter("vec_rwkv"), counter("act_rwkv"), counter("pool_rwkv")
        vec_hgrn, act_hgrn, pool_hgrn = counter("vec_hgrn"), counter("act_hgrn"), counter("pool_hgrn")
        vec_merge, act_merge = counter("vec_merge"), counter("act_merge")
        vec_mlp, act_mlp, pool_mlp = counter("vec_mlp"), counter("act_mlp"), counter("pool_mlp")
        weights = [counter(f"weights_{i}") for i in range(RING)]
        loaded_vectors, loaded_x = counter("loaded_vectors"), counter("loaded_x")
        loaded_ret_constants, loaded_small_weights = counter("loaded_ret_constants"), counter("loaded_small_weights")
        x_saved, x_back, stored = counter("x_saved"), counter("x_back"), counter("stored")
        block = ctx.enter_context(nc.Block())

        def banks(first, n, width=1):
            return Banks(psum, first, n, width, steps, known, loaded_vectors)

        big = banks(0, 2)
        wide = banks(2, 1, 2)
        mid = banks(4, 2)
        outb = banks(6, 2)

        slots = schedule_slots()
        slot_at = {key: i for i, (key, _) in enumerate(slots)}

        def wk(off, n=N):
            return work[:, off:off + n]

        def chunks(off, n=64, at=0, step=64, m0=0):
            return work[:, off:off + M * step].rearrange("p (m t) -> p m t", t=step)[:, m0:, at:at + n]

        def kcol(off, n):
            return kc[:, off:off + n]

        def over_chunks(ap, n, m0=0):
            return ap.rearrange("p (a t) -> p a t", a=1).broadcast_to([P, M - m0, n])

        def pcol(l, name, i=0, n=1):
            o = l * NPL + COL[name] + i
            return par[:, o:o + n]

        def dcol(o, n=1):
            return der[:, o:o + n]

        mod = der[:, D_MOD:D_MOD + 96].rearrange("p (t s) -> p t s", s=2)
        ident = kcol(K_ID, P)
        ones = kcol(K_ONE, P)
        bones = kcol(K_BONE, P)
        eps = {"rms": kcol(K_EPS, 1), "ln": kcol(K_EPS + 1, 1), "l2": kcol(K_EPS + 2, 1)}
        segs = [(0, 0, NC), (1, NC, N)]

        def live(l):
            return [(0, 0, NC), (1, NC, N)] if l < L - 1 else [(1, NC, N)]

        def rspan(l):
            s = live(l)
            return s[0][1], s[-1][2]

        def first_query(l):
            lo = rspan(l)[0]
            return lo, N - lo, lo // C

        ret_order = [("P", 0), ("R", 0), ("P", 1), ("A", 0), ("R", 1), ("O", 0), ("P", 2), ("A", 1), ("N", 0), ("R", 2),
                     ("O", 1), ("P", 3), ("A", 2), ("N", 1), ("R", 3), ("O", 2), ("A", 3), ("N", 2), ("O", 3), ("N", 3)]
        def wants_context(l, i):
            return l < L - 1 or (i >= NT and i != 14)

        scut = [(0, 0), (512, 0), (1024, NC), (1280, NC)]

        def chain_order(d):
            h = M // 2
            return list(range(M)) if d == 0 else list(range(h - 1, -1, -1)) + list(range(M - 1, h - 1, -1))

        @block.tensor
        def _(eng):
            mm = nc.tensor.matmul

            def slot(*key):
                i = slot_at[key]
                eng.wait_ge(weights[i % RING].sem, 16 * (i // RING + 1))
                return ring[:, i % RING, :]

            def tiled(s, j, k):
                return s[:, (j * KT + k) * P:(j * KT + k + 1) * P]

            def project(s, j, key, t0=0, t1=N):
                ps = big.fill(*key)
                eng.wait_ge(*big.freed())
                for k in range(KT):
                    last = mm(ps[:, 0:t1 - t0], tiled(s, j, k), hT[:, k, t0:t1], start=(k == 0), stop=(k == KT - 1))
                last.then_inc(big_filled.sem, big_filled.step(key))

            def sum_over(lhs, rhs, key, n=N):
                ps = big.fill(*key)
                eng.wait_ge(*big.freed())
                mm(ps[:, 0:n], lhs, rhs, start=True, stop=True).then_inc(big_filled.sem, big_filled.step(key))

            def per_head(ps, w, lhs, rhs, m0=0):
                for m in range(m0, M):
                    for h in range(2):
                        q = slice(64 * h, 64 * h + 64)
                        last = mm(ps[q, w * m:w * m + w], lhs(q, m), rhs(q, m), start=True, stop=True)
                return last

            def with_keys_and_queries(ps, lhs, B, m0):
                for m in range(M):
                    n = 64 if m < m0 else 128
                    for h in range(2):
                        q = slice(64 * h, 64 * h + 64)
                        last = mm(ps[q, 128 * m:128 * m + n], lhs(q, m), work[q, B + KR + 128 * m:B + KR + 128 * m + n],
                                  start=True, stop=True)
                return last

            def norm(l, which):
                t0, t1 = (0, N) if which == 1 or l < L - 1 else (NC, N)
                if which == 3:
                    t0 = NC
                ps = big.fill("sumsq", l, which)
                eng.wait_ge(*big.freed())
                for k in range(KT):
                    eng.wait_ge(act_norm.sem, act_norm.at("square", l, which, k))
                    last = mm(ps[:, 0:t1 - t0], ones, work[:, TN + 512 * (k % 2):TN + 512 * (k % 2) + t1 - t0],
                              start=(k == 0), stop=(k == KT - 1))
                    last.then_inc(big_filled.sem, big_filled.step(("squares read", l, which, k)))

            rows = []

            def modulation(*place):
                for what in ADA_AT.get(place, ()):
                    if what is not None:
                        s = slot("ada", *what)
                        ps = outb.fill("ada", *what)
                        eng.wait_ge(*outb.freed())
                        for k in range(KT):
                            last = mm(ps[64:66, :], der[:, D_CS + 2 * k:D_CS + 2 * k + 2], s[:, BW * k:BW * k + BW],
                                      start=(k == 0), stop=(k == KT - 1))
                        last.then_inc(out_filled.sem, out_filled.step(("ada", *what)))
                    if rows:
                        before = rows.pop()
                        eng.wait_ge(act_cond.sem, act_cond.at("drained", "ada", *before))
                        ps = outb.fill("ada columns", *before)
                        eng.wait_ge(*outb.freed())
                        for j in range(4):
                            last = mm(ps[:, 2 * j:2 * j + 2], work[64:66, ROWS2 + P * j:ROWS2 + P * j + P],
                                      kc[64:66, K_ID + 64:K_ID + 66], start=True, stop=True)
                        last.then_inc(out_filled.sem, out_filled.step(("ada columns", *before)))
                    if what is not None:
                        rows.append(what)

            eng.wait_ge(loaded_vectors.sem, loaded_vectors.at("vectors"))
            eng.wait_ge(act_cond.sem, act_cond.at("cond silu"))
            for l in range(L):
                lo, w, m0 = first_query(l)
                modulation("start", l)
                norm(l, 1)
                modulation("norm1", l)

                eng.wait_ge(act_norm.sem, act_norm.at("h", l, 1))
                for what, c in ret_order:
                    qk = RT_QK + 1024 * (c % 2)
                    v = RT_V + 512 * (c % 2)
                    A = RT_A + 1536 * (c % 2)
                    if what == "P":
                        s = slot("ret", l, c)
                        project(s, 0, ("rq", l, c), lo, N)
                        project(s, 1, ("rk", l, c))
                        if c == 0:
                            modulation("strips", l)
                        ps = big.fill("rv", l, c)
                        eng.wait_ge(*big.freed())
                        for i in range(4):
                            for k in range(KT):
                                last = mm(ps[:, P * i:P * i + P], hT[:, k, P * i:P * i + P], tiled(s, 2, k),
                                          start=(k == 0), stop=(k == KT - 1))
                        last.then_inc(big_filled.sem, big_filled.step(("rv", l, c)))
                        project(s, 3, ("rg", l, c), lo, N)
                    if what == "R":
                        for i, n in enumerate(("rq", "rk")):
                            eng.wait_ge(act_ret.sem, act_ret.at("drained", n, l, c))
                            t0 = lo if n == "rq" else 0
                            sum_over(kcol(K_ROT, P), wk(qk + 512 * i)[:, t0:N], (n + " turned", l, c), N - t0)
                    if what == "A":
                        eng.wait_ge(vec_ret.sem, vec_ret.at("roped", l, c))
                        for i in range(2):
                            if i == 0 or lo == 0:
                                ps = mid.fill("rA", l, c, i)
                                eng.wait_ge(*mid.freed())
                            o = 0 if lo == 0 else NC * i
                            last = mm(ps[:, o:o + w], work[:, qk + 512 + P * i:qk + 512 + P * i + P], work[:, qk + lo:qk + N],
                                      start=True, stop=True)
                            if i == 1 or lo == 0:
                                last.then_inc(mid_filled.sem, mid_filled.step(("rA", l, c, i if lo == 0 else 0)))
                        ps = mid.fill("rA", l, c, 2)
                        eng.wait_ge(*mid.freed())
                        for i in range(2, 4):
                            last = mm(ps[:, 256 * (i - 2):256 * (i - 2) + 256],
                                      work[:, qk + 512 + P * i:qk + 512 + P * i + P],
                                      work[:, qk + NC:qk + N], start=True, stop=True)
                        last.then_inc(mid_filled.sem, mid_filled.step(("rA", l, c, 2)))
                    if what == "O":
                        eng.wait_ge(vec_ret.sem, vec_ret.at("drained", "rA", l, c, 2))
                        eng.wait_ge(act_ret.sem, act_ret.at("drained", "rv", l, c))
                        ps = outb.fill("rO", l, c)
                        eng.wait_ge(*outb.freed())
                        for i, (col, t0) in enumerate(scut):
                            u = max(t0, lo)
                            last = mm(ps[:, u:N], work[:, v + P * i:v + P * i + P],
                                      work[:, A + col + u - t0:A + col + N - t0], start=(i == 0), stop=(i == 3))
                        last.then_inc(out_filled.sem, out_filled.step(("rO", l, c)))
                    if what == "N":
                        eng.wait_ge(pool_ret.sem, pool_ret.at("ret squared", l, c))
                        sum_over(ones, wk(RT_O + 512)[:, lo:N], ("rN", l, c), w)

                s = slot("small", l)
                for j in range(3):
                    project(s, j, ("small", l, j), lo if j == 2 else 0, N)
                eng.wait_ge(loaded_small_weights.sem, loaded_small_weights.at("small weights", l))
                if l > 0:
                    ps = big.fill("vd", l)
                    eng.wait_ge(*big.freed())
                    for k in range(KT):
                        last = mm(ps[0:32, :], work[:, RW_W + 1536 + 32 * k:RW_W + 1536 + 32 * k + 32], hT[:, k, :],
                                  start=(k == 0), stop=(k == KT - 1))
                    last.then_inc(big_filled.sem, big_filled.step(("vd", l)))
                modulation("small", l)
                eng.wait_ge(act_rwkv.sem, act_rwkv.at("small ready", l))
                for c in range(NT):
                    wcol = slice(P * c, P * c + P)
                    s = slot("rw", l, c)
                    for j in range(3):
                        project(s, j, ("rkv", l, c, j), lo if j == 0 else 0, N)
                    if l > 0:
                        eng.wait_ge(act_rwkv.sem, act_rwkv.at("drained", "vd", l))
                        ps = big.fill("vgate", l, c)
                        eng.wait_ge(*big.freed())
                        last = mm(ps, wsm_up(work, wcol), work[0:32, RW_VD:RW_VD + N], start=True, stop=True)
                        last.then_inc(big_filled.sem, big_filled.step(("vgate", l, c)))
                    modulation("kk", l, c)
                    eng.wait_ge(pool_rwkv.sem, pool_rwkv.at("kk squared", l, c))
                    sum_over(bones, wk(RW_SQ), ("kk norm", l, c))
                    for d in range(2):
                        q = slice(64 * d, 64 * d + 64)
                        for j, n in enumerate(("zw", "za")):
                            ps = big.fill(n, l, c, d)
                            eng.wait_ge(*big.freed())
                            last = mm(ps, work[q, RW_W + 512 * j + P * c:RW_W + 512 * j + P * c + P],
                                      work[q, RW_SMALL + 512 * j:RW_SMALL + 512 * j + N], start=True, stop=True)
                            last.then_inc(big_filled.sem, big_filled.step((n, l, c, d)))
                    eng.wait_ge(vec_rwkv.sem, vec_rwkv.at("v ready", l, c))
                    vsrc = (lambda q, m: vfirst[q, c, 64 * m:64 * m + 64]) if l == 0 else (
                        lambda q, m: work[q, RW_RKV + 1024 + 64 * m:RW_RKV + 1024 + 64 * m + 64])
                    idq = lambda q, m: kc[q, K_ID + q.start:K_ID + q.start + 64]
                    ps = mid.fill("vT", l, c)
                    eng.wait_ge(*mid.freed())
                    per_head(ps, 64, vsrc, idq).then_inc(mid_filled.sem, mid_filled.step(("vT", l, c)))

                    def cell(off, step=64, at=0, n=64):
                        return lambda q, m: work[q, off + step * m + at:off + step * m + at + n]

                    modulation("keys", l, c)
                    for d in range(2):
                        B = RW_D[d]
                        eng.wait_ge(vec_rwkv.sem, vec_rwkv.at("prepared", l, c, d))
                        ps = wide.fill("gb", l, c, d)
                        eng.wait_ge(*wide.freed())
                        with_keys_and_queries(ps, cell(B + BT), B, m0).then_inc(wide_filled.sem, wide_filled.step(("gb", l, c, d)))
                        ps = mid.fill("tkk", l, c, d)
                        eng.wait_ge(*mid.freed())
                        per_head(ps, 64, cell(B + KR, 128), idq).then_inc(mid_filled.sem, mid_filled.step(("tkk", l, c, d)))
                        ps = mid.fill("tb", l, c, d)
                        eng.wait_ge(*mid.freed())
                        per_head(ps, 64, cell(B + BT), idq).then_inc(mid_filled.sem, mid_filled.step(("tb", l, c, d)))
                        ps = wide.fill("gk", l, c, d)
                        eng.wait_ge(*wide.freed())
                        with_keys_and_queries(ps, cell(B + KTI), B, m0).then_inc(wide_filled.sem, wide_filled.step(("gk", l, c, d)))
                        ps = mid.fill("tk", l, c, d)
                        eng.wait_ge(*mid.freed())
                        per_head(ps, 64, cell(B + KTI), idq).then_inc(mid_filled.sem, mid_filled.step(("tk", l, c, d)))
                    for d in range(2):
                        B = RW_D[d]
                        eng.wait_ge(vec_rwkv.sem, vec_rwkv.at("level", l, c, d, 0))
                        ps = mid.fill("l1", l, c, d)
                        eng.wait_ge(*mid.freed())
                        per_head(ps, 64, cell(B + BT), idq).then_inc(mid_filled.sem, mid_filled.step(("l1", l, c, d)))
                        eng.wait_ge(act_rwkv.sem, act_rwkv.at("drained", "vT", l, c))
                        ps = mid.fill("mv", l, c, d)
                        eng.wait_ge(*mid.freed())
                        per_head(ps, 64, cell(B + MT), cell(RW_VT)).then_inc(mid_filled.sem, mid_filled.step(("mv", l, c, d)))
                    for j in range(1, 6):
                        for d in range(2):
                            B = RW_D[d]
                            eng.wait_ge(pool_rwkv.sem, pool_rwkv.at("level", l, c, d, j))
                            if j == 1:
                                eng.wait_ge(vec_rwkv.sem, vec_rwkv.at("drained", "l1", l, c, d))
                            else:
                                eng.wait_ge(vec_rwkv.sem, vec_rwkv.at("drained", "dT", l, c, d, j - 1))
                            ps = mid.fill("Z", l, c, d, j)
                            eng.wait_ge(*mid.freed())
                            per_head(ps, 64, cell(B + (KTI if j % 2 else BT)), cell(B + TT)).then_inc(mid_filled.sem, mid_filled.step(("Z", l, c, d, j)))
                        for d in range(2):
                            B = RW_D[d]
                            eng.wait_ge(act_rwkv.sem, act_rwkv.at("drained", "Z", l, c, d, j))
                            if j > 1:
                                eng.wait_ge(vec_rwkv.sem, vec_rwkv.at("drained", "dR", l, c, d, j - 1))
                            if j < 5:
                                ps = mid.fill("dT", l, c, d, j)
                                eng.wait_ge(*mid.freed())
                                per_head(ps, 64, cell(B + RR), cell(B + MT)).then_inc(mid_filled.sem, mid_filled.step(("dT", l, c, d, j)))
                            ps = mid.fill("dR", l, c, d, j)
                            eng.wait_ge(*mid.freed())
                            per_head(ps, 64, cell(B + MT), cell(B + RR)).then_inc(mid_filled.sem, mid_filled.step(("dR", l, c, d, j)))
                    for d in range(2):
                        B = RW_D[d]
                        eng.wait_ge(vec_rwkv.sem, vec_rwkv.at("drained", "dR", l, c, d, 5))
                        ps = wide.fill("uk", l, c, d)
                        eng.wait_ge(*wide.freed())
                        per_head(ps, 128, cell(B + RR), cell(B + YK, 128, 0, 128)).then_inc(wide_filled.sem, wide_filled.step(("uk", l, c, d)))
                    for d in range(2):
                        B = RW_D[d]
                        eng.wait_ge(act_rwkv.sem, act_rwkv.at("drained", "uk", l, c, d))
                        ps = mid.fill("rr", l, c, d)
                        eng.wait_ge(*mid.freed())
                        per_head(ps, 64, cell(B + LT, 128, 64), cell(B + ABT), m0).then_inc(mid_filled.sem, mid_filled.step(("rr", l, c, d)))
                        ps = mid.fill("pt", l, c, d)
                        eng.wait_ge(*mid.freed())
                        per_head(ps, 64, cell(B + LT, 128, 64), cell(B + BTT)).then_inc(mid_filled.sem, mid_filled.step(("pt", l, c, d)))
                    for d in range(2):
                        outb.fill("O", l, c, d)
                        eng.wait_ge(*outb.freed())
                    for i in range(M):
                        for d in range(2):
                            B = RW_D[d]
                            m = chain_order(d)[i]
                            if i < M - 1:
                                if i > 0:
                                    eng.wait_ge(vec_rwkv.sem, vec_rwkv.at("S", l, c, d, i))
                                if i == 1:
                                    eng.wait_ge(vec_rwkv.sem, vec_rwkv.at("drained", "pt", l, c, d))
                                ps = mid.fill("dS", l, c, d, i)
                                eng.wait_ge(*mid.freed())
                                for h in range(2):
                                    q = slice(64 * h, 64 * h + 64)
                                    ops = [(KTT, RW_VT, 64), (BTT, B + LT, 128)]
                                    for n, (a, r, rs) in enumerate(ops):
                                        last = mm(ps[q, 0:64], work[q, B + a + 64 * m:B + a + 64 * m + 64],
                                                  work[q, r + rs * m:r + rs * m + 64],
                                                  start=(n == 0), stop=(n == 1 and i == 0))
                                    if i > 0:
                                        last = mm(ps[q, 0:64], work[q, B + MT + 64 * m:B + MT + 64 * m + 64],
                                                  work[q, B + YK + 64 * i:B + YK + 64 * i + 64], start=False, stop=True)
                                last.then_inc(mid_filled.sem, mid_filled.step(("dS", l, c, d, i)))
                            if i == M - 1:
                                eng.wait_ge(vec_rwkv.sem, vec_rwkv.at("S", l, c, d, i))
                            if m < m0:
                                continue
                            ps = outb.get("O", l, c, d)
                            if i == m0:
                                eng.wait_ge(vec_rwkv.sem, vec_rwkv.at("drained", "rr", l, c, d))
                            for h in range(2):
                                q = slice(64 * h, 64 * h + 64)
                                o = ps[q, 64 * m:64 * m + 64]
                                mm(o, work[q, RW_VT + 64 * m:RW_VT + 64 * m + 64],
                                   work[q, B + AKT + 64 * m:B + AKT + 64 * m + 64], start=True, stop=False)
                                last = mm(o, work[q, B + LT + 128 * m:B + LT + 128 * m + 64],
                                          work[q, B + ABT + 64 * m:B + ABT + 64 * m + 64], start=False, stop=(i == 0))
                                if i > 0:
                                    last = mm(o, work[q, B + YK + 64 * i:B + YK + 64 * i + 64],
                                              work[q, B + KR + 128 * m + 64:B + KR + 128 * m + 128],
                                              start=False, stop=True)
                            if i == M - 1:
                                last.then_inc(out_filled.sem, out_filled.step(("O", l, c, d)))
                    eng.wait_ge(vec_rwkv.sem, vec_rwkv.at("o summed", l, c))
                    sum_over(bones, wk(RW_SCR)[:, lo:N], ("mean", l, c), w)
                    eng.wait_ge(vec_rwkv.sem, vec_rwkv.at("bonus terms", l, c))
                    sum_over(bones, wk(RW_KS)[:, lo:N], ("bonus", l, c), w)
                    eng.wait_ge(pool_rwkv.sem, pool_rwkv.at("centred squared", l, c))
                    sum_over(bones, wk(RW_SCR + 512)[:, lo:N], ("var", l, c), w)
                    sum_over(work[:, RW_W + 1024 + P * c:RW_W + 1024 + P * c + P], wk(RW_SMALL + 1024)[:, lo:N],
                             ("gate", l, c), w)

                s = slot("hi", l)
                for i in range(4):
                    ps = big.fill("hi", l, i)
                    eng.wait_ge(*big.freed())
                    for k in range(KT):
                        last = mm(ps, hT[:, k, P * i:P * i + P], s[:, BW * k:BW * k + BW], start=(k == 0), stop=(k == KT - 1))
                    last.then_inc(big_filled.sem, big_filled.step(("hi", l, i)))

                def hdiag(h):
                    eng.wait_ge(vec_hgrn.sem, vec_hgrn.at("hq ready", l, h))
                    ps = mid.fill("hd", l, h)
                    eng.wait_ge(*mid.freed())
                    for i in range(lo // P, 4):
                        t = slice(P * i, P * i + P)
                        for dd in range(2):
                            last = mm(ps[:, t], wk(HG_K + 2048 * dd + 512 * h)[:, t], wk(HG_T + 512 * (h % 2))[:, t],
                                      start=(dd == 0), stop=(dd == 1))
                    last.then_inc(mid_filled.sem, mid_filled.step(("hd", l, h)))

                for h in range(4):
                    s = slot("hf", l, h)
                    for j in range(4):
                        project(s, j, ("hf", l, h, j), lo if j >= 2 else 0, N)
                    if h > 0:
                        hdiag(h - 1)
                hdiag(3)
                for j in range(9):
                    for h in range(4):
                        if j > 0:
                            eng.wait_ge(vec_hgrn.sem, vec_hgrn.at("hq up", l, h, j - 1))
                            eng.wait_ge(pool_hgrn.sem, pool_hgrn.at("hk up", l, h, j - 1))
                        q_ = [wk(HG_Q_of(dd, h)) for dd in range(2)]
                        k_ = [wk(HG_K + 2048 * dd + 512 * h) for dd in range(2)]
                        ps = mid.fill("hl", l, h, j)
                        eng.wait_ge(*mid.freed())
                        if j < 7:
                            b = 1 << j
                            for i in range(lo // P, 4):
                                t = slice(P * i, P * i + P)
                                for dd in range(2):
                                    side = 1 - dd
                                    cols = lambda ap: ap[:, t].rearrange("p (n s b) -> p n s b", s=2, b=b)[:, :, side, :]
                                    last = mm(cols(ps), k_[dd][:, t], cols(q_[dd]), start=True, stop=True)
                        elif j == 7:
                            for i in range(lo // P, 4):
                                dd, o = i % 2, i ^ 1
                                last = mm(ps[:, P * i:P * i + P], k_[dd][:, P * i:P * i + P], q_[dd][:, P * o:P * o + P],
                                          start=True, stop=True)
                        else:
                            for i in range(2):
                                for dd in range(2):
                                    last = mm(ps[:, 256 * i:256 * i + 256], k_[dd][:, P * i:P * i + P], q_[dd][:, NC:N],
                                              start=(dd == 0), stop=(dd == 1))
                        last.then_inc(mid_filled.sem, mid_filled.step(("hl", l, h, j)))
                for h in range(4):
                    eng.wait_ge(act_hgrn.sem, act_hgrn.at("drained", "hl", l, h, 7))
                    eng.wait_ge(act_hgrn.sem, act_hgrn.at("drained", "hl", l, h, 8))
                    if h == 0:
                        eng.wait_ge(act_hgrn.sem, act_hgrn.at("drained", "hi", l, 3))
                    ps = outb.fill("hO", l, h)
                    eng.wait_ge(*outb.freed())
                    A = HG_A + 1536 * h
                    for i, (col, t0) in enumerate(scut):
                        u = max(t0, lo)
                        last = mm(ps[:, u:N], work[:, HG_V + 512 * i + P * h:HG_V + 512 * i + P * h + P],
                                  work[:, A + col + u - t0:A + col + N - t0], start=(i == 0), stop=(i == 3))
                    last.then_inc(out_filled.sem, out_filled.step(("hO", l, h)))
                for h in range(4):
                    if h == 2:
                        modulation("out", l)
                    eng.wait_ge(pool_hgrn.sem, pool_hgrn.at("hgrn squared", l, h))
                    sum_over(ones, wk(HG_T + 512 + 512 * (h % 2))[:, lo:N], ("hN", l, h), w)

                t0, t1 = rspan(l)
                eng.wait_ge(vec_hgrn.sem, vec_hgrn.at("y ready", l))
                for f in range(KT):
                    s = slot("gb", l, f)
                    for b in range(3):
                        project(s, b, ("ga", l, f, b), t0, t1)
                        ps = big.fill("br", l, f, b)
                        eng.wait_ge(*big.freed())
                        for k in range(NT):
                            w0 = 3 * KT * P + (b * NT + k) * P
                            last = mm(ps[:, 0:t1 - t0], s[:, w0:w0 + P], work[:, Y[b] + 512 * k + t0:Y[b] + 512 * k + t1],
                                      start=(k == 0), stop=(k == NT - 1))
                        last.then_inc(big_filled.sem, big_filled.step(("br", l, f, b)))
                for f in range(KT):
                    if f % 4 == 0:
                        s = slot("out", l, f // 4)
                    ps = big.fill("ot", l, f)
                    eng.wait_ge(*big.freed())
                    for k in range(KT):
                        if f == 0:
                            eng.wait_ge(vec_merge.sem, vec_merge.at("merged", l, k))
                        last = mm(ps[:, 0:t1 - t0], tiled(s, f % 4, k), work[:, MG + 512 * k + t0:MG + 512 * k + t1],
                                  start=(k == 0), stop=(k == KT - 1))
                    last.then_inc(big_filled.sem, big_filled.step(("ot", l, f)))
                norm(l, 2)
                modulation("norm2", l)
                eng.wait_ge(act_norm.sem, act_norm.at("h", l, 2))
                for f in range(32):
                    if f % 4 == 0:
                        s = slot("m1", l, f // 4)
                    project(s, f % 4, ("m1", l, f), t0, t1)
                for f in range(KT):
                    s = slot("m2", l, f)
                    ps = big.fill("m2", l, f)
                    eng.wait_ge(*big.freed())
                    for k in range(32):
                        if f == 0:
                            eng.wait_ge(pool_mlp.sem, pool_mlp.at("hidden", l, k))
                        last = mm(ps[:, 0:t1 - t0], s[:, P * k:P * k + P], work[:, hid(k) + t0:hid(k) + t1],
                                  start=(k == 0), stop=(k == 31))
                    last.then_inc(big_filled.sem, big_filled.step(("m2", l, f)))
            norm(L - 1, 3)

        @block.vector
        def _(eng):
            tt, ts, stt, cp = (nc.vector.tensor_tensor, nc.vector.tensor_scalar, nc.vector.scalar_tensor_tensor,
                               nc.vector.tensor_copy)

            def drain_diag(l, h):
                eng.wait_ge(pool_hgrn.sem, pool_hgrn.at("scores clear", l, h))
                eng.wait_ge(mid_filled.sem, mid_filled.at("hd", l, h))
                msk = kc[:, K_ID:K_ID + P].bitcast(U32).rearrange("p (a t) -> p a t", a=1).broadcast_to([P, 2, P])
                for half, diag in enumerate(scores_diag(work, h)):
                    if half < first_query(l)[0] // NC:
                        continue
                    ps = mid.get("hd", l, h)[:, 256 * half:256 * half + 256].rearrange("p (i t) -> p i t", t=P)
                    nc.vector.copy_predicated(diag, msk, ps).then_inc(
                        vec_hgrn.sem, vec_hgrn.step(("drained", "hd", l, h) if half else None))
                    eng.wait_ge(vec_hgrn.sem, vec_hgrn.n)

            def hgrn_tail(l, h):
                eng.wait_ge(act_hgrn.sem, act_hgrn.at("hgrn rms", l, h))
                lo = first_query(l)[0]
                o = wk(HG_T + 1536 if h % 2 else HG_T)[:, lo:N]
                y = wk(Y[YH] + 512 * h)[:, lo:N]
                stt(o, o, pcol(l, "hnw", h), wk(HG_T + 512 + 512 * (h % 2))[:, lo:N], ALU.mult, ALU.mult).then_inc(
                    vec_hgrn.sem, vec_hgrn.step())
                eng.wait_ge(vec_hgrn.sem, vec_hgrn.n)
                tt(y, y, o, ALU.mult).then_inc(vec_hgrn.sem, vec_hgrn.step(("hgrn y", l, h)))
                eng.wait_ge(vec_hgrn.sem, vec_hgrn.n)

            def add_gated(done, ps, tile, x, parts, t0, key):
                for i, (sg, u0, u1) in enumerate(parts):
                    stt(work[:, x + u0:x + u1], ps[:, u0 - t0:u1 - t0], mod[:, tile, sg:sg + 1],
                        work[:, x + u0:x + u1], ALU.mult, ALU.add).then_inc(
                            done.sem, done.step(key if i == len(parts) - 1 else None))
                    eng.wait_ge(done.sem, done.n)

            def tail(l, which):
                t0, t1 = (0, N) if which == 1 or l < L - 1 else (NC, N)
                if which == 3:
                    t0 = NC
                eng.wait_ge(act_norm.sem, act_norm.at("rms", l, which))
                for k in range(KT):
                    o = TN + 1536 + 512 * (k % 2)
                    if which == 3:
                        stt(wk(X + 512 * k)[:, t0:t1], wk(X + 512 * k)[:, t0:t1],
                                     par[:, L * NPL + k:L * NPL + k + 1], work[:, TN + 1024:TN + 1024 + t1 - t0],
                                     ALU.mult, ALU.mult).then_inc(vec_norm.sem, vec_norm.step(("final", k)))
                        eng.wait_ge(vec_norm.sem, vec_norm.n)
                        continue
                    if k >= 2:
                        eng.wait_ge(act_norm.sem, act_norm.at("h tile", l, which, k - 2))
                    tt(work[:, o:o + t1 - t0], wk(X + 512 * k)[:, t0:t1], work[:, TN + 1024:TN + 1024 + t1 - t0],
                                ALU.mult).then_inc(vec_norm.sem, vec_norm.step(("x scaled", l, which, k)))
                    eng.wait_ge(vec_norm.sem, vec_norm.n)

            eng.wait_ge(loaded_vectors.sem, loaded_vectors.at("vectors"))
            lbs = [pcol(l, "lb", 0, 8) for l in range(L)]
            t = [dcol(D_TMP + 8 * i, 8) for i in range(4)]
            tt(t[0], lbs[0], lbs[1], ALU.max).then_inc(vec_cond.sem, vec_cond.step())
            eng.wait_ge(vec_cond.sem, vec_cond.n)
            tt(t[1], lbs[0], t[0], ALU.subtract).then_inc(vec_cond.sem, vec_cond.step())
            eng.wait_ge(vec_cond.sem, vec_cond.n)
            tt(t[2], lbs[1], t[0], ALU.subtract).then_inc(vec_cond.sem, vec_cond.step(("lb centred",)))
            eng.wait_ge(vec_cond.sem, vec_cond.n)
            eng.wait_ge(act_cond.sem, act_cond.at("lb exp"))
            tt(t[3], t[1], t[2], ALU.add).then_inc(vec_cond.sem, vec_cond.step())
            eng.wait_ge(vec_cond.sem, vec_cond.n)
            nc.vector.reciprocal(t[0], t[3]).then_inc(vec_cond.sem, vec_cond.step())
            eng.wait_ge(vec_cond.sem, vec_cond.n)
            tt(t[1], t[1], t[0], ALU.mult).then_inc(vec_cond.sem, vec_cond.step())
            eng.wait_ge(vec_cond.sem, vec_cond.n)
            tt(t[2], t[2], t[0], ALU.mult).then_inc(vec_cond.sem, vec_cond.step())
            eng.wait_ge(vec_cond.sem, vec_cond.n)
            tt(t[3], t[1], t[2], ALU.add).then_inc(vec_cond.sem, vec_cond.step())
            eng.wait_ge(vec_cond.sem, vec_cond.n)
            tt(dcol(D_LOW, 8), t[1], t[1], ALU.subtract).then_inc(vec_cond.sem, vec_cond.step())
            eng.wait_ge(vec_cond.sem, vec_cond.n)
            tt(dcol(D_LOW + 8, 8), t[3], t[1], ALU.subtract).then_inc(vec_cond.sem, vec_cond.step())
            eng.wait_ge(vec_cond.sem, vec_cond.n)
            ts(dcol(D_OML, 16), dcol(D_LOW, 16), -1.0, 1.0, ALU.mult, ALU.add).then_inc(vec_cond.sem, vec_cond.step())
            eng.wait_ge(vec_cond.sem, vec_cond.n)

            rows = []

            def modulation(*place):
                for what in ADA_AT.get(place, ()):
                    if rows:
                        l_, a = rows.pop()
                        eng.wait_ge(out_filled.sem, out_filled.at("ada columns", l_, a))
                        ps = outb.get("ada columns", l_, a)[:, 0:8].rearrange("p (j s) -> p j s", s=2)
                        bias = pcol(l_, "adab", 4 * a, 4).rearrange("p (j s) -> p j s", s=1).broadcast_to([P, 4, 2])
                        tt(mod[:, 4 * a:4 * a + 4, :], ps, bias, ALU.add).then_inc(vec_cond.sem, vec_cond.step(("drained", "ada columns", l_, a)))
                        eng.wait_ge(vec_cond.sem, vec_cond.n)
                    if what is not None:
                        rows.append(what)

            def norm_scale(l, dst, sc, w):
                wb = pcol(l, w, 0, 8).rearrange("p (j s) -> p j s", s=1).broadcast_to([P, 8, 2])
                stt(dcol(dst, 16).rearrange("p (j s) -> p j s", s=2), mod[:, sc:sc + 8, :], 1.0, wb,
                    ALU.add, ALU.mult).then_inc(vec_cond.sem, vec_cond.step(("norm scale", l, w)))
                eng.wait_ge(vec_cond.sem, vec_cond.n)

            for l in range(L):
                lo, w, m0 = first_query(l)
                modulation("start", l)
                norm_scale(l, D_WS1, 8, "n1")
                ts(dcol(D_HMU, 15), pcol(l, "mu", 0, 15), 0.5, None, ALU.mult).then_inc(vec_cond.sem, vec_cond.step())
                eng.wait_ge(vec_cond.sem, vec_cond.n)
                ts(dcol(D_QMU, 15), pcol(l, "mu", 0, 15), 0.25, None, ALU.mult).then_inc(vec_cond.sem, vec_cond.step())
                eng.wait_ge(vec_cond.sem, vec_cond.n)
                ts(dcol(D_OMU, 15), pcol(l, "mu", 0, 15), -1.0, 1.0, ALU.mult, ALU.add).then_inc(vec_cond.sem, vec_cond.step())
                eng.wait_ge(vec_cond.sem, vec_cond.n)
                ts(dcol(D_OMKA, 4), pcol(l, "ka", 0, 4), -1.0, 1.0, ALU.mult, ALU.add).then_inc(vec_cond.sem, vec_cond.step())
                eng.wait_ge(vec_cond.sem, vec_cond.n)
                eng.wait_ge(act_cond.sem, act_cond.at("ret decay exp", l))
                ts(dcol(D_LG, 8), dcol(D_LG, 8), -1.0, None, ALU.mult).then_inc(vec_cond.sem, vec_cond.step(("vectors derived", l)))
                eng.wait_ge(vec_cond.sem, vec_cond.n)
                tail(l, 1)
                modulation("norm1", l)

                for h in range(4):
                    S = RT_STRIP + 768 * h
                    eng.wait_ge(act_ret.sem, act_ret.at("strip exps", l, h))
                    tt(wk(S, 384), wk(S, 384), wk(RT_LAG + 768, 384), ALU.mult).then_inc(vec_ret.sem, vec_ret.step())
                    eng.wait_ge(vec_ret.sem, vec_ret.n)
                    tt(wk(RT_A + 768 * h, 384), wk(RT_A + 768 * h, 384), wk(RT_LAG + 1152, 384), ALU.mult).then_inc(vec_ret.sem, vec_ret.step())
                    eng.wait_ge(vec_ret.sem, vec_ret.n)
                    tt(wk(S, 768), wk(S, 768), wk(RT_A + 768 * h, 768), ALU.add).then_inc(vec_ret.sem, vec_ret.step())
                    eng.wait_ge(vec_ret.sem, vec_ret.n)
                    ts(wk(S, 768), wk(S, 768), float(P) ** -0.5, None, ALU.mult).then_inc(vec_ret.sem, vec_ret.step(("strip", l, h)))
                    eng.wait_ge(vec_ret.sem, vec_ret.n)
                for what, c in ret_order:
                    qk = RT_QK + 1024 * (c % 2)
                    A = RT_A + 1536 * (c % 2)
                    if what == "P" and c == 0:
                        modulation("strips", l)
                    if what == "R":
                        for i, n in enumerate(("rq", "rk")):
                            eng.wait_ge(big_filled.sem, big_filled.at(n + " turned", l, c))
                            t0 = lo if n == "rq" else 0
                            rot, x_ = wk(RT_ROT)[:, t0:N], wk(qk + 512 * i)[:, t0:N]
                            tt(rot, big.get(n + " turned", l, c)[:, 0:N - t0], wk(RT_CS + 512)[:, t0:N], ALU.mult).then_inc(vec_ret.sem, vec_ret.step(("drained", n + " turned", l, c)))
                            eng.wait_ge(vec_ret.sem, vec_ret.n)
                            tt(x_, x_, wk(RT_CS)[:, t0:N], ALU.mult).then_inc(vec_ret.sem, vec_ret.step())
                            eng.wait_ge(vec_ret.sem, vec_ret.n)
                            tt(x_, x_, rot, ALU.add).then_inc(vec_ret.sem, vec_ret.step(("roped", l, c) if i else None))
                            eng.wait_ge(vec_ret.sem, vec_ret.n)
                    if what == "A":
                        S = RT_STRIP + 768 * c
                        for i in range(2):
                            if lo == 0:
                                eng.wait_ge(mid_filled.sem, mid_filled.at("rA", l, c, i))
                                ps = mid.get("rA", l, c, i)
                                tt(wk(A + 512 * i, 256), ps[:, 0:256], wk(S + 128 - 128 * i, 256), ALU.mult).then_inc(vec_ret.sem, vec_ret.step())
                                eng.wait_ge(vec_ret.sem, vec_ret.n)
                                ps = ps[:, 256:512]
                            else:
                                eng.wait_ge(mid_filled.sem, mid_filled.at("rA", l, c, 0))
                                ps = mid.get("rA", l, c, 0)[:, NC * i:NC * i + NC]
                            tt(wk(A + 512 * i + 256, 256), ps, wk(S + 384 + 128 - 128 * i, 256),
                                        ALU.mult).then_inc(vec_ret.sem, vec_ret.step())
                            if lo == 0:
                                vec_ret.also(("drained", "rA", l, c, i))
                            elif i == 1:
                                vec_ret.also(("drained", "rA", l, c, 0))
                            eng.wait_ge(vec_ret.sem, vec_ret.n)
                        eng.wait_ge(mid_filled.sem, mid_filled.at("rA", l, c, 2))
                        ps = mid.get("rA", l, c, 2)
                        for i in range(2):
                            tt(wk(A + 1024 + 256 * i, 256), ps[:, 256 * i:256 * i + 256],
                                        wk(S + 128 - 128 * i, 256), ALU.mult).then_inc(vec_ret.sem, vec_ret.step(("drained", "rA", l, c, 2) if i else None))
                            eng.wait_ge(vec_ret.sem, vec_ret.n)
                    if what == "O":
                        eng.wait_ge(out_filled.sem, out_filled.at("rO", l, c))
                        cp(wk(RT_O)[:, lo:N], outb.get("rO", l, c)[:, lo:N]).then_inc(vec_ret.sem, vec_ret.step(("drained", "rO", l, c)))
                        eng.wait_ge(vec_ret.sem, vec_ret.n)
                    if what == "N":
                        eng.wait_ge(act_ret.sem, act_ret.at("ret rms", l, c))
                        tt(wk(RT_O)[:, lo:N], wk(RT_O)[:, lo:N], wk(RT_O + 1024)[:, lo:N], ALU.mult).then_inc(vec_ret.sem, vec_ret.step())
                        eng.wait_ge(vec_ret.sem, vec_ret.n)
                        eng.wait_ge(act_ret.sem, act_ret.at("drained", "rg", l, c))
                        y = wk(Y[YR] + 512 * c)[:, lo:N]
                        tt(y, y, wk(RT_O)[:, lo:N], ALU.mult).then_inc(vec_ret.sem, vec_ret.step(("ret y", l, c)))
                        eng.wait_ge(vec_ret.sem, vec_ret.n)

                def mix(i, dst, key):
                    eng.wait_ge(pool_rwkv.sem, pool_rwkv.at("neighbours", l, i))
                    raw = RW_SCR
                    ctx = wants_context(l, i)
                    if ctx:
                        ts(dst[:, 0:NC], wk(raw + 1, NC), dcol(D_OMU + i), None, ALU.mult).then_inc(vec_rwkv.sem, vec_rwkv.step())
                        eng.wait_ge(vec_rwkv.sem, vec_rwkv.n)
                    grid = wk(raw + 258, 396).rearrange("p (r t) -> p r t", t=66)[:, 1:5, 1:65]
                    dg = dst[:, NC:N].rearrange("p (r t) -> p r t", t=GRID)
                    ts(dg, grid, dcol(D_OMU + i), None, ALU.mult).then_inc(vec_rwkv.sem, vec_rwkv.step())
                    eng.wait_ge(vec_rwkv.sem, vec_rwkv.n)
                    if ctx:
                        stt(dst[:, 0:NC], wk(raw + 654, NC), dcol(D_HMU + i), dst[:, 0:NC], ALU.mult, ALU.add).then_inc(vec_rwkv.sem, vec_rwkv.step())
                        eng.wait_ge(vec_rwkv.sem, vec_rwkv.n)
                    stt(dst[:, NC:N], wk(raw + 654 + NC, NC), dcol(D_QMU + i), dst[:, NC:N], ALU.mult, ALU.add).then_inc(vec_rwkv.sem, vec_rwkv.step(key))
                    eng.wait_ge(vec_rwkv.sem, vec_rwkv.n)

                eng.wait_ge(x_saved.sem, x_saved.at("x saved", l))
                for j in range(3):
                    mix(12 + j, wk(RW_SMALL + 512 * j), ("mixed", l, 12 + j))
                modulation("small", l)
                for c in range(NT):
                    r, k = wk(RW_RKV), wk(RW_RKV + 512)
                    vv = vfirst[:, c, :] if l == 0 else wk(RW_RKV + 1024)
                    for j, dst in enumerate((r, k, vv)):
                        mix(4 * j + c, dst, ("mixed", l, 4 * j + c))
                    ts(wk(RW_KK), k, pcol(l, "kk", c), None, ALU.mult).then_inc(vec_rwkv.sem, vec_rwkv.step(("kk raw", l, c)))
                    eng.wait_ge(vec_rwkv.sem, vec_rwkv.n)
                    if l > 0:
                        tt(wk(RW_SCR + 512), vfirst[:, c, :], vv, ALU.subtract).then_inc(vec_rwkv.sem, vec_rwkv.step())
                        eng.wait_ge(vec_rwkv.sem, vec_rwkv.n)
                        eng.wait_ge(act_rwkv.sem, act_rwkv.at("vgate sigmoid", l, c))
                        tt(wk(RW_SCR + 512), wk(RW_SCR + 512), wk(RW_SCR), ALU.mult).then_inc(vec_rwkv.sem, vec_rwkv.step())
                        eng.wait_ge(vec_rwkv.sem, vec_rwkv.n)
                        tt(vv, vv, wk(RW_SCR + 512), ALU.add).then_inc(vec_rwkv.sem, vec_rwkv.step(("v ready", l, c)))
                        eng.wait_ge(vec_rwkv.sem, vec_rwkv.n)
                    else:
                        vec_rwkv.also(("v ready", l, c))
                    eng.wait_ge(act_rwkv.sem, act_rwkv.at("kk rms", l, c))
                    tt(wk(RW_KK), wk(RW_KK), wk(RW_SQ), ALU.mult).then_inc(vec_rwkv.sem, vec_rwkv.step(("kk ready", l, c)))
                    eng.wait_ge(vec_rwkv.sem, vec_rwkv.n)
                    modulation("kk", l, c)
                    for d in range(2):
                        B = RW_D[d]
                        eng.wait_ge(act_rwkv.sem, act_rwkv.at("decay sigmoid", l, c, d))
                        G, s, msk = wk(RW_SCR + 512 * d), wk(B + WW), kcol(K_SCAN + 512 * d, N)
                        if d == 1:
                            G, s, msk = G[:, ::-1], s[:, ::-1], msk[:, ::-1]
                        nc.vector.tensor_tensor_scan(G, msk, s, 0.0, ALU.mult, ALU.add).then_inc(vec_rwkv.sem, vec_rwkv.step(("decay sums", l, c, d)))
                        eng.wait_ge(vec_rwkv.sem, vec_rwkv.n)
                    for d in range(2):
                        B = RW_D[d]
                        eng.wait_ge(act_rwkv.sem, act_rwkv.at("a sigmoid", l, c, d))
                        ts(wk(B + KTI), wk(B + BT), pcol(l, "ka", c), dcol(D_OMKA + c), ALU.mult, ALU.add).then_inc(vec_rwkv.sem, vec_rwkv.step(("a read", l, c, d)))
                        eng.wait_ge(vec_rwkv.sem, vec_rwkv.n)
                        tt(wk(B + KTI), wk(B + KTI), k, ALU.mult).then_inc(vec_rwkv.sem, vec_rwkv.step())
                        eng.wait_ge(vec_rwkv.sem, vec_rwkv.n)
                    ks = wk(RW_KS)[:, lo:N]
                    tt(ks, wk(RW_D[0] + KTI)[:, lo:N], wk(RW_D[1] + KTI)[:, lo:N], ALU.add).then_inc(vec_rwkv.sem, vec_rwkv.step())
                    eng.wait_ge(vec_rwkv.sem, vec_rwkv.n)
                    ts(ks, ks, pcol(l, "rk", c), None, ALU.mult).then_inc(vec_rwkv.sem, vec_rwkv.step())
                    eng.wait_ge(vec_rwkv.sem, vec_rwkv.n)
                    tt(ks, ks, r[:, lo:N], ALU.mult).then_inc(vec_rwkv.sem, vec_rwkv.step(("bonus terms", l, c)))
                    eng.wait_ge(vec_rwkv.sem, vec_rwkv.n)
                    for d in range(2):
                        B = RW_D[d]
                        eng.wait_ge(act_rwkv.sem, act_rwkv.at("decays", l, c, d))
                        kk3, W3 = chunks(RW_KK), chunks(B + WW)
                        KR3 = chunks(B + KR, 64, 0, 128)
                        e = 0 if d == 0 else 63
                        a, b = (slice(1, 64), slice(0, 63)) if d == 0 else (slice(0, 63), slice(1, 64))
                        tt(KR3[:, :, a], kk3[:, :, a], W3[:, :, b], ALU.mult).then_inc(vec_rwkv.sem, vec_rwkv.step())
                        eng.wait_ge(vec_rwkv.sem, vec_rwkv.n)
                        cp(KR3[:, :, e:e + 1], kk3[:, :, e:e + 1]).then_inc(vec_rwkv.sem, vec_rwkv.step())
                        eng.wait_ge(vec_rwkv.sem, vec_rwkv.n)
                        tt(chunks(B + KR, 64, 64, 128, m0), chunks(RW_RKV, m0=m0), W3[:, m0:, :], ALU.mult).then_inc(vec_rwkv.sem, vec_rwkv.step())
                        eng.wait_ge(vec_rwkv.sem, vec_rwkv.n)
                        eng.wait_ge(pool_rwkv.sem, pool_rwkv.at("b ready", l, c, d))
                        tt(wk(B + KTI), wk(B + KTI), wk(RW_SCR + 1024 + 512 * d), ALU.mult).then_inc(vec_rwkv.sem, vec_rwkv.step(("prepared", l, c, d)))
                        eng.wait_ge(vec_rwkv.sem, vec_rwkv.n)
                    modulation("keys", l, c)
                    for d in range(2):
                        B = RW_D[d]
                        eng.wait_ge(wide_filled.sem, wide_filled.at("gb", l, c, d))
                        ps = wide.get("gb", l, c, d).rearrange("p (m t) -> p m t", t=128)
                        tt(chunks(B + LT), ps[:, :, 0:64], over_chunks(kcol(K_STRICT + 64 * d, 64), 64), ALU.mult).then_inc(vec_rwkv.sem, vec_rwkv.step())
                        eng.wait_ge(vec_rwkv.sem, vec_rwkv.n)
                        tt(chunks(B + ABT, m0=m0), ps[:, m0:, 64:128], over_chunks(kcol(K_INCL + 64 * d, 64), 64, m0), ALU.mult).then_inc(vec_rwkv.sem, vec_rwkv.step(("drained", "gb", l, c, d)))
                        eng.wait_ge(vec_rwkv.sem, vec_rwkv.n)
                        eng.wait_ge(wide_filled.sem, wide_filled.at("gk", l, c, d))
                        ps = wide.get("gk", l, c, d).rearrange("p (m t) -> p m t", t=128)
                        tt(chunks(B + MT), ps[:, :, 0:64], over_chunks(kcol(K_STRICT + 64 * d, 64), 64), ALU.mult).then_inc(vec_rwkv.sem, vec_rwkv.step())
                        eng.wait_ge(vec_rwkv.sem, vec_rwkv.n)
                        tt(chunks(B + AKT, m0=m0), ps[:, m0:, 64:128], over_chunks(kcol(K_INCL + 64 * d, 64), 64, m0), ALU.mult).then_inc(vec_rwkv.sem, vec_rwkv.step(("drained", "gk", l, c, d)))
                        eng.wait_ge(vec_rwkv.sem, vec_rwkv.n)
                        eng.wait_ge(mid_filled.sem, mid_filled.at("tb", l, c, d))
                        tt(chunks(B + BT), chunks(B + LT), over_chunks(kcol(K_LEV, 64), 64), ALU.mult).then_inc(vec_rwkv.sem, vec_rwkv.step(("level", l, c, d, 0)))
                        eng.wait_ge(vec_rwkv.sem, vec_rwkv.n)
                        tt(chunks(B + RR), ident64(kc), chunks(B + BT), ALU.subtract).then_inc(vec_rwkv.sem, vec_rwkv.step(("R first", l, c, d)))
                        eng.wait_ge(vec_rwkv.sem, vec_rwkv.n)
                    for d in range(2):
                        B = RW_D[d]
                        eng.wait_ge(mid_filled.sem, mid_filled.at("l1", l, c, d))
                        tt(chunks(B + TT), ident64(kc), mid.get("l1", l, c, d).rearrange("p (m t) -> p m t", t=64),
                                    ALU.subtract).then_inc(vec_rwkv.sem, vec_rwkv.step(("drained", "l1", l, c, d)))
                        eng.wait_ge(vec_rwkv.sem, vec_rwkv.n)
                    for j in range(1, 6):
                        for d in range(2):
                            B = RW_D[d]
                            for n, o in (("dT", TT), ("dR", RR)):
                                if n == "dT" and j == 5:
                                    continue
                                eng.wait_ge(mid_filled.sem, mid_filled.at(n, l, c, d, j))
                                tt(wk(B + o), wk(B + o), mid.get(n, l, c, d, j), ALU.subtract).then_inc(vec_rwkv.sem, vec_rwkv.step(("drained", n, l, c, d, j)))
                                eng.wait_ge(vec_rwkv.sem, vec_rwkv.n)
                    for d in range(2):
                        B = RW_D[d]
                        eng.wait_ge(mid_filled.sem, mid_filled.at("rr", l, c, d))
                        tt(chunks(B + KR, 64, 64, 128, m0), chunks(B + KR, 64, 64, 128, m0),
                                    mid.get("rr", l, c, d).rearrange("p (m t) -> p m t", t=64)[:, m0:, :], ALU.add).then_inc(vec_rwkv.sem, vec_rwkv.step(("drained", "rr", l, c, d)))
                        eng.wait_ge(vec_rwkv.sem, vec_rwkv.n)
                        eng.wait_ge(mid_filled.sem, mid_filled.at("pt", l, c, d))
                        tt(chunks(B + MT), ident64(kc), mid.get("pt", l, c, d).rearrange("p (m t) -> p m t", t=64),
                                    ALU.add).then_inc(vec_rwkv.sem, vec_rwkv.step(("drained", "pt", l, c, d)))
                        eng.wait_ge(vec_rwkv.sem, vec_rwkv.n)
                    for i in range(M - 1):
                        for d in range(2):
                            B = RW_D[d]
                            m = chain_order(d)[i]
                            e = 64 * m + (63 if d == 0 else 0)
                            eng.wait_ge(mid_filled.sem, mid_filled.at("dS", l, c, d, i))
                            ts(wk(B + YK + 64 * (i + 1), 64), mid.get("dS", l, c, d, i)[:, 0:64],
                                        work[:, B + WW + e:B + WW + e + 1], None, ALU.mult).then_inc(vec_rwkv.sem, vec_rwkv.step(("S", l, c, d, i + 1)))
                            eng.wait_ge(vec_rwkv.sem, vec_rwkv.n)
                            vec_rwkv.also(("drained", "dS", l, c, d, i))
                    eng.wait_ge(out_filled.sem, out_filled.at("O", l, c, 0))
                    cp(wk(RW_SCR)[:, lo:N], outb.get("O", l, c, 0)[:, lo:N]).then_inc(vec_rwkv.sem, vec_rwkv.step(("drained", "O", l, c, 0)))
                    eng.wait_ge(vec_rwkv.sem, vec_rwkv.n)
                    eng.wait_ge(out_filled.sem, out_filled.at("O", l, c, 1))
                    tt(wk(RW_SCR)[:, lo:N], wk(RW_SCR)[:, lo:N], outb.get("O", l, c, 1)[:, lo:N], ALU.add).then_inc(vec_rwkv.sem, vec_rwkv.step(("drained", "O", l, c, 1)))
                    eng.wait_ge(vec_rwkv.sem, vec_rwkv.n)
                    vec_rwkv.also(("o summed", l, c))
                    eng.wait_ge(big_filled.sem, big_filled.at("mean", l, c))
                    stt(wk(RW_SCR)[:, lo:N], big.get("mean", l, c)[:, 0:w], -1.0 / 64, wk(RW_SCR)[:, lo:N], ALU.mult, ALU.add).then_inc(vec_rwkv.sem, vec_rwkv.step(("drained", "mean", l, c)))
                    eng.wait_ge(vec_rwkv.sem, vec_rwkv.n)
                    eng.wait_ge(big_filled.sem, big_filled.at("bonus", l, c))
                    tt(wk(RW_SCR + 1536)[:, lo:N], big.get("bonus", l, c)[:, 0:w], vv[:, lo:N], ALU.mult).then_inc(vec_rwkv.sem, vec_rwkv.step(("drained", "bonus", l, c)))
                    eng.wait_ge(vec_rwkv.sem, vec_rwkv.n)
                    eng.wait_ge(act_rwkv.sem, act_rwkv.at("rwkv rms", l, c))
                    tt(wk(RW_SCR)[:, lo:N], wk(RW_SCR)[:, lo:N], wk(RW_SCR + 1024)[:, lo:N], ALU.mult).then_inc(vec_rwkv.sem, vec_rwkv.step())
                    eng.wait_ge(vec_rwkv.sem, vec_rwkv.n)
                    ts(wk(RW_SCR)[:, lo:N], wk(RW_SCR)[:, lo:N], pcol(l, "lnw", c), pcol(l, "lnb", c), ALU.mult, ALU.add).then_inc(vec_rwkv.sem, vec_rwkv.step())
                    eng.wait_ge(vec_rwkv.sem, vec_rwkv.n)
                    tt(wk(RW_SCR)[:, lo:N], wk(RW_SCR)[:, lo:N], wk(RW_SCR + 1536)[:, lo:N], ALU.add).then_inc(vec_rwkv.sem, vec_rwkv.step())
                    eng.wait_ge(vec_rwkv.sem, vec_rwkv.n)
                    eng.wait_ge(big_filled.sem, big_filled.at("gate", l, c))
                    tt(wk(Y[0] + 512 * c)[:, lo:N], wk(RW_SCR)[:, lo:N], big.get("gate", l, c)[:, 0:w], ALU.mult).then_inc(vec_rwkv.sem, vec_rwkv.step(("drained", "gate", l, c)))
                    eng.wait_ge(vec_rwkv.sem, vec_rwkv.n)

                for h in range(4):
                    for dd in range(2):
                        F, K = wk(HG_F + 2048 * dd + 512 * h), wk(HG_K + 2048 * dd + 512 * h)
                        om, low = dcol(D_OML + 8 * l + 4 * dd + h), dcol(D_LOW + 8 * l + 4 * dd + h)
                        eng.wait_ge(act_hgrn.sem, act_hgrn.at("forget sigmoid", l, h, dd))
                        ts(F, F, om, low, ALU.mult, ALU.add).then_inc(vec_hgrn.sem, vec_hgrn.step())
                        eng.wait_ge(vec_hgrn.sem, vec_hgrn.n)
                        ts(K, K, om, None, ALU.mult).then_inc(vec_hgrn.sem, vec_hgrn.step())
                        eng.wait_ge(vec_hgrn.sem, vec_hgrn.n)
                    eng.wait_ge(act_hgrn.sem, act_hgrn.at("hq silu", l, h))
                    for dd in range(2):
                        tt(wk(HG_Q_of(dd, h))[:, lo:N], wk(HG_T + 512 * (h % 2))[:, lo:N], wk(HG_F + 2048 * dd + 512 * h)[:, lo:N],
                           ALU.mult).then_inc(vec_hgrn.sem, vec_hgrn.step(("hq ready", l, h) if dd else None))
                        eng.wait_ge(vec_hgrn.sem, vec_hgrn.n)
                    if h > 0:
                        drain_diag(l, h - 1)
                drain_diag(l, 3)
                for j in range(9):
                    for h in range(4):
                        if j < 7:
                            eng.wait_ge(mid_filled.sem, mid_filled.at("hl", l, h, j))
                            diag = scores_diag(work, h)
                            for half in range(lo // NC, 2):
                                msk = kc[:, K_HLEV + 128 * j:K_HLEV + 128 * j + 128].bitcast(U32) \
                                    .rearrange("p (a t) -> p a t", a=1).broadcast_to([P, 2, P])
                                nc.vector.copy_predicated(
                                    diag[half], msk,
                                    mid.get("hl", l, h, j)[:, 256 * half:256 * half + 256].rearrange("p (i t) -> p i t", t=P)).then_inc(vec_hgrn.sem, vec_hgrn.step(("drained", "hl", l, h, j) if half else None))
                                eng.wait_ge(vec_hgrn.sem, vec_hgrn.n)
                        if j < 8:
                            if j == 7:
                                eng.wait_ge(mid_filled.sem, mid_filled.at("hl", l, h, j))
                            if j > 0:
                                eng.wait_ge(pool_hgrn.sem, pool_hgrn.at("F up", l, h, j - 1))
                            b = 1 << j
                            for dd in range(2):
                                pair = lambda ap: ap[:, lo:N].rearrange("p (n s b) -> p n s b", s=2, b=b)
                                side = 1 - dd
                                q = pair(wk(HG_Q_of(dd, h)))[:, :, side, :]
                                fe = pair(wk(HG_F + 2048 * dd + 512 * h))[:, :, 1 - side, 0:1].broadcast_to([P, w // (2 * b), b])
                                tt(q, q, fe, ALU.mult).then_inc(vec_hgrn.sem, vec_hgrn.step(("hq up", l, h, j) if dd else None))
                                eng.wait_ge(vec_hgrn.sem, vec_hgrn.n)
                for h in range(4):
                    eng.wait_ge(out_filled.sem, out_filled.at("hO", l, h))
                    o = HG_T + 1536 if h % 2 else HG_T
                    cp(wk(o)[:, lo:N], outb.get("hO", l, h)[:, lo:N]).then_inc(vec_hgrn.sem, vec_hgrn.step(("drained", "hO", l, h)))
                    eng.wait_ge(vec_hgrn.sem, vec_hgrn.n)
                    if h > 0:
                        hgrn_tail(l, h - 1)
                hgrn_tail(l, 3)
                vec_hgrn.also(("y ready", l))
                modulation("out", l)
                norm_scale(l, D_WS2, 32, "n2")

                t0, t1 = rspan(l)
                n = t1 - t0
                for f in range(KT):
                    mg = wk(MG + 512 * f)[:, t0:t1]
                    for b in range(3):
                        eng.wait_ge(big_filled.sem, big_filled.at("br", l, f, b))
                        eng.wait_ge(act_merge.sem, act_merge.at("drained", "ga", l, f, b))
                        sg = work[:, MG_T + 512 * ((3 * f + b) % 3):MG_T + 512 * ((3 * f + b) % 3) + n]
                        o = mg if b == 0 else work[:, MG_T + 1536:MG_T + 1536 + n]
                        tt(o, big.get("br", l, f, b)[:, 0:n], sg, ALU.mult).then_inc(vec_merge.sem, vec_merge.step(("drained", "br", l, f, b)))
                        eng.wait_ge(vec_merge.sem, vec_merge.n)
                        if b:
                            tt(mg, mg, o, ALU.add).then_inc(vec_merge.sem, vec_merge.step(("merged", l, f) if b == 2 else None))
                            eng.wait_ge(vec_merge.sem, vec_merge.n)
                eng.wait_ge(x_back.sem, x_back.at("x back", l))
                for f in range(KT):
                    eng.wait_ge(big_filled.sem, big_filled.at("ot", l, f))
                    add_gated(vec_merge, big.get("ot", l, f), 16 + f, X + 512 * f, live(l), t0, ("drained", "ot", l, f))
                tail(l, 2)
                modulation("norm2", l)
                for f in range(KT):
                    eng.wait_ge(big_filled.sem, big_filled.at("m2", l, f))
                    add_gated(vec_mlp, big.get("m2", l, f), 40 + f, X + 512 * f, live(l), t0, ("drained", "m2", l, f))
            tail(L - 1, 3)

        @block.scalar
        def _(eng):
            act = nc.scalar.activation

            eng.dma_start(par[:, :], vec).then_inc(loaded_vectors.sem, loaded_vectors.step(None, 16))
            eng.dma_start(kc[:, :], con).then_inc(loaded_vectors.sem, loaded_vectors.step(("vectors",), 16))
            eng.dma_start(work[:, X:X + KT * N], xin).then_inc(loaded_x.sem, loaded_x.step(("x loaded",), 16))

            def rsqrt(done, dst, ps, scale, e, key, drained):
                act(dst, ps, ACT.Ln, bias=eps[e], scale=scale).then_inc(done.sem, done.step(drained))
                eng.wait_ge(done.sem, done.n)
                act(dst, dst, ACT.Exp, scale=-0.5).then_inc(done.sem, done.step(key))
                eng.wait_ge(done.sem, done.n)

            def norm(l, which):
                t0, t1 = (0, N) if which == 1 or l < L - 1 else (NC, N)
                if which == 3:
                    t0 = NC
                n = t1 - t0
                if which == 1 and l == 0:
                    eng.wait_ge(loaded_x.sem, loaded_x.at("x loaded"))
                elif which == 2:
                    eng.wait_ge(vec_merge.sem, vec_merge.at("drained", "ot", l, 7))
                else:
                    eng.wait_ge(vec_mlp.sem, vec_mlp.at("drained", "m2", l if which == 3 else l - 1, 7))
                for k in range(KT):
                    if k >= 2:
                        eng.wait_ge(big_filled.sem, big_filled.at("squares read", l, which, k - 2))
                    act(work[:, TN + 512 * (k % 2):TN + 512 * (k % 2) + n], wk(X + 512 * k)[:, t0:t1], ACT.Square).then_inc(act_norm.sem, act_norm.step(("square", l, which, k)))
                    eng.wait_ge(act_norm.sem, act_norm.n)
                eng.wait_ge(big_filled.sem, big_filled.at("squares read", l, which, 7))
                rsqrt(act_norm, work[:, TN + 1024:TN + 1024 + n], big.get("sumsq", l, which)[:, 0:n], 1.0 / D, "rms",
                      ("rms", l, which), ("drained", "sumsq", l, which))
                if which == 3:
                    return
                eng.wait_ge(vec_cond.sem, vec_cond.at("vectors derived", l) if which == 1 else vec_cond.at("norm scale", l, "n2"))
                ws, sh = (D_WS1, 0) if which == 1 else (D_WS2, 24)
                for k in range(KT):
                    eng.wait_ge(vec_norm.sem, vec_norm.at("x scaled", l, which, k))
                    o = TN + 1536 + 512 * (k % 2)
                    parts = [s for s in segs if s[1] >= t0]
                    for i, (sg, u0, u1) in enumerate(parts):
                        last = i == len(parts) - 1
                        act(hT[:, k, u0:u1], work[:, o + u0 - t0:o + u1 - t0], ACT.Identity,
                                     bias=mod[:, sh + k, sg:sg + 1], scale=dcol(ws + 2 * k + sg)).then_inc(act_norm.sem, act_norm.step(("h tile", l, which, k) if last else None))
                        eng.wait_ge(act_norm.sem, act_norm.n)
                act_norm.also(("h", l, which))

            rows = []

            def modulation(*place):
                for what in ADA_AT.get(place, ()):
                    if what is not None:
                        eng.wait_ge(out_filled.sem, out_filled.at("ada", *what))
                        if rows:
                            eng.wait_ge(out_filled.sem, out_filled.at("ada columns", *rows[-1]))
                        rows.append(what)
                        act(work[64:66, ROWS2:ROWS2 + BW], outb.get("ada", *what)[64:66, :], ACT.Copy).then_inc(
                            act_cond.sem, act_cond.step(("drained", "ada", *what)))
                        eng.wait_ge(act_cond.sem, act_cond.n)

            eng.wait_ge(loaded_vectors.sem, loaded_vectors.at("vectors"))
            act(dcol(D_CS, 16), par[:, L * NPL + 8:L * NPL + 24], ACT.Silu).then_inc(act_cond.sem, act_cond.step(("cond silu",)))
            eng.wait_ge(act_cond.sem, act_cond.n)
            eng.wait_ge(vec_cond.sem, vec_cond.at("lb centred"))
            act(dcol(D_TMP + 8, 16), dcol(D_TMP + 8, 16), ACT.Exp).then_inc(act_cond.sem, act_cond.step(("lb exp",)))
            eng.wait_ge(act_cond.sem, act_cond.n)
            for l in range(L):
                lo, w, m0 = first_query(l)
                if l > 0:
                    eng.wait_ge(big_filled.sem, big_filled.at("m2", l - 1, 7))
                act(dcol(D_LG, 8), pcol(l, "dec", 0, 8), ACT.Exp).then_inc(act_cond.sem, act_cond.step(("ret decay exp", l)))
                eng.wait_ge(act_cond.sem, act_cond.n)
                modulation("start", l)
                norm(l, 1)

                modulation("norm1", l)
                eng.dma_start(xscr, work[:, X:X + KT * N]).then_inc(x_saved.sem, x_saved.step(("x saved", l), 16))
                eng.wait_ge(vec_norm.sem, vec_norm.at("x scaled", l, 1, 7))
                eng.dma_start(wk(RT_CS, 1024), rcon[:, 0:1024]).then_inc(loaded_ret_constants.sem, loaded_ret_constants.step(None, 16))
                eng.dma_start(wk(RT_LAG, 2304), rcon[:, 1024:NRC]).then_inc(loaded_ret_constants.sem, loaded_ret_constants.step(("ret constants", l), 16))

                eng.wait_ge(loaded_ret_constants.sem, loaded_ret_constants.at("ret constants", l))
                lg = lambda dd, h: dcol(D_LG + 4 * dd + h)
                for h in range(4):
                    S, E = RT_STRIP + 768 * h, RT_A + 768 * h
                    act(wk(S, 384), wk(RT_LAG, 384), ACT.Exp, scale=lg(0, h)).then_inc(act_ret.sem, act_ret.step())
                    eng.wait_ge(act_ret.sem, act_ret.n)
                    act(wk(E, 384), wk(RT_LAG + 384, 384), ACT.Exp, scale=lg(1, h)).then_inc(act_ret.sem, act_ret.step())
                    eng.wait_ge(act_ret.sem, act_ret.n)
                    act(wk(S + 384, 384), wk(RT_LAG + 1536, 384), ACT.Exp, scale=lg(0, h)).then_inc(act_ret.sem, act_ret.step())
                    eng.wait_ge(act_ret.sem, act_ret.n)
                    act(wk(E + 384, 384), wk(RT_LAG + 1920, 384), ACT.Exp, scale=lg(1, h)).then_inc(act_ret.sem, act_ret.step(("strip exps", l, h)))
                    eng.wait_ge(act_ret.sem, act_ret.n)
                for what, c in ret_order:
                    qk = RT_QK + 1024 * (c % 2)
                    if what == "P":
                        for i, n in enumerate(("rq", "rk")):
                            eng.wait_ge(big_filled.sem, big_filled.at(n, l, c))
                            t0 = lo if n == "rq" else 0
                            act(wk(qk + 512 * i)[:, t0:N], big.get(n, l, c)[:, 0:N - t0], ACT.Copy).then_inc(act_ret.sem, act_ret.step(("drained", n, l, c)))
                            eng.wait_ge(act_ret.sem, act_ret.n)
                        if c == 0:
                            modulation("strips", l)
                        eng.wait_ge(big_filled.sem, big_filled.at("rv", l, c))
                        act(wk(RT_V + 512 * (c % 2)), big.get("rv", l, c), ACT.Copy).then_inc(act_ret.sem, act_ret.step(("drained", "rv", l, c)))
                        eng.wait_ge(act_ret.sem, act_ret.n)
                        eng.wait_ge(big_filled.sem, big_filled.at("rg", l, c))
                        act(wk(Y[YR] + 512 * c)[:, lo:N], big.get("rg", l, c)[:, 0:w], ACT.Silu).then_inc(act_ret.sem, act_ret.step(("drained", "rg", l, c)))
                        eng.wait_ge(act_ret.sem, act_ret.n)
                    if what == "N":
                        eng.wait_ge(big_filled.sem, big_filled.at("rN", l, c))
                        rsqrt(act_ret, wk(RT_O + 1024)[:, lo:N], big.get("rN", l, c)[:, 0:w], 1.0 / P, "rms", ("ret rms", l, c), ("drained", "rN", l, c))

                eng.wait_ge(vec_ret.sem, vec_ret.at("ret y", l, 3))
                eng.dma_start(wk(RW_W, 2304), wsm[l]).then_inc(loaded_small_weights.sem, loaded_small_weights.step(("small weights", l), 16))

                def raw(i, ps, key):
                    if i != 12:
                        eng.wait_ge(vec_rwkv.sem, vec_rwkv.at("mixed", l, last_mixed[0]))
                    if wants_context(l, i):
                        act(wk(RW_SCR + 1, NC), ps[:, 0:NC], ACT.Copy).then_inc(act_rwkv.sem, act_rwkv.step())
                        eng.wait_ge(act_rwkv.sem, act_rwkv.n)
                        ps = ps[:, NC:N]
                    grid = wk(RW_SCR + 258, 396).rearrange("p (r t) -> p r t", t=66)[:, 1:5, 1:65]
                    act(grid, ps[:, 0:NC].rearrange("p (r t) -> p r t", t=GRID), ACT.Copy).then_inc(act_rwkv.sem, act_rwkv.step(key))
                    eng.wait_ge(act_rwkv.sem, act_rwkv.n)
                    act_rwkv.also(("raw", l, i))
                    last_mixed[0] = i

                last_mixed = [None]
                eng.wait_ge(pool_rwkv.sem, pool_rwkv.at("pads rwkv", l, -1))
                for j in range(3):
                    eng.wait_ge(big_filled.sem, big_filled.at("small", l, j))
                    raw(12 + j, big.get("small", l, j), ("drained", "small", l, j))
                if l > 0:
                    eng.wait_ge(big_filled.sem, big_filled.at("vd", l))
                    act(work[0:32, RW_VD:RW_VD + N], big.get("vd", l)[0:32, :], ACT.Copy).then_inc(act_rwkv.sem, act_rwkv.step(("drained", "vd", l)))
                    eng.wait_ge(act_rwkv.sem, act_rwkv.n)
                eng.wait_ge(vec_rwkv.sem, vec_rwkv.at("mixed", l, 12))
                act(wk(RW_SMALL), wk(RW_SMALL), ACT.Tanh).then_inc(act_rwkv.sem, act_rwkv.step())
                eng.wait_ge(act_rwkv.sem, act_rwkv.n)
                eng.wait_ge(vec_rwkv.sem, vec_rwkv.at("mixed", l, 14))
                act(wk(RW_SMALL + 1024)[:, lo:N], wk(RW_SMALL + 1024)[:, lo:N], ACT.Sigmoid).then_inc(act_rwkv.sem, act_rwkv.step(("small ready", l)))
                eng.wait_ge(act_rwkv.sem, act_rwkv.n)
                modulation("small", l)
                for c in range(NT):
                    if c > 0:
                        eng.wait_ge(pool_rwkv.sem, pool_rwkv.at("pads rwkv", l, c - 1))
                    for j in range(3):
                        eng.wait_ge(big_filled.sem, big_filled.at("rkv", l, c, j))
                        raw(4 * j + c, big.get("rkv", l, c, j), ("drained", "rkv", l, c, j))
                    eng.wait_ge(vec_rwkv.sem, vec_rwkv.at("mixed", l, 8 + c))
                    if l > 0:
                        eng.wait_ge(big_filled.sem, big_filled.at("vgate", l, c))
                        act(wk(RW_SCR), big.get("vgate", l, c), ACT.Sigmoid, bias=pcol(l, "v0", c)).then_inc(act_rwkv.sem, act_rwkv.step(("drained", "vgate", l, c)))
                        eng.wait_ge(act_rwkv.sem, act_rwkv.n)
                        act_rwkv.also(("vgate sigmoid", l, c))
                    eng.wait_ge(big_filled.sem, big_filled.at("kk norm", l, c))
                    rsqrt(act_rwkv, wk(RW_SQ), big.get("kk norm", l, c), 1.0, "l2", ("kk rms", l, c), ("drained", "kk norm", l, c))
                    for d in range(2):
                        B = RW_D[d]
                        eng.wait_ge(big_filled.sem, big_filled.at("zw", l, c, d))
                        act(wk(B + WW), big.get("zw", l, c, d), ACT.Sigmoid, bias=pcol(l, "w0", 4 * d + c)).then_inc(act_rwkv.sem, act_rwkv.step(("drained", "zw", l, c, d)))
                        eng.wait_ge(act_rwkv.sem, act_rwkv.n)
                        act_rwkv.also(("decay sigmoid", l, c, d))
                        eng.wait_ge(big_filled.sem, big_filled.at("za", l, c, d))
                        act(wk(B + BT), big.get("za", l, c, d), ACT.Sigmoid, bias=pcol(l, "a0", 4 * d + c)).then_inc(act_rwkv.sem, act_rwkv.step(("drained", "za", l, c, d)))
                        eng.wait_ge(act_rwkv.sem, act_rwkv.n)
                        act_rwkv.also(("a sigmoid", l, c, d))
                    for d in range(2):
                        B = RW_D[d]
                        eng.wait_ge(vec_rwkv.sem, vec_rwkv.at("decay sums", l, c, d))
                        act(wk(B + WW), wk(RW_SCR + 512 * d), ACT.Exp, scale=-DECAY).then_inc(act_rwkv.sem, act_rwkv.step())
                        eng.wait_ge(act_rwkv.sem, act_rwkv.n)
                        act(wk(RW_SCR + 1024 + 512 * d), wk(RW_SCR + 512 * d), ACT.Exp, scale=DECAY).then_inc(act_rwkv.sem, act_rwkv.step(("decays", l, c, d)))
                        eng.wait_ge(act_rwkv.sem, act_rwkv.n)
                    modulation("kk", l, c)
                    eng.wait_ge(mid_filled.sem, mid_filled.at("vT", l, c))
                    act(wk(RW_VT), mid.get("vT", l, c), ACT.Copy).then_inc(act_rwkv.sem, act_rwkv.step(("drained", "vT", l, c)))
                    eng.wait_ge(act_rwkv.sem, act_rwkv.n)
                    for d in range(2):
                        B = RW_D[d]
                        for n, dst in (("tkk", chunks(B + YK, 64, 64, 128)), ("tb", chunks(B + BTT)), ("tk", chunks(B + KTT))):
                            eng.wait_ge(mid_filled.sem, mid_filled.at(n, l, c, d))
                            act(dst, mid.get(n, l, c, d).rearrange("p (m t) -> p m t", t=64), ACT.Copy).then_inc(act_rwkv.sem, act_rwkv.step(("drained", n, l, c, d)))
                            eng.wait_ge(act_rwkv.sem, act_rwkv.n)
                    modulation("keys", l, c)
                    for d in range(2):
                        B = RW_D[d]
                        eng.wait_ge(mid_filled.sem, mid_filled.at("mv", l, c, d))
                        act(chunks(B + YK, 64, 0, 128), mid.get("mv", l, c, d).rearrange("p (m t) -> p m t", t=64),
                                     ACT.Copy).then_inc(act_rwkv.sem, act_rwkv.step(("drained", "mv", l, c, d)))
                        eng.wait_ge(act_rwkv.sem, act_rwkv.n)
                    for j in range(1, 6):
                        for d in range(2):
                            B = RW_D[d]
                            eng.wait_ge(mid_filled.sem, mid_filled.at("Z", l, c, d, j))
                            act(wk(B + MT), mid.get("Z", l, c, d, j), ACT.Copy).then_inc(act_rwkv.sem, act_rwkv.step(("drained", "Z", l, c, d, j)))
                            eng.wait_ge(act_rwkv.sem, act_rwkv.n)
                    for d in range(2):
                        B = RW_D[d]
                        eng.wait_ge(wide_filled.sem, wide_filled.at("uk", l, c, d))
                        act(wk(B + LT, 1024), wide.get("uk", l, c, d), ACT.Copy, scale=-1.0).then_inc(act_rwkv.sem, act_rwkv.step(("drained", "uk", l, c, d)))
                        eng.wait_ge(act_rwkv.sem, act_rwkv.n)
                    eng.wait_ge(big_filled.sem, big_filled.at("var", l, c))
                    rsqrt(act_rwkv, wk(RW_SCR + 1024)[:, lo:N], big.get("var", l, c)[:, 0:w], 1.0 / 64, "ln", ("rwkv rms", l, c),
                          ("drained", "var", l, c))

                eng.wait_ge(vec_rwkv.sem, vec_rwkv.at("drained", "gate", l, 3))
                for i in range(4):
                    eng.wait_ge(big_filled.sem, big_filled.at("hi", l, i))
                    act(wk(HG_V + 512 * i), big.get("hi", l, i), ACT.Copy).then_inc(act_hgrn.sem, act_hgrn.step(("drained", "hi", l, i)))
                    eng.wait_ge(act_hgrn.sem, act_hgrn.n)
                for h in range(4):
                    for dd in range(2):
                        eng.wait_ge(big_filled.sem, big_filled.at("hf", l, h, dd))
                        ps = big.get("hf", l, h, dd)
                        act(wk(HG_F + 2048 * dd + 512 * h), ps, ACT.Sigmoid).then_inc(act_hgrn.sem, act_hgrn.step())
                        eng.wait_ge(act_hgrn.sem, act_hgrn.n)
                        act(wk(HG_K + 2048 * dd + 512 * h), ps, ACT.Sigmoid, scale=-1.0).then_inc(act_hgrn.sem, act_hgrn.step(("drained", "hf", l, h, dd)))
                        eng.wait_ge(act_hgrn.sem, act_hgrn.n)
                        act_hgrn.also(("forget sigmoid", l, h, dd))
                    eng.wait_ge(big_filled.sem, big_filled.at("hf", l, h, 2))
                    if h >= 2:
                        eng.wait_ge(mid_filled.sem, mid_filled.at("hd", l, h - 2))
                    act(wk(HG_T + 512 * (h % 2))[:, lo:N], big.get("hf", l, h, 2)[:, 0:w], ACT.Silu).then_inc(act_hgrn.sem, act_hgrn.step(("drained", "hf", l, h, 2)))
                    eng.wait_ge(act_hgrn.sem, act_hgrn.n)
                    act_hgrn.also(("hq silu", l, h))
                    eng.wait_ge(big_filled.sem, big_filled.at("hf", l, h, 3))
                    act(wk(Y[YH] + 512 * h)[:, lo:N], big.get("hf", l, h, 3)[:, 0:w], ACT.Silu).then_inc(act_hgrn.sem, act_hgrn.step(("drained", "hf", l, h, 3)))
                    eng.wait_ge(act_hgrn.sem, act_hgrn.n)
                for h in range(4):
                    A = HG_A + 1536 * h
                    eng.wait_ge(mid_filled.sem, mid_filled.at("hl", l, h, 7))
                    ps = mid.get("hl", l, h, 7)
                    for i, o in enumerate((128, 512, 1152, 1280)):
                        if i < lo // P:
                            continue
                        act(wk(A + o, P), ps[:, P * i:P * i + P], ACT.Copy).then_inc(act_hgrn.sem, act_hgrn.step(("drained", "hl", l, h, 7) if i == 3 else None))
                        eng.wait_ge(act_hgrn.sem, act_hgrn.n)
                for h in range(4):
                    A = HG_A + 1536 * h
                    eng.wait_ge(mid_filled.sem, mid_filled.at("hl", l, h, 8))
                    ps = mid.get("hl", l, h, 8)
                    for i in range(2):
                        act(wk(A + 512 * i + 256, 256), ps[:, 256 * i:256 * i + 256], ACT.Copy).then_inc(act_hgrn.sem, act_hgrn.step(("drained", "hl", l, h, 8) if i else None))
                        eng.wait_ge(act_hgrn.sem, act_hgrn.n)
                for h in range(4):
                    eng.wait_ge(big_filled.sem, big_filled.at("hN", l, h))
                    rsqrt(act_hgrn, wk(HG_T + 512 + 512 * (h % 2))[:, lo:N], big.get("hN", l, h)[:, 0:w], 1.0 / P, "rms", ("hgrn rms", l, h),
                          ("drained", "hN", l, h))

                modulation("out", l)
                t0, t1 = rspan(l)
                n = t1 - t0
                eng.wait_ge(vec_hgrn.sem, vec_hgrn.at("y ready", l))
                eng.wait_ge(x_saved.sem, x_saved.at("x saved", l))
                eng.dma_start(work[:, X:X + KT * N], xscr).then_inc(x_back.sem, x_back.step(("x back", l), 16))
                for f in range(KT):
                    for b in range(3):
                        i = 3 * f + b
                        eng.wait_ge(big_filled.sem, big_filled.at("ga", l, f, b))
                        if i >= 3:
                            eng.wait_ge(vec_merge.sem, vec_merge.at("drained", "br", l, (i - 3) // 3, (i - 3) % 3))
                        act(work[:, MG_T + 512 * (i % 3):MG_T + 512 * (i % 3) + n],
                                     big.get("ga", l, f, b)[:, 0:n], ACT.Sigmoid).then_inc(act_merge.sem, act_merge.step(("drained", "ga", l, f, b)))
                        eng.wait_ge(act_merge.sem, act_merge.n)
                norm(l, 2)
                modulation("norm2", l)
                for f in range(32):
                    eng.wait_ge(big_filled.sem, big_filled.at("m1", l, f))
                    act(work[:, hid(f) + t0:hid(f) + t1], big.get("m1", l, f)[:, 0:n], ACT.Relu).then_inc(act_mlp.sem, act_mlp.step(("drained", "m1", l, f)))
                    eng.wait_ge(act_mlp.sem, act_mlp.n)
            norm(L - 1, 3)

        @block.gpsimd
        def _(eng):
            tt = nc.gpsimd.tensor_tensor
            for l in range(L):
                lo, w, m0 = first_query(l)
                for what, c in ret_order:
                    if what == "O":
                        eng.wait_ge(vec_ret.sem, vec_ret.at("drained", "rO", l, c))
                        if c > 0:
                            eng.wait_ge(big_filled.sem, big_filled.at("rN", l, c - 1))
                        tt(wk(RT_O + 512)[:, lo:N], wk(RT_O)[:, lo:N], wk(RT_O)[:, lo:N], ALU.mult).then_inc(pool_ret.sem, pool_ret.step(("ret squared", l, c)))
                        eng.wait_ge(pool_ret.sem, pool_ret.n)
                def pads(c):
                    nc.gpsimd.memset(wk(RW_SCR, 654), 0.0).then_inc(pool_rwkv.sem, pool_rwkv.step(("pads rwkv", l, c)))
                    eng.wait_ge(pool_rwkv.sem, pool_rwkv.n)

                def neighbours(i):
                    eng.wait_ge(act_rwkv.sem, act_rwkv.at("raw", l, i))
                    S = RW_SCR + 654
                    if wants_context(l, i):
                        tt(wk(S, NC), wk(RW_SCR, NC), wk(RW_SCR + 2, NC), ALU.add).then_inc(pool_rwkv.sem, pool_rwkv.step())
                        eng.wait_ge(pool_rwkv.sem, pool_rwkv.n)
                    grid = wk(RW_SCR + 258, 396).rearrange("p (r t) -> p r t", t=66)
                    s3 = wk(S + NC, NC).rearrange("p (r t) -> p r t", t=GRID)
                    tt(s3, grid[:, 0:4, 1:65], grid[:, 2:6, 1:65], ALU.add).then_inc(pool_rwkv.sem, pool_rwkv.step())
                    eng.wait_ge(pool_rwkv.sem, pool_rwkv.n)
                    tt(s3, s3, grid[:, 1:5, 0:64], ALU.add).then_inc(pool_rwkv.sem, pool_rwkv.step())
                    eng.wait_ge(pool_rwkv.sem, pool_rwkv.n)
                    tt(s3, s3, grid[:, 1:5, 2:66], ALU.add).then_inc(pool_rwkv.sem, pool_rwkv.step(("neighbours", l, i)))
                    eng.wait_ge(pool_rwkv.sem, pool_rwkv.n)

                eng.wait_ge(vec_ret.sem, vec_ret.at("ret y", l, 3))
                pads(-1)
                for j in range(3):
                    neighbours(12 + j)
                for c in range(NT):
                    for j in range(3):
                        neighbours(4 * j + c)
                    eng.wait_ge(vec_rwkv.sem, vec_rwkv.at("kk raw", l, c))
                    tt(wk(RW_SQ), wk(RW_KK), wk(RW_KK), ALU.mult).then_inc(pool_rwkv.sem, pool_rwkv.step(("kk squared", l, c)))
                    eng.wait_ge(pool_rwkv.sem, pool_rwkv.n)
                    eng.wait_ge(vec_rwkv.sem, vec_rwkv.at("kk ready", l, c))
                    for d in range(2):
                        B = RW_D[d]
                        eng.wait_ge(vec_rwkv.sem, vec_rwkv.at("a read", l, c, d))
                        tt(wk(B + BT), wk(B + BT), wk(RW_KK), ALU.mult).then_inc(pool_rwkv.sem, pool_rwkv.step())
                        eng.wait_ge(pool_rwkv.sem, pool_rwkv.n)
                    for d in range(2):
                        B = RW_D[d]
                        eng.wait_ge(act_rwkv.sem, act_rwkv.at("decays", l, c, d))
                        tt(wk(B + BT), wk(B + BT), wk(RW_SCR + 1024 + 512 * d), ALU.mult).then_inc(pool_rwkv.sem, pool_rwkv.step(("b ready", l, c, d)))
                        eng.wait_ge(pool_rwkv.sem, pool_rwkv.n)
                    for j in range(1, 6):
                        for d in range(2):
                            B = RW_D[d]
                            if j == 1:
                                eng.wait_ge(mid_filled.sem, mid_filled.at("tk", l, c, d))
                                eng.wait_ge(vec_rwkv.sem, vec_rwkv.at("level", l, c, d, 0))
                            elif j == 2:
                                eng.wait_ge(mid_filled.sem, mid_filled.at("l1", l, c, d))
                                eng.wait_ge(vec_rwkv.sem, vec_rwkv.at("R first", l, c, d))
                            else:
                                eng.wait_ge(mid_filled.sem, mid_filled.at("Z", l, c, d, j - 2))
                            tt(chunks(B + (KTI if j % 2 else BT)), chunks(B + LT),
                                        over_chunks(kcol(K_LEV + 64 * j, 64), 64), ALU.mult).then_inc(pool_rwkv.sem, pool_rwkv.step(("level", l, c, d, j)))
                            eng.wait_ge(pool_rwkv.sem, pool_rwkv.n)
                    eng.wait_ge(vec_rwkv.sem, vec_rwkv.at("drained", "mean", l, c))
                    tt(wk(RW_SCR + 512)[:, lo:N], wk(RW_SCR)[:, lo:N], wk(RW_SCR)[:, lo:N], ALU.mult).then_inc(pool_rwkv.sem, pool_rwkv.step(("centred squared", l, c)))
                    eng.wait_ge(pool_rwkv.sem, pool_rwkv.n)
                    if c < NT - 1:
                        eng.wait_ge(vec_rwkv.sem, vec_rwkv.at("drained", "gate", l, c))
                        pads(c)
                eng.wait_ge(vec_rwkv.sem, vec_rwkv.at("drained", "gate", l, 3))
                for h in range(4):
                    nc.gpsimd.memset(wk(HG_A + 1536 * h, 1536), 0.0).then_inc(pool_hgrn.sem, pool_hgrn.step(("scores clear", l, h)))
                    eng.wait_ge(pool_hgrn.sem, pool_hgrn.n)
                for j in range(8):
                    for h in range(4):
                        eng.wait_ge(mid_filled.sem, mid_filled.at("hl", l, h, j))
                        b = 1 << j
                        for dd in range(2):
                            pair = lambda ap: ap.rearrange("p (n s b) -> p n s b", s=2, b=b)
                            side = dd
                            k = pair(wk(HG_K + 2048 * dd + 512 * h))[:, :, side, :]
                            fe = pair(wk(HG_F + 2048 * dd + 512 * h))[:, :, 1 - side, 0:1].broadcast_to([P, N // (2 * b), b])
                            tt(k, k, fe, ALU.mult).then_inc(pool_hgrn.sem, pool_hgrn.step(("hk up", l, h, j) if dd else None))
                            eng.wait_ge(pool_hgrn.sem, pool_hgrn.n)
                        eng.wait_ge(vec_hgrn.sem, vec_hgrn.at("hq up", l, h, j))
                        if j < 7:
                            for dd in range(2):
                                f = pair(wk(HG_F + 2048 * dd + 512 * h))
                                tt(f[:, :, 0, 0:1], f[:, :, 0, 0:1], f[:, :, 1, 0:1], ALU.mult).then_inc(pool_hgrn.sem, pool_hgrn.step(("F up", l, h, j) if dd else None))
                                eng.wait_ge(pool_hgrn.sem, pool_hgrn.n)
                for h in range(4):
                    eng.wait_ge(vec_hgrn.sem, vec_hgrn.at("drained", "hO", l, h))
                    if h >= 2:
                        eng.wait_ge(vec_hgrn.sem, vec_hgrn.at("hgrn y", l, h - 2))
                    o = HG_T + 1536 if h % 2 else HG_T
                    tt(wk(HG_T + 512 + 512 * (h % 2))[:, lo:N], wk(o)[:, lo:N], wk(o)[:, lo:N], ALU.mult).then_inc(pool_hgrn.sem, pool_hgrn.step(("hgrn squared", l, h)))
                    eng.wait_ge(pool_hgrn.sem, pool_hgrn.n)
                t0, t1 = rspan(l)
                for f in range(32):
                    eng.wait_ge(act_mlp.sem, act_mlp.at("drained", "m1", l, f))
                    h_ = work[:, hid(f) + t0:hid(f) + t1]
                    tt(h_, h_, h_, ALU.mult).then_inc(pool_mlp.sem, pool_mlp.step(("hidden", l, f)))
                    eng.wait_ge(pool_mlp.sem, pool_mlp.n)

        @block.sync
        def _(eng):
            for i, (key, n) in enumerate(slots):
                if i >= RING and slots[i - RING][0][0] == "ada":
                    eng.wait_ge(out_filled.sem, out_filled.at(*slots[i - RING][0]))
                elif i >= RING:
                    eng.wait_ge(big_filled.sem, big_filled.at(*last_use(slots[i - RING][0])))
                eng.dma_start(ring[:, i % RING, 0:n], wts[i][:, 0:n]).then_inc(weights[i % RING].sem, weights[i % RING].step(None, 16))
            for k in range(KT):
                eng.wait_ge(vec_norm.sem, vec_norm.at("final", k))
                eng.dma_start(out[P * k:P * k + P, :], work[:, X + 512 * k + NC:X + 512 * k + N]).then_inc(stored.sem, stored.step(None, 16))
            eng.wait_ge(stored.sem, stored.n)
            eng.wait_ge(x_saved.sem, 16 * L)
    return log


def last_use(key):
    kind, l, *i = key
    return {"ret": lambda: ("rg", l, *i), "small": lambda: ("small", l, 2),
            "rw": lambda: ("rkv", l, *i, 2), "hi": lambda: ("hi", l, 3), "hf": lambda: ("hf", l, *i, 3),
            "gb": lambda: ("br", l, *i, 2), "out": lambda: ("ot", l, 4 * i[0] + 3),
            "m1": lambda: ("m1", l, 4 * i[0] + 3), "m2": lambda: ("m2", l, *i)}[kind]()


def hid(f):
    return 512 * f if f < 12 else 14336 + 512 * (f - 12)


def wsm_up(work, wcol):
    return work[0:32, RW_W + 1792 + wcol.start:RW_W + 1792 + wcol.stop]


def HG_Q_of(dd, h):
    return HG_Q + 2048 * dd + 512 * h


def ident64(kc):
    return kc[:, K_ID2:K_ID2 + C].rearrange("p (a t) -> p a t", a=1).broadcast_to([P, M, C])


def scores_diag(work, h):
    A = HG_A + 1536 * h
    ctx = work[:, A:A + 1280].rearrange("p (i t) -> p i t", t=640)[:, :, 0:P]
    lat = work[:, A + 1024:A + 1024 + 768].rearrange("p (i t) -> p i t", t=384)[:, :, 0:P]
    return ctx, lat


def constants():
    k = np.zeros((P, NCONST), np.float32)
    p = np.arange(P)
    k[:, K_ID:K_ID + P] = np.eye(P)
    k[:, K_ONE:K_ONE + P] = 1
    k[:, K_BONE:K_BONE + P] = p[:, None] // 64 == p[None] // 64
    k[:, K_ROT:K_ROT + P] = 1.0 * (p[:, None] == p[None] - 64) - 1.0 * (p[:, None] == p[None] + 64)
    s, t = (p % 64)[:, None], np.arange(64)[None]
    k[:, K_STRICT:K_STRICT + 64], k[:, K_STRICT + 64:K_STRICT + 128] = s < t, s > t
    k[:, K_INCL:K_INCL + 64], k[:, K_INCL + 64:K_INCL + 128] = s <= t, s >= t
    for j in range(6):
        k[:, K_LEV + 64 * j:K_LEV + 64 * j + 64] = (s ^ t) >> j == 1
    for j in range(7):
        k[:, K_HLEV + P * j:K_HLEV + P * j + P] = (p[:, None] ^ p[None]) >> j == 1
    t = np.arange(N)
    k[:, K_SCAN:K_SCAN + N], k[:, K_SCAN + N:K_SCAN + 2 * N] = t % C != 0, t % C != C - 1
    k[:, K_EPS], k[:, K_EPS + 1], k[:, K_EPS + 2] = 1e-6, 64e-5, 1e-12
    k[:, K_ID2:K_ID2 + 64] = (p % 64)[:, None] == np.arange(64)[None]

    r = np.zeros((P, NRC), np.float32)
    half = P // 2
    inv = np.float32(10000.0) ** (-np.arange(half, dtype=np.float32) / np.float32(half))
    ang = np.arange(N, dtype=np.float32)[None] * inv[:, None]
    r[:, R_COS:R_COS + N] = np.tile(np.cos(ang), (2, 1))
    r[:, R_SIN:R_SIN + N] = np.tile(np.sin(ang), (2, 1))
    lag = np.arange(384)[None] - P - p[:, None]
    cross = lag + 2 * P
    for i, a in enumerate((np.maximum(lag, 0), np.maximum(-lag, 0), lag >= 0, lag <= 0, cross, N - cross)):
        r[:, R_LAG + 384 * i:R_LAG + 384 * i + 384] = a
    return k, r


def lay_out(inp):
    slots = schedule_slots()
    w = np.zeros((len(slots), P, SLOT), np.float32)

    def tiles(m):
        return m.reshape(m.shape[0] // P, P, m.shape[1] // P, P).transpose(1, 2, 0, 3)

    rw = np.cumsum([0, BW, BW, BW, 128, 128, 128])
    ret0 = int(rw[-1])
    hg0 = ret0 + 4 * BW
    ga0 = hg0 + 5 * BW
    for i, ((kind, l, *a), n) in enumerate(slots):
        wi = inp["w_in"][l]
        cut = lambda o: wi[:, o:o + P]
        if kind == "ada":
            m = inp["ada_w"][l][:, BW * a[0]:BW * a[0] + BW].reshape(KT, P, BW).transpose(1, 0, 2)
        elif kind == "ret":
            m = tiles(np.concatenate([cut(ret0 + BW * j + P * a[0]) for j in range(4)], 1))
        elif kind == "small":
            m = tiles(wi[:, 3 * BW:3 * BW + 3 * P])
        elif kind == "rw":
            m = tiles(np.concatenate([cut(BW * j + P * a[0]) for j in range(3)], 1))
        elif kind == "hi":
            m = wi[:, hg0 + 3 * BW:hg0 + 4 * BW].reshape(KT, P, BW).transpose(1, 0, 2)
        elif kind == "hf":
            m = tiles(np.concatenate([cut(hg0 + BW * j + P * a[0]) for j in (1, 2, 0, 4)], 1))
        elif kind == "gb":
            gates = tiles(np.concatenate([cut(ga0 + D * b + P * a[0]) for b in range(3)], 1)).reshape(P, -1)
            outs = [tiles(inp["w_branch"][l, b][:, P * a[0]:P * a[0] + P]).reshape(P, -1) for b in range(3)]
            m = np.concatenate([gates] + outs, 1)
        elif kind == "out":
            m = tiles(inp["w_out"][l][:, 4 * P * a[0]:4 * P * a[0] + 4 * P])
        elif kind == "m1":
            m = tiles(inp["mlp_w1"][l][:, 4 * P * a[0]:4 * P * a[0] + 4 * P])
        else:
            m = tiles(inp["mlp_w2"][l][:, P * a[0]:P * a[0] + P])
        w[i, :, :n] = m.reshape(P, n)

    small = np.zeros((L, P, 2304), np.float32)
    for l in range(L):
        small[l, :, 0:512] = inp["rwkv_w_up"][l].reshape(P, BW)
        small[l, :, 512:1024] = inp["rwkv_a_up"][l].reshape(P, BW)
        small[l, :, 1024:1536] = inp["rwkv_g_up"][l]
        if l:
            small[l, :, 1536:1792] = inp["rwkv_v_down"][l - 1].reshape(KT, P, 32).transpose(1, 0, 2).reshape(P, 256)
            small[l, 0:32, 1792:2304] = inp["rwkv_v_up"][l - 1]

    vec = np.zeros((P, NPAR), np.float32)
    col = lambda a: np.asarray(a).reshape(-1, P).T
    for l in range(L):
        got = dict(mu=inp["rwkv_mu"][l], w0=inp["rwkv_w0"][l], a0=inp["rwkv_a0"][l], kk=inp["rwkv_k_k"][l],
                   ka=inp["rwkv_k_a"][l], rk=inp["rwkv_r_k"][l], lnw=inp["rwkv_lnx_w"][l], lnb=inp["rwkv_lnx_b"][l],
                   lb=inp["hgrn_lb"][l], hnw=inp["hgrn_norm_w"][l], n1=inp["norm1_w"][l], n2=inp["norm2_w"][l],
                   adab=inp["ada_b"][l])
        if l:
            got["v0"] = inp["rwkv_v0"][l - 1]
        for name, a in got.items():
            vec[:, l * NPL + COL[name]:l * NPL + COL[name] + PARTS[name]] = col(a)
        vec[:, l * NPL + COL["dec"]:l * NPL + COL["dec"] + 8] = inp["ret_decay"][l].reshape(1, 8)
    vec[:, L * NPL:L * NPL + 8] = col(inp["final_norm_w"])
    cond = np.stack([inp["c_ctx"], inp["c"][0]])
    vec[:, L * NPL + 8:] = cond.reshape(2, KT, P).transpose(2, 1, 0).reshape(P, 16)
    x = np.concatenate([inp["ctx"][0], inp["x"][0]], 0)
    x = x.T.reshape(KT, P, N).transpose(1, 0, 2).reshape(P, KT * N)
    con, rcon = constants()
    return dict(weights=w, small_weights=small, vectors=vec, constants=con, ret_constants=rcon,
                x=np.ascontiguousarray(x))


def kernel(**inputs):
    import concourse.bacc as bacc
    from concourse.bass_utils import run_bass_kernel_spmd

    inp = {k: np.asarray(v) for k, v in inputs.items()}
    arrays = lay_out(inp)

    def program(known):
        nc = bacc.Bacc("TRN2", target_bir_lowering=False, num_devices=1)
        a = {k: nc.dram_tensor(f"in_{k}", v.shape, F32, kind="ExternalInput").ap() for k, v in arrays.items()}
        xscr = nc.dram_tensor("x_scratch", (P, KT * N), F32, kind="Internal").ap()
        out = nc.dram_tensor("out", (D, N - NC), F32, kind="ExternalOutput").ap()
        marks = build_program(nc, known, a["weights"], a["small_weights"], a["vectors"], a["constants"],
                              a["ret_constants"], a["x"], xscr, out)
        return nc, marks

    _, marks = program(None)
    nc, _ = program(marks)
    r = run_bass_kernel_spmd(nc, [{f"in_{k}": v for k, v in arrays.items()}], core_ids=[0])
    return np.ascontiguousarray(r.results[0]["out"].T)[None]
```

```python
import numpy as np
import concourse.bass as bass
import concourse.mybir as mybir
from contextlib import ExitStack

F32 = mybir.dt.float32
F32R = mybir.dt.float32r
U32 = mybir.dt.uint32
ALU = mybir.AluOpType
ACT = mybir.ActivationFunctionType

P = 128
D = 1024
KT = D // P
N = 512
NC = 256
L = 2
BW = 512
NT = BW // P
C = 64
M = N // C
FF = 4 * D
GRID = 64
ROWS = (N - NC) // GRID
SLOT = KT * P * 3 + NT * P * 3
RING = 3
DECAY = float(np.exp(-0.5))

K_ID, K_ONE, K_BONE, K_ROT = 0, 128, 256, 384
K_STRICT, K_INCL, K_LEV = 512, 640, 768
K_HLEV = 1152
K_SCAN = 2048
K_EPS = 3072
K_ID2 = 3076
NCONST = 3140
R_COS, R_SIN, R_LAG = 0, 512, 1024
NRC = 1024 + 6 * 384

PARTS = dict(mu=15, w0=8, a0=8, kk=4, ka=4, rk=4, lnw=4, lnb=4, v0=4, lb=8, hnw=4, n1=8, n2=8, adab=48, dec=8)
COL, NPL = {}, 0
for _n, _w in PARTS.items():
    COL[_n] = NPL
    NPL += _w
NPAR = L * NPL + 8 + 16

D_MOD, D_HMU, D_QMU, D_OMU, D_OMKA, D_WS1, D_WS2, D_LG, D_CS, D_LOW, D_OML = (
    0, 96, 111, 126, 141, 145, 161, 177, 185, 201, 217)
D_TMP = 233
NDER = 265

Y = [0, 2048, 4096]
YR, YH = 1, 2
X = 10240
TN = 24576
RT_A = 7168
RT_CS, RT_LAG, RT_STRIP = 6144, 14336, 16640
RT_QK, RT_V, RT_ROT, RT_O = 19712, 21760, 22784, 23808
RW_D = [4096, 11776]
RW_SCR, RW_KK, RW_SQ, RW_KS, RW_VT = 19456, 21504, 22016, 22528, 23040
RW_RKV, RW_SMALL, RW_W, RW_VD = 23552, 25088, 26624, 28928
(KR, BT, KTI, LT, TT, ABT, MT, AKT, RR, YK, BTT, KTT, WW) = (
    0, 1024, 1536, 2048, 2560, 3072, 3584, 4096, 4608, 5120, 6144, 6656, 7168)
HG_F, HG_Q, HG_K, HG_A, HG_V, HG_T = 6144, 10240, 14336, 18432, 24576, 26624
MG, MG_T = 14336, 18432
GATE_HI = 6144
HID_HI, HID_LO, NORMED_HI, HID_T = 0, 4096, 14336, 27136
WORK = 29440
ROWS2 = 28928


ADA_AT = {
    ("start", 0): [(0, 0), (0, 1), (0, 2), (0, 3), None], ("norm1", 0): [(0, 4), (0, 5)], ("strips", 0): [(0, 6)],
    ("small", 0): [(0, 7)],
    ("kk", 0, 0): [(0, 8)], ("keys", 0, 0): [(1, 0)], ("kk", 0, 1): [(0, 9)], ("keys", 0, 1): [(1, 1)],
    ("kk", 0, 2): [(0, 10)], ("keys", 0, 2): [(1, 2)], ("kk", 0, 3): [(1, 3)],
    ("out", 0): [(0, 11)], ("norm2", 0): [(1, 4)], ("mlp", 0): [(1, 5)],
    ("norm1", 1): [(1, 6), (1, 7)], ("strips", 1): [(1, 8)], ("small", 1): [(1, 9)],
    ("kk", 1, 0): [(1, 10)], ("kk", 1, 1): [(1, 11)], ("kk", 1, 2): [None],
}


def mlp_slots(l):
    return [(kind, l, 2 * q + g) for q in range(4) for kind in ("m1", "m2q") for g in range(2)]


def schedule_slots():
    out = []

    def ada(*place):
        for what in ADA_AT.get(place, ()):
            if what is not None:
                out.append((("ada", *what), 4 * KT * P))

    for l in range(L):
        ada("start", l)
        ada("norm1", l)
        for c in range(NT):
            out += [(("ret", l, c), 4 * KT * P)]
            if c == 0:
                ada("strips", l)
        out += [(("small", l), 3 * KT * P)]
        ada("small", l)
        for c in range(NT):
            out += [(("rw", l, c), 3 * KT * P)]
            ada("kk", l, c)
            ada("keys", l, c)
        out += [(("hi", l), 4 * KT * P)]
        out += [(("hf", l, c), 4 * KT * P) for c in range(NT)]
        ada("out", l)
        out += [(("gb", l, f), SLOT) for f in range(KT)]
        out += [(("out", l, a), 4 * KT * P) for a in range(2)]
        ada("norm2", l)
        if l < L - 1:
            for n, key in enumerate(mlp_slots(l)):
                out += [(key, 4 * KT * P)]
                if n == 1:
                    ada("mlp", l)
        else:
            out += [(("m1", l, a), 4 * KT * P) for a in range(8)]
            out += [(("m2", l, f), 32 * P) for f in range(8)]
    return out


class Steps:

    def __init__(self, ctx, nc, name, log, known):
        self.sem, self.name, self.log, self.known, self.n = ctx.enter_context(nc.semaphore(name)), name, log, known, 0

    def step(self, key=None, by=1):
        self.n += by
        if key is not None:
            self.also(key)
        return by

    def also(self, key):
        assert key not in self.log, key
        self.log[key] = (self.name, self.n)

    def at(self, *key):
        if self.known is None:
            return 1
        name, n = self.known[key]
        assert name == self.name, (key, name, self.name)
        return n


class Banks:

    def __init__(self, psum, first, n, width, steps, known, loaded):
        self.psum, self.first, self.n, self.width, self.steps, self.known = psum, first, n, width, steps, known
        self.loaded, self.keys, self.where = loaded, [], {}

    def fill(self, *key):
        self.where[key] = len(self.keys) % self.n
        self.keys.append(key)
        return self.get(*key)

    def freed(self):
        i = len(self.keys) - 1 - self.n
        if i < 0 or self.known is None:
            return self.loaded.sem, 16
        name, n = self.known[("drained", *self.keys[i])]
        return self.steps[name].sem, n

    def get(self, *key):
        b = self.first + self.where[key] * self.width
        return self.psum[:, 512 * b:512 * (b + self.width)]


def build_program(nc, known, wts, wsm, vec, con, rcon, xin, xscr, out):
    log = {}
    with ExitStack() as ctx:
        place = {}

        def sb(name, shape, dt=F32):
            t = ctx.enter_context(nc.sbuf_tensor(name, shape, dt))
            place[name] = nc.sbuf_base - 4 * int(np.prod(shape[1:]))
            return t

        ring = sb("weight_ring", [P, RING, SLOT])
        hT = sb("normed", [P, KT, N])
        vfirst = sb("v_first", [P, NT, N])
        kc = sb("constants", [P, NCONST])
        par = sb("vectors", [P, NPAR])
        der = sb("derived", [P, NDER])
        work = sb("work", [P, WORK])
        psum = ctx.enter_context(nc.psum_tensor("psum", [P, 4096], F32))

        def same_place(of, name, shape, at=0):
            return nc.alloc_sbuf_tensor_at(name, shape, F32R, offset=place[of] + 4 * at)

        ring_r = same_place("weight_ring", "weight_ring_parts", [P, RING, SLOT])
        hT_r = same_place("normed", "normed_low_part", [P, KT, N])
        hidden_hi = same_place("work", "hidden_high", [P, KT, N], HID_HI)
        hidden_lo = same_place("work", "hidden_low", [P, KT, N], HID_LO)
        normed_hi = same_place("work", "normed_high", [P, KT, N], NORMED_HI)
        gate_in_hi = same_place("work", "gate_input_high", [P, KT, N], GATE_HI)
        gate_in_lo = same_place("work", "gate_input_low", [P, KT, N], X)
        gate_whi = [same_place("work", f"gate_weights_high_{b}", [P, 3 * KT * P], o) for b, o in enumerate((20480, 24576))]
        whi = [[same_place("work", f"weights_high_{b}_{half}", [P, 2048], o) for half, o in enumerate(places)]
               for b, places in enumerate(((18432, 20480), (8192, 22528)))]

        steps = {}

        def counter(name):
            steps[name] = Steps(ctx, nc, name, log, known)
            return steps[name]

        big_filled, wide_filled = counter("big_filled"), counter("wide_filled")
        mid_filled, out_filled = counter("mid_filled"), counter("out_filled")
        vec_cond, act_cond = counter("vec_cond"), counter("act_cond")
        vec_norm, act_norm = counter("vec_norm"), counter("act_norm")
        vec_ret, act_ret, pool_ret = counter("vec_ret"), counter("act_ret"), counter("pool_ret")
        vec_rwkv, act_rwkv, pool_rwkv = counter("vec_rwkv"), counter("act_rwkv"), counter("pool_rwkv")
        vec_hgrn, act_hgrn, pool_hgrn = counter("vec_hgrn"), counter("act_hgrn"), counter("pool_hgrn")
        vec_merge, act_merge = counter("vec_merge"), counter("act_merge")
        vec_mlp, act_mlp, pool_mlp = counter("vec_mlp"), counter("act_mlp"), counter("pool_mlp")
        weights = [counter(f"weights_{i}") for i in range(RING)]
        loaded_vectors, loaded_x = counter("loaded_vectors"), counter("loaded_x")
        loaded_constants = counter("loaded_constants")
        loaded_ret_constants, loaded_small_weights = counter("loaded_ret_constants"), counter("loaded_small_weights")
        x_saved, x_back, stored = counter("x_saved"), counter("x_back"), counter("stored")
        block = ctx.enter_context(nc.Block())

        def banks(first, n, width=1):
            return Banks(psum, first, n, width, steps, known, loaded_vectors)

        big = banks(0, 2)
        wide = banks(2, 1, 2)
        mid = banks(4, 2)
        outb = banks(6, 2)

        slots = schedule_slots()
        slot_at = {key: i for i, (key, _) in enumerate(slots)}

        def wk(off, n=N):
            return work[:, off:off + n]

        def chunks(off, n=64, at=0, step=64, m0=0):
            return work[:, off:off + M * step].rearrange("p (m t) -> p m t", t=step)[:, m0:, at:at + n]

        def weights_hi(n, half):
            return whi[n % 2][half][:, :]

        def kcol(off, n):
            return kc[:, off:off + n]

        def over_chunks(ap, n, m0=0):
            return ap.rearrange("p (a t) -> p a t", a=1).broadcast_to([P, M - m0, n])

        def pcol(l, name, i=0, n=1):
            o = l * NPL + COL[name] + i
            return par[:, o:o + n]

        def dcol(o, n=1):
            return der[:, o:o + n]

        mod = der[:, D_MOD:D_MOD + 96].rearrange("p (t s) -> p t s", s=2)
        ident = kcol(K_ID, P)
        ones = kcol(K_ONE, P)
        bones = kcol(K_BONE, P)
        eps = {"rms": kcol(K_EPS, 1), "ln": kcol(K_EPS + 1, 1), "l2": kcol(K_EPS + 2, 1)}
        segs = [(0, 0, NC), (1, NC, N)]

        def live(l):
            return [(0, 0, NC), (1, NC, N)] if l < L - 1 else [(1, NC, N)]

        def rspan(l):
            s = live(l)
            return s[0][1], s[-1][2]

        def first_query(l):
            lo = rspan(l)[0]
            return lo, N - lo, lo // C

        def ada_steps(rows, what):
            if what is None:
                return [rows.pop(0) for _ in range(len(rows))]
            rows.append(what)
            return [rows.pop(0)] if len(rows) > 2 else []

        ada_order = [what for place in ADA_AT.values() for what in place if what is not None]

        def rows_at(what):
            p0 = 32 + 32 * (ada_order.index(what) % 2)
            return slice(p0, p0 + 2)

        ret_order = [("P", 0), ("R", 0), ("P", 1), ("A", 0), ("R", 1), ("O", 0), ("P", 2), ("A", 1), ("N", 0), ("R", 2),
                     ("O", 1), ("P", 3), ("A", 2), ("N", 1), ("R", 3), ("O", 2), ("A", 3), ("N", 2), ("O", 3), ("N", 3)]
        def wants_context(l, i):
            return l < L - 1 or (i >= NT and i != 14)

        scut = [(0, 0), (512, 0), (1024, NC), (1280, NC)]

        def chain_order(d):
            h = M // 2
            return list(range(M)) if d == 0 else list(range(h - 1, -1, -1)) + list(range(M - 1, h - 1, -1))

        @block.tensor
        def _(eng):
            mm = nc.tensor.matmul

            def slot(*key):
                i = slot_at[key]
                eng.wait_ge(weights[i % RING].sem, 16 * (i // RING + 1))
                return ring[:, i % RING, :]

            def tiled(s, j, k):
                return s[:, (j * KT + k) * P:(j * KT + k + 1) * P]

            def project(s, j, key, t0=0, t1=N, after_norm=None):
                ps = big.fill(*key)
                eng.wait_ge(*big.freed())
                for k in range(KT):
                    if after_norm is not None:
                        eng.wait_ge(act_norm.sem, act_norm.at("h tile", key[1], after_norm, k))
                    last = mm(ps[:, 0:t1 - t0], tiled(s, j, k), hT[:, k, t0:t1], start=(k == 0), stop=(k == KT - 1))
                last.then_inc(big_filled.sem, big_filled.step(key))

            def sum_over(lhs, rhs, key, n=N):
                ps = big.fill(*key)
                eng.wait_ge(*big.freed())
                mm(ps[:, 0:n], lhs, rhs, start=True, stop=True).then_inc(big_filled.sem, big_filled.step(key))

            def per_head(ps, w, lhs, rhs, m0=0):
                for m in range(m0, M):
                    for h in range(2):
                        q = slice(64 * h, 64 * h + 64)
                        last = mm(ps[q, w * m:w * m + w], lhs(q, m), rhs(q, m), start=True, stop=True)
                return last

            def with_keys_and_queries(ps, lhs, B, m0):
                for m in range(M):
                    n = 64 if m < m0 else 128
                    for h in range(2):
                        q = slice(64 * h, 64 * h + 64)
                        last = mm(ps[q, 128 * m:128 * m + n], lhs(q, m), work[q, B + KR + 128 * m:B + KR + 128 * m + n],
                                  start=True, stop=True)
                return last

            def norm(l, which, tiles=range(KT)):
                t0, t1 = (0, N) if which == 1 or l < L - 1 else (NC, N)
                if which == 3:
                    t0 = NC
                for k in tiles:
                    if k == 0:
                        outb.fill("sumsq", l, which)
                        eng.wait_ge(*outb.freed())
                    ps = outb.get("sumsq", l, which)
                    eng.wait_ge(act_norm.sem, act_norm.at("square", l, which, k))
                    last = mm(ps[:, 0:t1 - t0], ones, work[:, TN + 512 * (k % 2):TN + 512 * (k % 2) + t1 - t0],
                              start=(k == 0), stop=(k == KT - 1))
                    last.then_inc(out_filled.sem, out_filled.step(("squares read", l, which, k)))

            def norm_behind(l, which, f):
                norm(l, which, [f - 2] if 2 <= f < KT - 1 else [f - 2, f - 1, f] if f == KT - 1 else [])

            rows = []

            def modulation(*place):
                for what in ADA_AT.get(place, ()):
                    finished = ada_steps(rows, what)
                    if what is not None:
                        s = slot("ada", *what)
                        ps = mid.fill("ada", *what)
                        eng.wait_ge(*mid.freed())
                        for k in range(KT):
                            last = mm(ps[rows_at(what), :], der[:, D_CS + 2 * k:D_CS + 2 * k + 2], s[:, BW * k:BW * k + BW],
                                      start=(k == 0), stop=(k == KT - 1))
                        last.then_inc(mid_filled.sem, mid_filled.step(("ada", *what)))
                    for before in finished:
                        q = rows_at(before)
                        eng.wait_ge(loaded_constants.sem, loaded_constants.at("constants"))
                        eng.wait_ge(act_cond.sem, act_cond.at("drained", "ada", *before))
                        ps = outb.fill("ada columns", *before)
                        eng.wait_ge(*outb.freed())
                        for j in range(4):
                            last = mm(ps[:, 2 * j:2 * j + 2], work[q, ROWS2 + P * j:ROWS2 + P * j + P],
                                      kc[q, K_ID + q.start:K_ID + q.stop], start=True, stop=True)
                        last.then_inc(out_filled.sem, out_filled.step(("ada columns", *before)))

            eng.wait_ge(loaded_vectors.sem, loaded_vectors.at("vectors"))
            eng.wait_ge(act_cond.sem, act_cond.at("cond silu"))
            for l in range(L):
                lo, w, m0 = first_query(l)
                modulation("start", l)
                if l == 0:
                    norm(l, 1)
                modulation("norm1", l)

                for what, c in ret_order:
                    qk = RT_QK + 1024 * (c % 2)
                    v = RT_V + 512 * (c % 2)
                    A = RT_A + 1536 * (c % 2)
                    if what == "P":
                        s = slot("ret", l, c)
                        project(s, 0, ("rq", l, c), lo, N, 1 if c == 0 else None)
                        project(s, 1, ("rk", l, c))
                        if c == 0:
                            modulation("strips", l)
                        ps = big.fill("rv", l, c)
                        eng.wait_ge(*big.freed())
                        for i in range(4):
                            for k in range(KT):
                                last = mm(ps[:, P * i:P * i + P], hT[:, k, P * i:P * i + P], tiled(s, 2, k),
                                          start=(k == 0), stop=(k == KT - 1))
                        last.then_inc(big_filled.sem, big_filled.step(("rv", l, c)))
                        project(s, 3, ("rg", l, c), lo, N)
                    if what == "R":
                        for i, n in enumerate(("rq", "rk")):
                            eng.wait_ge(act_ret.sem, act_ret.at("drained", n, l, c))
                            t0 = lo if n == "rq" else 0
                            sum_over(kcol(K_ROT, P), wk(qk + 512 * i)[:, t0:N], (n + " turned", l, c), N - t0)
                    if what == "A":
                        eng.wait_ge(vec_ret.sem, vec_ret.at("roped", l, c))
                        for i in range(2):
                            if i == 0 or lo == 0:
                                ps = mid.fill("rA", l, c, i)
                                eng.wait_ge(*mid.freed())
                            o = 0 if lo == 0 else NC * i
                            last = mm(ps[:, o:o + w], work[:, qk + 512 + P * i:qk + 512 + P * i + P], work[:, qk + lo:qk + N],
                                      start=True, stop=True)
                            if i == 1 or lo == 0:
                                last.then_inc(mid_filled.sem, mid_filled.step(("rA", l, c, i if lo == 0 else 0)))
                        ps = mid.fill("rA", l, c, 2)
                        eng.wait_ge(*mid.freed())
                        for i in range(2, 4):
                            last = mm(ps[:, 256 * (i - 2):256 * (i - 2) + 256],
                                      work[:, qk + 512 + P * i:qk + 512 + P * i + P],
                                      work[:, qk + NC:qk + N], start=True, stop=True)
                        last.then_inc(mid_filled.sem, mid_filled.step(("rA", l, c, 2)))
                    if what == "O":
                        eng.wait_ge(vec_ret.sem, vec_ret.at("drained", "rA", l, c, 2))
                        eng.wait_ge(act_ret.sem, act_ret.at("drained", "rv", l, c))
                        ps = outb.fill("rO", l, c)
                        eng.wait_ge(*outb.freed())
                        for i, (col, t0) in enumerate(scut):
                            u = max(t0, lo)
                            last = mm(ps[:, u:N], work[:, v + P * i:v + P * i + P],
                                      work[:, A + col + u - t0:A + col + N - t0], start=(i == 0), stop=(i == 3))
                        last.then_inc(out_filled.sem, out_filled.step(("rO", l, c)))
                    if what == "N":
                        eng.wait_ge(pool_ret.sem, pool_ret.at("ret squared", l, c))
                        sum_over(ones, wk(RT_O + 512)[:, lo:N], ("rN", l, c), w)

                s = slot("small", l)
                for j in range(3):
                    project(s, j, ("small", l, j), lo if j == 2 else 0, N)
                eng.wait_ge(loaded_small_weights.sem, loaded_small_weights.at("small weights", l))
                if l > 0:
                    ps = big.fill("vd", l)
                    eng.wait_ge(*big.freed())
                    for k in range(KT):
                        last = mm(ps[0:32, :], work[:, RW_W + 1536 + 32 * k:RW_W + 1536 + 32 * k + 32], hT[:, k, :],
                                  start=(k == 0), stop=(k == KT - 1))
                    last.then_inc(big_filled.sem, big_filled.step(("vd", l)))
                modulation("small", l)

                def low_rank(c, d):
                    q = slice(64 * d, 64 * d + 64)
                    for j, n in enumerate(("zw", "za")):
                        ps = big.fill(n, l, c, d)
                        eng.wait_ge(*big.freed())
                        last = mm(ps, work[q, RW_W + 512 * j + P * c:RW_W + 512 * j + P * c + P],
                                  work[q, RW_SMALL + 512 * j:RW_SMALL + 512 * j + N], start=True, stop=True)
                        last.then_inc(big_filled.sem, big_filled.step((n, l, c, d)))

                for c in range(NT):
                    wcol = slice(P * c, P * c + P)
                    s = slot("rw", l, c)
                    project(s, 1, ("rkv", l, c, 1))
                    if c == 0:
                        eng.wait_ge(act_rwkv.sem, act_rwkv.at("small ready", l))
                    for d in range(2):
                        low_rank(c, d)
                    project(s, 0, ("rkv", l, c, 0), lo, N)
                    eng.wait_ge(pool_rwkv.sem, pool_rwkv.at("kk squared", l, c))
                    sum_over(bones, wk(RW_SQ), ("kk norm", l, c))
                    project(s, 2, ("rkv", l, c, 2))
                    if l > 0:
                        eng.wait_ge(act_rwkv.sem, act_rwkv.at("drained", "vd", l))
                        ps = big.fill("vgate", l, c)
                        eng.wait_ge(*big.freed())
                        last = mm(ps, wsm_up(work, wcol), work[0:32, RW_VD:RW_VD + N], start=True, stop=True)
                        last.then_inc(big_filled.sem, big_filled.step(("vgate", l, c)))
                    modulation("kk", l, c)
                    modulation("keys", l, c)
                    vsrc = (lambda q, m: vfirst[q, c, 64 * m:64 * m + 64]) if l == 0 else (
                        lambda q, m: work[q, RW_RKV + 1024 + 64 * m:RW_RKV + 1024 + 64 * m + 64])
                    idq = lambda q, m: kc[q, K_ID + q.start:K_ID + q.start + 64]

                    def cell(off, step=64, at=0, n=64):
                        return lambda q, m: work[q, off + step * m + at:off + step * m + at + n]

                    for d in range(2):
                        B = RW_D[d]
                        eng.wait_ge(vec_rwkv.sem, vec_rwkv.at("prepared", l, c, d))
                        eng.wait_ge(pool_rwkv.sem, pool_rwkv.at("b ready", l, c, d))
                        ps = wide.fill("gb", l, c, d)
                        eng.wait_ge(*wide.freed())
                        with_keys_and_queries(ps, cell(B + BT), B, m0).then_inc(wide_filled.sem, wide_filled.step(("gb", l, c, d)))
                        ps = mid.fill("tkk", l, c, d)
                        eng.wait_ge(*mid.freed())
                        per_head(ps, 64, cell(B + KR, 128), idq).then_inc(mid_filled.sem, mid_filled.step(("tkk", l, c, d)))
                        ps = mid.fill("tb", l, c, d)
                        eng.wait_ge(*mid.freed())
                        per_head(ps, 64, cell(B + BT), idq).then_inc(mid_filled.sem, mid_filled.step(("tb", l, c, d)))
                        ps = wide.fill("gk", l, c, d)
                        eng.wait_ge(*wide.freed())
                        with_keys_and_queries(ps, cell(B + KTI), B, m0).then_inc(wide_filled.sem, wide_filled.step(("gk", l, c, d)))
                        ps = mid.fill("tk", l, c, d)
                        eng.wait_ge(*mid.freed())
                        per_head(ps, 64, cell(B + KTI), idq).then_inc(mid_filled.sem, mid_filled.step(("tk", l, c, d)))
                    eng.wait_ge(vec_rwkv.sem, vec_rwkv.at("v ready", l, c))
                    ps = mid.fill("vT", l, c)
                    eng.wait_ge(*mid.freed())
                    per_head(ps, 64, vsrc, idq).then_inc(mid_filled.sem, mid_filled.step(("vT", l, c)))
                    for d in range(2):
                        B = RW_D[d]
                        eng.wait_ge(vec_rwkv.sem, vec_rwkv.at("level", l, c, d, 0))
                        ps = mid.fill("l1", l, c, d)
                        eng.wait_ge(*mid.freed())
                        per_head(ps, 64, cell(B + BT), idq).then_inc(mid_filled.sem, mid_filled.step(("l1", l, c, d)))
                        eng.wait_ge(act_rwkv.sem, act_rwkv.at("drained", "vT", l, c))
                        ps = mid.fill("mv", l, c, d)
                        eng.wait_ge(*mid.freed())
                        per_head(ps, 64, cell(B + MT), cell(RW_VT)).then_inc(mid_filled.sem, mid_filled.step(("mv", l, c, d)))
                    for j in range(1, 6):
                        for d in range(2):
                            B = RW_D[d]
                            eng.wait_ge(pool_rwkv.sem, pool_rwkv.at("level", l, c, d, j))
                            if j == 1:
                                eng.wait_ge(vec_rwkv.sem, vec_rwkv.at("drained", "l1", l, c, d))
                            else:
                                eng.wait_ge(vec_rwkv.sem, vec_rwkv.at("drained", "dT", l, c, d, j - 1))
                            ps = mid.fill("Z", l, c, d, j)
                            eng.wait_ge(*mid.freed())
                            per_head(ps, 64, cell(B + (KTI if j % 2 else BT)), cell(B + TT)).then_inc(mid_filled.sem, mid_filled.step(("Z", l, c, d, j)))
                        for d in range(2):
                            B = RW_D[d]
                            eng.wait_ge(act_rwkv.sem, act_rwkv.at("drained", "Z", l, c, d, j))
                            if j > 1:
                                eng.wait_ge(vec_rwkv.sem, vec_rwkv.at("drained", "dR", l, c, d, j - 1))
                            if j < 5:
                                ps = mid.fill("dT", l, c, d, j)
                                eng.wait_ge(*mid.freed())
                                per_head(ps, 64, cell(B + RR), cell(B + MT)).then_inc(mid_filled.sem, mid_filled.step(("dT", l, c, d, j)))
                            ps = mid.fill("dR", l, c, d, j)
                            eng.wait_ge(*mid.freed())
                            per_head(ps, 64, cell(B + MT), cell(B + RR)).then_inc(mid_filled.sem, mid_filled.step(("dR", l, c, d, j)))
                    for d in range(2):
                        B = RW_D[d]
                        eng.wait_ge(vec_rwkv.sem, vec_rwkv.at("drained", "dR", l, c, d, 5))
                        ps = wide.fill("uk", l, c, d)
                        eng.wait_ge(*wide.freed())
                        per_head(ps, 128, cell(B + RR), cell(B + YK, 128, 0, 128)).then_inc(wide_filled.sem, wide_filled.step(("uk", l, c, d)))
                    for d in range(2):
                        B = RW_D[d]
                        eng.wait_ge(act_rwkv.sem, act_rwkv.at("drained", "uk", l, c, d))
                        ps = mid.fill("rr", l, c, d)
                        eng.wait_ge(*mid.freed())
                        per_head(ps, 64, cell(B + LT, 128, 64), cell(B + ABT), m0).then_inc(mid_filled.sem, mid_filled.step(("rr", l, c, d)))
                        ps = mid.fill("pt", l, c, d)
                        eng.wait_ge(*mid.freed())
                        per_head(ps, 64, cell(B + LT, 128, 64), cell(B + BTT)).then_inc(mid_filled.sem, mid_filled.step(("pt", l, c, d)))
                    for d in range(2):
                        outb.fill("O", l, c, d)
                        eng.wait_ge(*outb.freed())
                    for i in range(M):
                        for d in range(2):
                            B = RW_D[d]
                            m = chain_order(d)[i]
                            if i < M - 1:
                                if i > 0:
                                    eng.wait_ge(vec_rwkv.sem, vec_rwkv.at("S", l, c, d, i))
                                if i == 1:
                                    eng.wait_ge(vec_rwkv.sem, vec_rwkv.at("drained", "pt", l, c, d))
                                ps = mid.fill("dS", l, c, d, i)
                                eng.wait_ge(*mid.freed())
                                for h in range(2):
                                    q = slice(64 * h, 64 * h + 64)
                                    ops = [(KTT, RW_VT, 64), (BTT, B + LT, 128)]
                                    for n, (a, r, rs) in enumerate(ops):
                                        last = mm(ps[q, 0:64], work[q, B + a + 64 * m:B + a + 64 * m + 64],
                                                  work[q, r + rs * m:r + rs * m + 64],
                                                  start=(n == 0), stop=(n == 1 and i == 0))
                                    if i > 0:
                                        last = mm(ps[q, 0:64], work[q, B + MT + 64 * m:B + MT + 64 * m + 64],
                                                  work[q, B + YK + 64 * i:B + YK + 64 * i + 64], start=False, stop=True)
                                last.then_inc(mid_filled.sem, mid_filled.step(("dS", l, c, d, i)))
                            if i == M - 1:
                                eng.wait_ge(vec_rwkv.sem, vec_rwkv.at("S", l, c, d, i))
                            if m < m0:
                                continue
                            ps = outb.get("O", l, c, d)
                            if i == m0:
                                eng.wait_ge(vec_rwkv.sem, vec_rwkv.at("drained", "rr", l, c, d))
                            for h in range(2):
                                q = slice(64 * h, 64 * h + 64)
                                o = ps[q, 64 * m:64 * m + 64]
                                mm(o, work[q, RW_VT + 64 * m:RW_VT + 64 * m + 64],
                                   work[q, B + AKT + 64 * m:B + AKT + 64 * m + 64], start=True, stop=False)
                                last = mm(o, work[q, B + LT + 128 * m:B + LT + 128 * m + 64],
                                          work[q, B + ABT + 64 * m:B + ABT + 64 * m + 64], start=False, stop=(i == 0))
                                if i > 0:
                                    last = mm(o, work[q, B + YK + 64 * i:B + YK + 64 * i + 64],
                                              work[q, B + KR + 128 * m + 64:B + KR + 128 * m + 128],
                                              start=False, stop=True)
                            if i == M - 1:
                                last.then_inc(out_filled.sem, out_filled.step(("O", l, c, d)))
                    eng.wait_ge(vec_rwkv.sem, vec_rwkv.at("o summed", l, c))
                    sum_over(bones, wk(RW_SCR)[:, lo:N], ("mean", l, c), w)
                    eng.wait_ge(vec_rwkv.sem, vec_rwkv.at("bonus terms", l, c))
                    sum_over(bones, wk(RW_KS)[:, lo:N], ("bonus", l, c), w)
                    eng.wait_ge(pool_rwkv.sem, pool_rwkv.at("centred squared", l, c))
                    sum_over(bones, wk(RW_SCR + 512)[:, lo:N], ("var", l, c), w)
                    sum_over(work[:, RW_W + 1024 + P * c:RW_W + 1024 + P * c + P], wk(RW_SMALL + 1024)[:, lo:N],
                             ("gate", l, c), w)

                s = slot("hi", l)
                for i in range(4):
                    ps = big.fill("hi", l, i)
                    eng.wait_ge(*big.freed())
                    for k in range(KT):
                        last = mm(ps, hT[:, k, P * i:P * i + P], s[:, BW * k:BW * k + BW], start=(k == 0), stop=(k == KT - 1))
                    last.then_inc(big_filled.sem, big_filled.step(("hi", l, i)))

                def hdiag(h):
                    eng.wait_ge(vec_hgrn.sem, vec_hgrn.at("hq ready", l, h))
                    ps = mid.fill("hd", l, h)
                    eng.wait_ge(*mid.freed())
                    for i in range(lo // P, 4):
                        t = slice(P * i, P * i + P)
                        for dd in range(2):
                            last = mm(ps[:, t], wk(HG_K + 2048 * dd + 512 * h)[:, t], wk(HG_T + 512 * (h % 2))[:, t],
                                      start=(dd == 0), stop=(dd == 1))
                    last.then_inc(mid_filled.sem, mid_filled.step(("hd", l, h)))

                for h in range(4):
                    s = slot("hf", l, h)
                    for j in range(4):
                        project(s, j, ("hf", l, h, j), lo if j >= 2 else 0, N)
                    if h > 0:
                        hdiag(h - 1)
                hdiag(3)
                for j in range(9):
                    for h in range(4):
                        if j > 0:
                            eng.wait_ge(vec_hgrn.sem, vec_hgrn.at("hq up", l, h, j - 1))
                            eng.wait_ge(pool_hgrn.sem, pool_hgrn.at("hk up", l, h, j - 1))
                        q_ = [wk(HG_Q_of(dd, h)) for dd in range(2)]
                        k_ = [wk(HG_K + 2048 * dd + 512 * h) for dd in range(2)]
                        ps = mid.fill("hl", l, h, j)
                        eng.wait_ge(*mid.freed())
                        if j < 7:
                            b = 1 << j
                            for i in range(lo // P, 4):
                                t = slice(P * i, P * i + P)
                                for dd in range(2):
                                    side = 1 - dd
                                    cols = lambda ap: ap[:, t].rearrange("p (n s b) -> p n s b", s=2, b=b)[:, :, side, :]
                                    last = mm(cols(ps), k_[dd][:, t], cols(q_[dd]), start=True, stop=True)
                        elif j == 7:
                            for i in range(lo // P, 4):
                                dd, o = i % 2, i ^ 1
                                last = mm(ps[:, P * i:P * i + P], k_[dd][:, P * i:P * i + P], q_[dd][:, P * o:P * o + P],
                                          start=True, stop=True)
                        else:
                            for i in range(2):
                                for dd in range(2):
                                    last = mm(ps[:, 256 * i:256 * i + 256], k_[dd][:, P * i:P * i + P], q_[dd][:, NC:N],
                                              start=(dd == 0), stop=(dd == 1))
                        last.then_inc(mid_filled.sem, mid_filled.step(("hl", l, h, j)))
                for h in range(4):
                    eng.wait_ge(act_hgrn.sem, act_hgrn.at("drained", "hl", l, h, 7))
                    eng.wait_ge(act_hgrn.sem, act_hgrn.at("drained", "hl", l, h, 8))
                    if h == 0:
                        eng.wait_ge(act_hgrn.sem, act_hgrn.at("drained", "hi", l, 3))
                    ps = outb.fill("hO", l, h)
                    eng.wait_ge(*outb.freed())
                    A = HG_A + 1536 * h
                    for i, (col, t0) in enumerate(scut):
                        u = max(t0, lo)
                        last = mm(ps[:, u:N], work[:, HG_V + 512 * i + P * h:HG_V + 512 * i + P * h + P],
                                  work[:, A + col + u - t0:A + col + N - t0], start=(i == 0), stop=(i == 3))
                    last.then_inc(out_filled.sem, out_filled.step(("hO", l, h)))
                for h in range(4):
                    if h == 2:
                        modulation("out", l)
                    eng.wait_ge(pool_hgrn.sem, pool_hgrn.at("hgrn squared", l, h))
                    sum_over(ones, wk(HG_T + 512 + 512 * (h % 2))[:, lo:N], ("hN", l, h), w)

                t0, t1 = rspan(l)
                eng.wait_ge(vec_hgrn.sem, vec_hgrn.at("y ready", l))
                for f in range(KT):
                    s = slot("gb", l, f)
                    for b in range(3):
                        if l < L - 1 and f > 0:
                            if b == 0:
                                eng.wait_ge(vec_merge.sem, vec_merge.at("gate weights split", l, f))
                            ps = big.fill("ga", l, f, b)
                            eng.wait_ge(*big.freed())
                            for k in range(KT):
                                t = (b * KT + k) * P
                                if f == 1 and b == 0:
                                    eng.wait_ge(vec_merge.sem, vec_merge.at("gate input split", l, k))
                                w_hi, w_lo = gate_whi[f % 2][:, t:t + P], ring_r[:, slot_at[("gb", l, f)] % RING, t:t + P]
                                mm(ps, w_hi, gate_in_hi[:, k, :], start=(k == 0), stop=False)
                                mm(ps, w_hi, gate_in_lo[:, k, :], start=False, stop=False)
                                last = mm(ps, w_lo, gate_in_hi[:, k, :], start=False, stop=(k == KT - 1))
                            last.then_inc(big_filled.sem, big_filled.step(("ga", l, f, b)))
                        else:
                            project(s, b, ("ga", l, f, b), t0, t1)
                        ps = big.fill("br", l, f, b)
                        eng.wait_ge(*big.freed())
                        for k in range(NT):
                            w0 = 3 * KT * P + (b * NT + k) * P
                            last = mm(ps[:, 0:t1 - t0], s[:, w0:w0 + P], work[:, Y[b] + 512 * k + t0:Y[b] + 512 * k + t1],
                                      start=(k == 0), stop=(k == NT - 1))
                        last.then_inc(big_filled.sem, big_filled.step(("br", l, f, b)))
                for f in range(KT):
                    if f % 4 == 0:
                        s = slot("out", l, f // 4)
                    ps = big.fill("ot", l, f)
                    eng.wait_ge(*big.freed())
                    for k in range(KT):
                        if f == 0:
                            eng.wait_ge(vec_merge.sem, vec_merge.at("merged", l, k))
                        last = mm(ps[:, 0:t1 - t0], tiled(s, f % 4, k), work[:, MG + 512 * k + t0:MG + 512 * k + t1],
                                  start=(k == 0), stop=(k == KT - 1))
                    last.then_inc(big_filled.sem, big_filled.step(("ot", l, f)))
                    norm_behind(l, 2, f)
                modulation("norm2", l)
                for n, key in enumerate(mlp_slots(l) if l < L - 1 else ()):
                    slot(*key)
                    s = ring_r[:, slot_at[key] % RING, :]
                    kind, _, a = key
                    eng.wait_ge(vec_mlp.sem, vec_mlp.at("weights split", l, n, 1))
                    for j in range(4):
                        if kind == "m1":
                            ps = big.fill("m1", l, 4 * a + j)
                            eng.wait_ge(*big.freed())
                            for k in range(KT):
                                t = j * KT + k
                                w_hi = weights_hi(n, t // 16)[:, P * (t % 16):P * (t % 16) + P]
                                if n == 0 and j == 0:
                                    eng.wait_ge(vec_mlp.sem, vec_mlp.at("normed split", l, k))
                                hi = normed_hi[:, k, :]
                                mm(ps, w_hi, hi, start=(k == 0), stop=False)
                                mm(ps, w_hi, hT_r[:, k, :], start=False, stop=False)
                                last = mm(ps, s[:, P * t:P * t + P], hi, start=False, stop=(k == KT - 1))
                            last.then_inc(big_filled.sem, big_filled.step(("m1", l, 4 * a + j)))
                        else:
                            q, f = a // 2, 4 * (a % 2) + j
                            ps = big.fill("m2", l, q, f)
                            eng.wait_ge(*big.freed())
                            for k in range(KT):
                                t = j * KT + k
                                w_hi = weights_hi(n, t // 16)[:, P * (t % 16):P * (t % 16) + P]
                                if f == 0:
                                    eng.wait_ge(vec_mlp.sem, vec_mlp.at("hidden", l, 8 * q + k))
                                hi = hidden_hi[:, k, :]
                                mm(ps, w_hi, hi, start=(k == 0), stop=False)
                                mm(ps, w_hi, hidden_lo[:, k, :], start=False, stop=False)
                                last = mm(ps, s[:, P * t:P * t + P], hi, start=False, stop=(k == KT - 1))
                            last.then_inc(big_filled.sem, big_filled.step(("m2", l, q, f)))
                            if q == 3:
                                norm_behind(l + 1, 1, f)
                    if n == 1:
                        modulation("mlp", l)
                for f in range(32 if l == L - 1 else 0):
                    if f % 4 == 0:
                        s = slot("m1", l, f // 4)
                    project(s, f % 4, ("m1", l, f), t0, t1, 2 if f == 0 else None)
                for f in range(KT if l == L - 1 else 0):
                    s = slot("m2", l, f)
                    ps = big.fill("m2", l, f)
                    eng.wait_ge(*big.freed())
                    for k in range(32):
                        if f == 0:
                            eng.wait_ge(pool_mlp.sem, pool_mlp.at("hidden", l, k))
                        last = mm(ps[:, 0:t1 - t0], s[:, P * k:P * k + P], work[:, hid(k) + t0:hid(k) + t1],
                                  start=(k == 0), stop=(k == 31))
                    last.then_inc(big_filled.sem, big_filled.step(("m2", l, f)))
                    norm_behind(l, 3, f)

        @block.vector
        def _(eng):
            tt, ts, stt, cp = (nc.vector.tensor_tensor, nc.vector.tensor_scalar, nc.vector.scalar_tensor_tensor,
                               nc.vector.tensor_copy)

            def drain_diag(l, h):
                eng.wait_ge(pool_hgrn.sem, pool_hgrn.at("scores clear", l, h))
                eng.wait_ge(mid_filled.sem, mid_filled.at("hd", l, h))
                msk = kc[:, K_ID:K_ID + P].bitcast(U32).rearrange("p (a t) -> p a t", a=1).broadcast_to([P, 2, P])
                for half, diag in enumerate(scores_diag(work, h)):
                    if half < first_query(l)[0] // NC:
                        continue
                    ps = mid.get("hd", l, h)[:, 256 * half:256 * half + 256].rearrange("p (i t) -> p i t", t=P)
                    nc.vector.copy_predicated(diag, msk, ps).then_inc(
                        vec_hgrn.sem, vec_hgrn.step(("drained", "hd", l, h) if half else None))
                    eng.wait_ge(vec_hgrn.sem, vec_hgrn.n)

            def hgrn_tail(l, h):
                eng.wait_ge(act_hgrn.sem, act_hgrn.at("hgrn rms", l, h))
                lo = first_query(l)[0]
                o = wk(HG_T + 1536 if h % 2 else HG_T)[:, lo:N]
                y = wk(Y[YH] + 512 * h)[:, lo:N]
                stt(o, o, pcol(l, "hnw", h), wk(HG_T + 512 + 512 * (h % 2))[:, lo:N], ALU.mult, ALU.mult).then_inc(
                    vec_hgrn.sem, vec_hgrn.step())
                eng.wait_ge(vec_hgrn.sem, vec_hgrn.n)
                tt(y, y, o, ALU.mult).then_inc(vec_hgrn.sem, vec_hgrn.step(("hgrn y", l, h)))
                eng.wait_ge(vec_hgrn.sem, vec_hgrn.n)

            def add_gated(done, ps, tile, x, parts, t0, key):
                for i, (sg, u0, u1) in enumerate(parts):
                    stt(work[:, x + u0:x + u1], ps[:, u0 - t0:u1 - t0], mod[:, tile, sg:sg + 1],
                        work[:, x + u0:x + u1], ALU.mult, ALU.add).then_inc(
                            done.sem, done.step(key if i == len(parts) - 1 else None))
                    eng.wait_ge(done.sem, done.n)

            def tail(l, which):
                t0, t1 = (0, N) if which == 1 or l < L - 1 else (NC, N)
                if which == 3:
                    t0 = NC
                eng.wait_ge(act_norm.sem, act_norm.at("rms", l, which))
                for k in range(KT):
                    o = TN + 1536 + 512 * (k % 2)
                    if which == 3:
                        stt(wk(X + 512 * k)[:, t0:t1], wk(X + 512 * k)[:, t0:t1],
                                     par[:, L * NPL + k:L * NPL + k + 1], work[:, TN + 1024:TN + 1024 + t1 - t0],
                                     ALU.mult, ALU.mult).then_inc(vec_norm.sem, vec_norm.step(("final", k)))
                        eng.wait_ge(vec_norm.sem, vec_norm.n)
                        continue
                    if k >= 2:
                        eng.wait_ge(act_norm.sem, act_norm.at("h tile", l, which, k - 2))
                    tt(work[:, o:o + t1 - t0], wk(X + 512 * k)[:, t0:t1], work[:, TN + 1024:TN + 1024 + t1 - t0],
                                ALU.mult).then_inc(vec_norm.sem, vec_norm.step(("x scaled", l, which, k)))
                    eng.wait_ge(vec_norm.sem, vec_norm.n)
                    if which == 2 and l < L - 1 and k >= 2:
                        normed_low(l, k - 2)
                if which == 2 and l < L - 1:
                    normed_low(l, KT - 2)
                    normed_low(l, KT - 1)

            def normed_low(l, k):
                eng.wait_ge(pool_mlp.sem, pool_mlp.at("normed high", l, k))
                hi = normed_hi[:, k, :].bitcast(F32)
                tt(hT_r[:, k, :], hT[:, k, :], hi, ALU.subtract).then_inc(vec_mlp.sem, vec_mlp.step(("normed split", l, k)))
                eng.wait_ge(vec_mlp.sem, vec_mlp.n)

            def weights_low(l, n):
                i = slot_at[mlp_slots(l)[n]]
                eng.wait_ge(weights[i % RING].sem, 16 * (i // RING + 1))
                for half in range(2):
                    eng.wait_ge(act_mlp.sem, act_mlp.at("weights high", l, n, half))
                    o = slice(2048 * half, 2048 * half + 2048)
                    tt(ring_r[:, i % RING, o], ring[:, i % RING, o], weights_hi(n, half).bitcast(F32), ALU.subtract).then_inc(
                        vec_mlp.sem, vec_mlp.step(("weights split", l, n, half)))
                    eng.wait_ge(vec_mlp.sem, vec_mlp.n)

            eng.wait_ge(loaded_vectors.sem, loaded_vectors.at("vectors"))
            lbs = [pcol(l, "lb", 0, 8) for l in range(L)]
            t = [dcol(D_TMP + 8 * i, 8) for i in range(4)]
            tt(t[0], lbs[0], lbs[1], ALU.max).then_inc(vec_cond.sem, vec_cond.step())
            eng.wait_ge(vec_cond.sem, vec_cond.n)
            tt(t[1], lbs[0], t[0], ALU.subtract).then_inc(vec_cond.sem, vec_cond.step())
            eng.wait_ge(vec_cond.sem, vec_cond.n)
            tt(t[2], lbs[1], t[0], ALU.subtract).then_inc(vec_cond.sem, vec_cond.step(("lb centred",)))
            eng.wait_ge(vec_cond.sem, vec_cond.n)
            eng.wait_ge(act_cond.sem, act_cond.at("lb exp"))
            tt(t[3], t[1], t[2], ALU.add).then_inc(vec_cond.sem, vec_cond.step())
            eng.wait_ge(vec_cond.sem, vec_cond.n)
            nc.vector.reciprocal(t[0], t[3]).then_inc(vec_cond.sem, vec_cond.step())
            eng.wait_ge(vec_cond.sem, vec_cond.n)
            tt(t[1], t[1], t[0], ALU.mult).then_inc(vec_cond.sem, vec_cond.step())
            eng.wait_ge(vec_cond.sem, vec_cond.n)
            tt(t[2], t[2], t[0], ALU.mult).then_inc(vec_cond.sem, vec_cond.step())
            eng.wait_ge(vec_cond.sem, vec_cond.n)
            tt(t[3], t[1], t[2], ALU.add).then_inc(vec_cond.sem, vec_cond.step())
            eng.wait_ge(vec_cond.sem, vec_cond.n)
            tt(dcol(D_LOW, 8), t[1], t[1], ALU.subtract).then_inc(vec_cond.sem, vec_cond.step())
            eng.wait_ge(vec_cond.sem, vec_cond.n)
            tt(dcol(D_LOW + 8, 8), t[3], t[1], ALU.subtract).then_inc(vec_cond.sem, vec_cond.step())
            eng.wait_ge(vec_cond.sem, vec_cond.n)
            ts(dcol(D_OML, 16), dcol(D_LOW, 16), -1.0, 1.0, ALU.mult, ALU.add).then_inc(vec_cond.sem, vec_cond.step())
            eng.wait_ge(vec_cond.sem, vec_cond.n)

            rows = []

            def modulation(*place):
                for what in ADA_AT.get(place, ()):
                    for l_, a in ada_steps(rows, what):
                        eng.wait_ge(out_filled.sem, out_filled.at("ada columns", l_, a))
                        ps = outb.get("ada columns", l_, a)[:, 0:8].rearrange("p (j s) -> p j s", s=2)
                        bias = pcol(l_, "adab", 4 * a, 4).rearrange("p (j s) -> p j s", s=1).broadcast_to([P, 4, 2])
                        tt(mod[:, 4 * a:4 * a + 4, :], ps, bias, ALU.add).then_inc(vec_cond.sem, vec_cond.step(("drained", "ada columns", l_, a)))
                        eng.wait_ge(vec_cond.sem, vec_cond.n)

            def norm_scale(l, dst, sc, w):
                wb = pcol(l, w, 0, 8).rearrange("p (j s) -> p j s", s=1).broadcast_to([P, 8, 2])
                stt(dcol(dst, 16).rearrange("p (j s) -> p j s", s=2), mod[:, sc:sc + 8, :], 1.0, wb,
                    ALU.add, ALU.mult).then_inc(vec_cond.sem, vec_cond.step(("norm scale", l, w)))
                eng.wait_ge(vec_cond.sem, vec_cond.n)

            eng.wait_ge(loaded_constants.sem, loaded_constants.at("constants"))
            for l in range(L):
                lo, w, m0 = first_query(l)
                modulation("start", l)
                norm_scale(l, D_WS1, 8, "n1")
                ts(dcol(D_HMU, 15), pcol(l, "mu", 0, 15), 0.5, None, ALU.mult).then_inc(vec_cond.sem, vec_cond.step())
                eng.wait_ge(vec_cond.sem, vec_cond.n)
                ts(dcol(D_QMU, 15), pcol(l, "mu", 0, 15), 0.25, None, ALU.mult).then_inc(vec_cond.sem, vec_cond.step())
                eng.wait_ge(vec_cond.sem, vec_cond.n)
                ts(dcol(D_OMU, 15), pcol(l, "mu", 0, 15), -1.0, 1.0, ALU.mult, ALU.add).then_inc(vec_cond.sem, vec_cond.step())
                eng.wait_ge(vec_cond.sem, vec_cond.n)
                ts(dcol(D_OMKA, 4), pcol(l, "ka", 0, 4), -1.0, 1.0, ALU.mult, ALU.add).then_inc(vec_cond.sem, vec_cond.step())
                eng.wait_ge(vec_cond.sem, vec_cond.n)
                eng.wait_ge(act_cond.sem, act_cond.at("ret decay exp", l))
                ts(dcol(D_LG, 8), dcol(D_LG, 8), -1.0, None, ALU.mult).then_inc(vec_cond.sem, vec_cond.step(("vectors derived", l)))
                eng.wait_ge(vec_cond.sem, vec_cond.n)
                tail(l, 1)
                modulation("norm1", l)

                for h in range(4):
                    S = RT_STRIP + 768 * h
                    eng.wait_ge(act_ret.sem, act_ret.at("strip exps", l, h))
                    tt(wk(S, 384), wk(S, 384), wk(RT_LAG + 768, 384), ALU.mult).then_inc(vec_ret.sem, vec_ret.step())
                    eng.wait_ge(vec_ret.sem, vec_ret.n)
                    tt(wk(RT_A + 768 * h, 384), wk(RT_A + 768 * h, 384), wk(RT_LAG + 1152, 384), ALU.mult).then_inc(vec_ret.sem, vec_ret.step())
                    eng.wait_ge(vec_ret.sem, vec_ret.n)
                    tt(wk(S, 768), wk(S, 768), wk(RT_A + 768 * h, 768), ALU.add).then_inc(vec_ret.sem, vec_ret.step())
                    eng.wait_ge(vec_ret.sem, vec_ret.n)
                    ts(wk(S, 768), wk(S, 768), float(P) ** -0.5, None, ALU.mult).then_inc(vec_ret.sem, vec_ret.step(("strip", l, h)))
                    eng.wait_ge(vec_ret.sem, vec_ret.n)
                for what, c in ret_order:
                    qk = RT_QK + 1024 * (c % 2)
                    A = RT_A + 1536 * (c % 2)
                    if what == "P" and c == 0:
                        modulation("strips", l)
                    if what == "R":
                        for i, n in enumerate(("rq", "rk")):
                            eng.wait_ge(big_filled.sem, big_filled.at(n + " turned", l, c))
                            t0 = lo if n == "rq" else 0
                            rot, x_ = wk(RT_ROT)[:, t0:N], wk(qk + 512 * i)[:, t0:N]
                            tt(rot, big.get(n + " turned", l, c)[:, 0:N - t0], wk(RT_CS + 512)[:, t0:N], ALU.mult).then_inc(vec_ret.sem, vec_ret.step(("drained", n + " turned", l, c)))
                            eng.wait_ge(vec_ret.sem, vec_ret.n)
                            tt(x_, x_, wk(RT_CS)[:, t0:N], ALU.mult).then_inc(vec_ret.sem, vec_ret.step())
                            eng.wait_ge(vec_ret.sem, vec_ret.n)
                            tt(x_, x_, rot, ALU.add).then_inc(vec_ret.sem, vec_ret.step(("roped", l, c) if i else None))
                            eng.wait_ge(vec_ret.sem, vec_ret.n)
                    if what == "A":
                        S = RT_STRIP + 768 * c
                        for i in range(2):
                            if lo == 0:
                                eng.wait_ge(mid_filled.sem, mid_filled.at("rA", l, c, i))
                                ps = mid.get("rA", l, c, i)
                                tt(wk(A + 512 * i, 256), ps[:, 0:256], wk(S + 128 - 128 * i, 256), ALU.mult).then_inc(vec_ret.sem, vec_ret.step())
                                eng.wait_ge(vec_ret.sem, vec_ret.n)
                                ps = ps[:, 256:512]
                            else:
                                eng.wait_ge(mid_filled.sem, mid_filled.at("rA", l, c, 0))
                                ps = mid.get("rA", l, c, 0)[:, NC * i:NC * i + NC]
                            tt(wk(A + 512 * i + 256, 256), ps, wk(S + 384 + 128 - 128 * i, 256),
                                        ALU.mult).then_inc(vec_ret.sem, vec_ret.step())
                            if lo == 0:
                                vec_ret.also(("drained", "rA", l, c, i))
                            elif i == 1:
                                vec_ret.also(("drained", "rA", l, c, 0))
                            eng.wait_ge(vec_ret.sem, vec_ret.n)
                        eng.wait_ge(mid_filled.sem, mid_filled.at("rA", l, c, 2))
                        ps = mid.get("rA", l, c, 2)
                        for i in range(2):
                            tt(wk(A + 1024 + 256 * i, 256), ps[:, 256 * i:256 * i + 256],
                                        wk(S + 128 - 128 * i, 256), ALU.mult).then_inc(vec_ret.sem, vec_ret.step(("drained", "rA", l, c, 2) if i else None))
                            eng.wait_ge(vec_ret.sem, vec_ret.n)
                    if what == "O":
                        eng.wait_ge(out_filled.sem, out_filled.at("rO", l, c))
                        cp(wk(RT_O)[:, lo:N], outb.get("rO", l, c)[:, lo:N]).then_inc(vec_ret.sem, vec_ret.step(("drained", "rO", l, c)))
                        eng.wait_ge(vec_ret.sem, vec_ret.n)
                    if what == "N":
                        eng.wait_ge(act_ret.sem, act_ret.at("ret rms", l, c))
                        tt(wk(RT_O)[:, lo:N], wk(RT_O)[:, lo:N], wk(RT_O + 1024)[:, lo:N], ALU.mult).then_inc(vec_ret.sem, vec_ret.step())
                        eng.wait_ge(vec_ret.sem, vec_ret.n)
                        eng.wait_ge(act_ret.sem, act_ret.at("drained", "rg", l, c))
                        y = wk(Y[YR] + 512 * c)[:, lo:N]
                        tt(y, y, wk(RT_O)[:, lo:N], ALU.mult).then_inc(vec_ret.sem, vec_ret.step(("ret y", l, c)))
                        eng.wait_ge(vec_ret.sem, vec_ret.n)

                def mix(i, dst, key):
                    eng.wait_ge(pool_rwkv.sem, pool_rwkv.at("neighbours", l, i))
                    raw = RW_SCR
                    ctx = wants_context(l, i)
                    if ctx:
                        ts(dst[:, 0:NC], wk(raw + 1, NC), dcol(D_OMU + i), None, ALU.mult).then_inc(vec_rwkv.sem, vec_rwkv.step())
                        eng.wait_ge(vec_rwkv.sem, vec_rwkv.n)
                    grid = wk(raw + 258, 396).rearrange("p (r t) -> p r t", t=66)[:, 1:5, 1:65]
                    dg = dst[:, NC:N].rearrange("p (r t) -> p r t", t=GRID)
                    ts(dg, grid, dcol(D_OMU + i), None, ALU.mult).then_inc(vec_rwkv.sem, vec_rwkv.step())
                    eng.wait_ge(vec_rwkv.sem, vec_rwkv.n)
                    if ctx:
                        stt(dst[:, 0:NC], wk(raw + 654, NC), dcol(D_HMU + i), dst[:, 0:NC], ALU.mult, ALU.add).then_inc(vec_rwkv.sem, vec_rwkv.step())
                        eng.wait_ge(vec_rwkv.sem, vec_rwkv.n)
                    stt(dst[:, NC:N], wk(raw + 654 + NC, NC), dcol(D_QMU + i), dst[:, NC:N], ALU.mult, ALU.add).then_inc(vec_rwkv.sem, vec_rwkv.step(key))
                    eng.wait_ge(vec_rwkv.sem, vec_rwkv.n)

                eng.wait_ge(x_saved.sem, x_saved.at("x saved", l))
                for j in range(3):
                    mix(12 + j, wk(RW_SMALL + 512 * j), ("mixed", l, 12 + j))
                modulation("small", l)
                for c in range(NT):
                    r, k = wk(RW_RKV), wk(RW_RKV + 512)
                    vv = vfirst[:, c, :] if l == 0 else wk(RW_RKV + 1024)

                    def decay_sums(d):
                        eng.wait_ge(act_rwkv.sem, act_rwkv.at("decay sigmoid", l, c, d))
                        G, sg, msk = wk(RW_D[d] + LT), wk(RW_D[d] + WW), kcol(K_SCAN + 512 * d, N)
                        if d == 1:
                            G, sg, msk = G[:, ::-1], sg[:, ::-1], msk[:, ::-1]
                        nc.vector.tensor_tensor_scan(G, msk, sg, 0.0, ALU.mult, ALU.add).then_inc(vec_rwkv.sem, vec_rwkv.step(("decay sums", l, c, d)))
                        eng.wait_ge(vec_rwkv.sem, vec_rwkv.n)

                    mix(4 + c, k, ("mixed", l, 4 + c))
                    ts(wk(RW_KK), k, pcol(l, "kk", c), None, ALU.mult).then_inc(vec_rwkv.sem, vec_rwkv.step(("kk raw", l, c)))
                    eng.wait_ge(vec_rwkv.sem, vec_rwkv.n)
                    for d in range(2):
                        decay_sums(d)
                    for d in range(2):
                        B = RW_D[d]
                        eng.wait_ge(act_rwkv.sem, act_rwkv.at("a sigmoid", l, c, d))
                        ts(wk(B + KTI), wk(B + BT), pcol(l, "ka", c), dcol(D_OMKA + c), ALU.mult, ALU.add).then_inc(vec_rwkv.sem, vec_rwkv.step(("a read", l, c, d)))
                        eng.wait_ge(vec_rwkv.sem, vec_rwkv.n)
                        tt(wk(B + KTI), wk(B + KTI), k, ALU.mult).then_inc(vec_rwkv.sem, vec_rwkv.step())
                        eng.wait_ge(vec_rwkv.sem, vec_rwkv.n)
                    mix(c, r, ("mixed", l, c))
                    ks = wk(RW_KS)[:, lo:N]
                    tt(ks, wk(RW_D[0] + KTI)[:, lo:N], wk(RW_D[1] + KTI)[:, lo:N], ALU.add).then_inc(vec_rwkv.sem, vec_rwkv.step())
                    eng.wait_ge(vec_rwkv.sem, vec_rwkv.n)
                    for d in range(2):
                        B = RW_D[d]
                        eng.wait_ge(act_rwkv.sem, act_rwkv.at("decays", l, c, d))
                        tt(wk(B + KTI), wk(B + KTI), wk(B + ABT), ALU.mult).then_inc(vec_rwkv.sem, vec_rwkv.step())
                        eng.wait_ge(vec_rwkv.sem, vec_rwkv.n)
                        tt(chunks(B + KR, 64, 64, 128, m0), chunks(RW_RKV, m0=m0), chunks(B + WW)[:, m0:, :], ALU.mult).then_inc(vec_rwkv.sem, vec_rwkv.step())
                        eng.wait_ge(vec_rwkv.sem, vec_rwkv.n)
                    eng.wait_ge(act_rwkv.sem, act_rwkv.at("kk rms", l, c))
                    tt(wk(RW_KK), wk(RW_KK), wk(RW_SQ), ALU.mult).then_inc(vec_rwkv.sem, vec_rwkv.step(("kk ready", l, c)))
                    eng.wait_ge(vec_rwkv.sem, vec_rwkv.n)
                    for d in range(2):
                        B = RW_D[d]
                        kk3, W3 = chunks(RW_KK), chunks(B + WW)
                        KR3 = chunks(B + KR, 64, 0, 128)
                        e = 0 if d == 0 else 63
                        a, b = (slice(1, 64), slice(0, 63)) if d == 0 else (slice(0, 63), slice(1, 64))
                        tt(KR3[:, :, a], kk3[:, :, a], W3[:, :, b], ALU.mult).then_inc(vec_rwkv.sem, vec_rwkv.step())
                        eng.wait_ge(vec_rwkv.sem, vec_rwkv.n)
                        cp(KR3[:, :, e:e + 1], kk3[:, :, e:e + 1]).then_inc(vec_rwkv.sem, vec_rwkv.step())
                        eng.wait_ge(vec_rwkv.sem, vec_rwkv.n)
                        vec_rwkv.also(("prepared", l, c, d))
                    mix(8 + c, vv, ("mixed", l, 8 + c))
                    if l > 0:
                        tt(wk(RW_SCR + 512), vfirst[:, c, :], vv, ALU.subtract).then_inc(vec_rwkv.sem, vec_rwkv.step())
                        eng.wait_ge(vec_rwkv.sem, vec_rwkv.n)
                        eng.wait_ge(act_rwkv.sem, act_rwkv.at("vgate sigmoid", l, c))
                        tt(wk(RW_SCR + 512), wk(RW_SCR + 512), wk(RW_SCR), ALU.mult).then_inc(vec_rwkv.sem, vec_rwkv.step())
                        eng.wait_ge(vec_rwkv.sem, vec_rwkv.n)
                        tt(vv, vv, wk(RW_SCR + 512), ALU.add).then_inc(vec_rwkv.sem, vec_rwkv.step(("v ready", l, c)))
                        eng.wait_ge(vec_rwkv.sem, vec_rwkv.n)
                    else:
                        vec_rwkv.also(("v ready", l, c))
                    ts(ks, ks, pcol(l, "rk", c), None, ALU.mult).then_inc(vec_rwkv.sem, vec_rwkv.step())
                    eng.wait_ge(vec_rwkv.sem, vec_rwkv.n)
                    tt(ks, ks, r[:, lo:N], ALU.mult).then_inc(vec_rwkv.sem, vec_rwkv.step(("bonus terms", l, c)))
                    eng.wait_ge(vec_rwkv.sem, vec_rwkv.n)
                    modulation("kk", l, c)
                    modulation("keys", l, c)
                    for d in range(2):
                        B = RW_D[d]
                        eng.wait_ge(wide_filled.sem, wide_filled.at("gb", l, c, d))
                        ps = wide.get("gb", l, c, d).rearrange("p (m t) -> p m t", t=128)
                        tt(chunks(B + LT), ps[:, :, 0:64], over_chunks(kcol(K_STRICT + 64 * d, 64), 64), ALU.mult).then_inc(vec_rwkv.sem, vec_rwkv.step())
                        eng.wait_ge(vec_rwkv.sem, vec_rwkv.n)
                        tt(chunks(B + ABT, m0=m0), ps[:, m0:, 64:128], over_chunks(kcol(K_INCL + 64 * d, 64), 64, m0), ALU.mult).then_inc(vec_rwkv.sem, vec_rwkv.step(("drained", "gb", l, c, d)))
                        eng.wait_ge(vec_rwkv.sem, vec_rwkv.n)
                        eng.wait_ge(wide_filled.sem, wide_filled.at("gk", l, c, d))
                        ps = wide.get("gk", l, c, d).rearrange("p (m t) -> p m t", t=128)
                        tt(chunks(B + MT), ps[:, :, 0:64], over_chunks(kcol(K_STRICT + 64 * d, 64), 64), ALU.mult).then_inc(vec_rwkv.sem, vec_rwkv.step())
                        eng.wait_ge(vec_rwkv.sem, vec_rwkv.n)
                        tt(chunks(B + AKT, m0=m0), ps[:, m0:, 64:128], over_chunks(kcol(K_INCL + 64 * d, 64), 64, m0), ALU.mult).then_inc(vec_rwkv.sem, vec_rwkv.step(("drained", "gk", l, c, d)))
                        eng.wait_ge(vec_rwkv.sem, vec_rwkv.n)
                        eng.wait_ge(mid_filled.sem, mid_filled.at("tb", l, c, d))
                        tt(chunks(B + BT), chunks(B + LT), over_chunks(kcol(K_LEV, 64), 64), ALU.mult).then_inc(vec_rwkv.sem, vec_rwkv.step(("level", l, c, d, 0)))
                        eng.wait_ge(vec_rwkv.sem, vec_rwkv.n)
                        tt(chunks(B + RR), ident64(kc), chunks(B + BT), ALU.subtract).then_inc(vec_rwkv.sem, vec_rwkv.step(("R first", l, c, d)))
                        eng.wait_ge(vec_rwkv.sem, vec_rwkv.n)
                    for d in range(2):
                        B = RW_D[d]
                        eng.wait_ge(mid_filled.sem, mid_filled.at("l1", l, c, d))
                        tt(chunks(B + TT), ident64(kc), mid.get("l1", l, c, d).rearrange("p (m t) -> p m t", t=64),
                                    ALU.subtract).then_inc(vec_rwkv.sem, vec_rwkv.step(("drained", "l1", l, c, d)))
                        eng.wait_ge(vec_rwkv.sem, vec_rwkv.n)
                    for j in range(1, 6):
                        for d in range(2):
                            B = RW_D[d]
                            for n, o in (("dT", TT), ("dR", RR)):
                                if n == "dT" and j == 5:
                                    continue
                                eng.wait_ge(mid_filled.sem, mid_filled.at(n, l, c, d, j))
                                tt(wk(B + o), wk(B + o), mid.get(n, l, c, d, j), ALU.subtract).then_inc(vec_rwkv.sem, vec_rwkv.step(("drained", n, l, c, d, j)))
                                eng.wait_ge(vec_rwkv.sem, vec_rwkv.n)
                    for d in range(2):
                        B = RW_D[d]
                        eng.wait_ge(mid_filled.sem, mid_filled.at("rr", l, c, d))
                        tt(chunks(B + KR, 64, 64, 128, m0), chunks(B + KR, 64, 64, 128, m0),
                                    mid.get("rr", l, c, d).rearrange("p (m t) -> p m t", t=64)[:, m0:, :], ALU.add).then_inc(vec_rwkv.sem, vec_rwkv.step(("drained", "rr", l, c, d)))
                        eng.wait_ge(vec_rwkv.sem, vec_rwkv.n)
                        eng.wait_ge(mid_filled.sem, mid_filled.at("pt", l, c, d))
                        tt(chunks(B + MT), ident64(kc), mid.get("pt", l, c, d).rearrange("p (m t) -> p m t", t=64),
                                    ALU.add).then_inc(vec_rwkv.sem, vec_rwkv.step(("drained", "pt", l, c, d)))
                        eng.wait_ge(vec_rwkv.sem, vec_rwkv.n)
                    for i in range(M - 1):
                        for d in range(2):
                            B = RW_D[d]
                            m = chain_order(d)[i]
                            e = 64 * m + (63 if d == 0 else 0)
                            eng.wait_ge(mid_filled.sem, mid_filled.at("dS", l, c, d, i))
                            ts(wk(B + YK + 64 * (i + 1), 64), mid.get("dS", l, c, d, i)[:, 0:64],
                                        work[:, B + WW + e:B + WW + e + 1], None, ALU.mult).then_inc(vec_rwkv.sem, vec_rwkv.step(("S", l, c, d, i + 1)))
                            eng.wait_ge(vec_rwkv.sem, vec_rwkv.n)
                            vec_rwkv.also(("drained", "dS", l, c, d, i))
                    eng.wait_ge(out_filled.sem, out_filled.at("O", l, c, 0))
                    cp(wk(RW_SCR)[:, lo:N], outb.get("O", l, c, 0)[:, lo:N]).then_inc(vec_rwkv.sem, vec_rwkv.step(("drained", "O", l, c, 0)))
                    eng.wait_ge(vec_rwkv.sem, vec_rwkv.n)
                    eng.wait_ge(out_filled.sem, out_filled.at("O", l, c, 1))
                    tt(wk(RW_SCR)[:, lo:N], wk(RW_SCR)[:, lo:N], outb.get("O", l, c, 1)[:, lo:N], ALU.add).then_inc(vec_rwkv.sem, vec_rwkv.step(("drained", "O", l, c, 1)))
                    eng.wait_ge(vec_rwkv.sem, vec_rwkv.n)
                    vec_rwkv.also(("o summed", l, c))
                    eng.wait_ge(big_filled.sem, big_filled.at("mean", l, c))
                    stt(wk(RW_SCR)[:, lo:N], big.get("mean", l, c)[:, 0:w], -1.0 / 64, wk(RW_SCR)[:, lo:N], ALU.mult, ALU.add).then_inc(vec_rwkv.sem, vec_rwkv.step(("drained", "mean", l, c)))
                    eng.wait_ge(vec_rwkv.sem, vec_rwkv.n)
                    eng.wait_ge(big_filled.sem, big_filled.at("bonus", l, c))
                    tt(wk(RW_SCR + 1536)[:, lo:N], big.get("bonus", l, c)[:, 0:w], vv[:, lo:N], ALU.mult).then_inc(vec_rwkv.sem, vec_rwkv.step(("drained", "bonus", l, c)))
                    eng.wait_ge(vec_rwkv.sem, vec_rwkv.n)
                    eng.wait_ge(act_rwkv.sem, act_rwkv.at("rwkv rms", l, c))
                    tt(wk(RW_SCR)[:, lo:N], wk(RW_SCR)[:, lo:N], wk(RW_SCR + 1024)[:, lo:N], ALU.mult).then_inc(vec_rwkv.sem, vec_rwkv.step())
                    eng.wait_ge(vec_rwkv.sem, vec_rwkv.n)
                    ts(wk(RW_SCR)[:, lo:N], wk(RW_SCR)[:, lo:N], pcol(l, "lnw", c), pcol(l, "lnb", c), ALU.mult, ALU.add).then_inc(vec_rwkv.sem, vec_rwkv.step())
                    eng.wait_ge(vec_rwkv.sem, vec_rwkv.n)
                    tt(wk(RW_SCR)[:, lo:N], wk(RW_SCR)[:, lo:N], wk(RW_SCR + 1536)[:, lo:N], ALU.add).then_inc(vec_rwkv.sem, vec_rwkv.step())
                    eng.wait_ge(vec_rwkv.sem, vec_rwkv.n)
                    eng.wait_ge(big_filled.sem, big_filled.at("gate", l, c))
                    tt(wk(Y[0] + 512 * c)[:, lo:N], wk(RW_SCR)[:, lo:N], big.get("gate", l, c)[:, 0:w], ALU.mult).then_inc(vec_rwkv.sem, vec_rwkv.step(("drained", "gate", l, c)))
                    eng.wait_ge(vec_rwkv.sem, vec_rwkv.n)

                for h in range(4):
                    for dd in range(2):
                        F, K = wk(HG_F + 2048 * dd + 512 * h), wk(HG_K + 2048 * dd + 512 * h)
                        om, low = dcol(D_OML + 8 * l + 4 * dd + h), dcol(D_LOW + 8 * l + 4 * dd + h)
                        eng.wait_ge(act_hgrn.sem, act_hgrn.at("forget sigmoid", l, h, dd))
                        ts(F, F, om, low, ALU.mult, ALU.add).then_inc(vec_hgrn.sem, vec_hgrn.step())
                        eng.wait_ge(vec_hgrn.sem, vec_hgrn.n)
                        ts(K, K, om, None, ALU.mult).then_inc(vec_hgrn.sem, vec_hgrn.step())
                        eng.wait_ge(vec_hgrn.sem, vec_hgrn.n)
                    eng.wait_ge(act_hgrn.sem, act_hgrn.at("hq silu", l, h))
                    for dd in range(2):
                        tt(wk(HG_Q_of(dd, h))[:, lo:N], wk(HG_T + 512 * (h % 2))[:, lo:N], wk(HG_F + 2048 * dd + 512 * h)[:, lo:N],
                           ALU.mult).then_inc(vec_hgrn.sem, vec_hgrn.step(("hq ready", l, h) if dd else None))
                        eng.wait_ge(vec_hgrn.sem, vec_hgrn.n)
                    if h > 0:
                        drain_diag(l, h - 1)
                drain_diag(l, 3)
                for j in range(9):
                    for h in range(4):
                        if j < 7:
                            eng.wait_ge(mid_filled.sem, mid_filled.at("hl", l, h, j))
                            diag = scores_diag(work, h)
                            for half in range(lo // NC, 2):
                                msk = kc[:, K_HLEV + 128 * j:K_HLEV + 128 * j + 128].bitcast(U32) \
                                    .rearrange("p (a t) -> p a t", a=1).broadcast_to([P, 2, P])
                                nc.vector.copy_predicated(
                                    diag[half], msk,
                                    mid.get("hl", l, h, j)[:, 256 * half:256 * half + 256].rearrange("p (i t) -> p i t", t=P)).then_inc(vec_hgrn.sem, vec_hgrn.step(("drained", "hl", l, h, j) if half else None))
                                eng.wait_ge(vec_hgrn.sem, vec_hgrn.n)
                        if j < 8:
                            if j == 7:
                                eng.wait_ge(mid_filled.sem, mid_filled.at("hl", l, h, j))
                            if j > 0:
                                eng.wait_ge(pool_hgrn.sem, pool_hgrn.at("F up", l, h, j - 1))
                            b = 1 << j
                            for dd in range(2):
                                pair = lambda ap: ap[:, lo:N].rearrange("p (n s b) -> p n s b", s=2, b=b)
                                side = 1 - dd
                                q = pair(wk(HG_Q_of(dd, h)))[:, :, side, :]
                                fe = pair(wk(HG_F + 2048 * dd + 512 * h))[:, :, 1 - side, 0:1].broadcast_to([P, w // (2 * b), b])
                                tt(q, q, fe, ALU.mult).then_inc(vec_hgrn.sem, vec_hgrn.step(("hq up", l, h, j) if dd else None))
                                eng.wait_ge(vec_hgrn.sem, vec_hgrn.n)
                for h in range(4):
                    eng.wait_ge(out_filled.sem, out_filled.at("hO", l, h))
                    o = HG_T + 1536 if h % 2 else HG_T
                    cp(wk(o)[:, lo:N], outb.get("hO", l, h)[:, lo:N]).then_inc(vec_hgrn.sem, vec_hgrn.step(("drained", "hO", l, h)))
                    eng.wait_ge(vec_hgrn.sem, vec_hgrn.n)
                    if h > 0:
                        hgrn_tail(l, h - 1)
                hgrn_tail(l, 3)
                vec_hgrn.also(("y ready", l))
                modulation("out", l)
                norm_scale(l, D_WS2, 32, "n2")

                t0, t1 = rspan(l)
                n = t1 - t0
                for f in range(KT):
                    mg = wk(MG + 512 * f)[:, t0:t1]
                    for b in range(3):
                        if l < L - 1 and f == 0:
                            for k in range(*((0, 3), (3, 6), (6, 8))[b]):
                                eng.wait_ge(pool_mlp.sem, pool_mlp.at("gate input high", l, k))
                                tt(gate_in_lo[:, k, :], hT[:, k, :], gate_in_hi[:, k, :].bitcast(F32), ALU.subtract).then_inc(
                                    vec_merge.sem, vec_merge.step(("gate input split", l, k)))
                                eng.wait_ge(vec_merge.sem, vec_merge.n)
                        eng.wait_ge(big_filled.sem, big_filled.at("br", l, f, b))
                        eng.wait_ge(act_merge.sem, act_merge.at("drained", "ga", l, f, b))
                        sg = work[:, MG_T + 512 * ((3 * f + b) % 3):MG_T + 512 * ((3 * f + b) % 3) + n]
                        o = mg if b == 0 else work[:, MG_T + 1536:MG_T + 1536 + n]
                        tt(o, big.get("br", l, f, b)[:, 0:n], sg, ALU.mult).then_inc(vec_merge.sem, vec_merge.step(("drained", "br", l, f, b)))
                        eng.wait_ge(vec_merge.sem, vec_merge.n)
                        if b:
                            tt(mg, mg, o, ALU.add).then_inc(vec_merge.sem, vec_merge.step(("merged", l, f) if b == 2 else None))
                            eng.wait_ge(vec_merge.sem, vec_merge.n)
                        if b == 0 and l < L - 1 and f < KT - 1:
                            i = slot_at[("gb", l, f + 1)]
                            eng.wait_ge(weights[i % RING].sem, 16 * (i // RING + 1))
                            eng.wait_ge(act_merge.sem, act_merge.at("gate weights high", l, f + 1))
                            cut = slice(0, 3 * KT * P)
                            tt(ring_r[:, i % RING, cut], ring[:, i % RING, cut], gate_whi[(f + 1) % 2][:, :].bitcast(F32),
                               ALU.subtract).then_inc(vec_merge.sem, vec_merge.step(("gate weights split", l, f + 1)))
                            eng.wait_ge(vec_merge.sem, vec_merge.n)
                eng.wait_ge(x_back.sem, x_back.at("x back", l))
                for f in range(KT):
                    eng.wait_ge(big_filled.sem, big_filled.at("ot", l, f))
                    add_gated(vec_merge, big.get("ot", l, f), 16 + f, X + 512 * f, live(l), t0, ("drained", "ot", l, f))
                    if f == 5 and l < L - 1:
                        weights_low(l, 0)
                tail(l, 2)
                modulation("norm2", l)
                for n, (kind, _, a) in enumerate(mlp_slots(l) if l < L - 1 else ()):
                    if n < 15:
                        weights_low(l, n + 1)
                    for j in range(4):
                        if kind == "m1":
                            f = 4 * a + j
                            eng.wait_ge(big_filled.sem, big_filled.at("m1", l, f))
                            if f >= 2:
                                eng.wait_ge(act_mlp.sem, act_mlp.at("hidden high", l, f - 2))
                            t = wk(HID_T + 512 * (f % 2))
                            ps = big.get("m1", l, f)
                            ts(t, ps, 0.0, None, ALU.max).then_inc(vec_mlp.sem, vec_mlp.step(("drained", "m1", l, f)))
                            eng.wait_ge(vec_mlp.sem, vec_mlp.n)
                            tt(t, t, t, ALU.mult).then_inc(vec_mlp.sem, vec_mlp.step(("squared", l, f)))
                            eng.wait_ge(vec_mlp.sem, vec_mlp.n)
                            eng.wait_ge(act_mlp.sem, act_mlp.at("hidden high", l, f))
                            hi = hidden_hi[:, f % 8, :].bitcast(F32)
                            tt(hidden_lo[:, f % 8, :], t, hi, ALU.subtract).then_inc(vec_mlp.sem, vec_mlp.step(("hidden", l, f)))
                            eng.wait_ge(vec_mlp.sem, vec_mlp.n)
                        else:
                            q, f = a // 2, 4 * (a % 2) + j
                            eng.wait_ge(big_filled.sem, big_filled.at("m2", l, q, f))
                            add_gated(vec_mlp, big.get("m2", l, q, f), 40 + f, X + 512 * f, live(l), t0, ("drained", "m2", l, q, f))
                            if q == 3:
                                vec_mlp.also(("drained", "m2", l, f))
                    if n == 1:
                        modulation("mlp", l)
                for f in range(KT if l == L - 1 else 0):
                    eng.wait_ge(big_filled.sem, big_filled.at("m2", l, f))
                    add_gated(vec_mlp, big.get("m2", l, f), 40 + f, X + 512 * f, live(l), t0, ("drained", "m2", l, f))
            tail(L - 1, 3)

        @block.scalar
        def _(eng):
            act = nc.scalar.activation

            eng.dma_start(par[:, :], vec).then_inc(loaded_vectors.sem, loaded_vectors.step(("vectors",), 16))
            eng.dma_start(kc[:, :], con).then_inc(loaded_constants.sem, loaded_constants.step(("constants",), 16))
            eng.dma_start(work[:, X:X + KT * N], xin).then_inc(loaded_x.sem, loaded_x.step(("x loaded",), 16))

            def rsqrt(done, dst, ps, scale, e, key, drained):
                act(dst, ps, ACT.Ln, bias=eps[e], scale=scale).then_inc(done.sem, done.step(drained))
                eng.wait_ge(done.sem, done.n)
                act(dst, dst, ACT.Exp, scale=-0.5).then_inc(done.sem, done.step(key))
                eng.wait_ge(done.sem, done.n)

            def weights_high(l, n):
                key = mlp_slots(l)[n]
                i = slot_at[key]
                eng.wait_ge(weights[i % RING].sem, 16 * (i // RING + 1))
                if n >= 2:
                    eng.wait_ge(big_filled.sem, big_filled.at(*last_use(mlp_slots(l)[n - 2])))
                for half in range(2):
                    act(weights_hi(n, half), ring[:, i % RING, 2048 * half:2048 * half + 2048], ACT.Copy).then_inc(
                        act_mlp.sem, act_mlp.step(("weights high", l, n, half)))
                    eng.wait_ge(act_mlp.sem, act_mlp.n)

            def norm(l, which):
                t0, t1 = (0, N) if which == 1 or l < L - 1 else (NC, N)
                if which == 3:
                    t0 = NC
                n = t1 - t0
                if which == 1 and l == 0:
                    eng.wait_ge(loaded_x.sem, loaded_x.at("x loaded"))
                for k in range(KT):
                    if which == 2 and l < L - 1 and k == 5:
                        weights_high(l, 0)
                    if which == 2:
                        eng.wait_ge(vec_merge.sem, vec_merge.at("drained", "ot", l, k))
                    elif which == 3 or l > 0:
                        eng.wait_ge(vec_mlp.sem, vec_mlp.at("drained", "m2", l if which == 3 else l - 1, k))
                    if k >= 2:
                        eng.wait_ge(out_filled.sem, out_filled.at("squares read", l, which, k - 2))
                    act(work[:, TN + 512 * (k % 2):TN + 512 * (k % 2) + n], wk(X + 512 * k)[:, t0:t1], ACT.Square).then_inc(act_norm.sem, act_norm.step(("square", l, which, k)))
                    eng.wait_ge(act_norm.sem, act_norm.n)
                eng.wait_ge(out_filled.sem, out_filled.at("squares read", l, which, 7))
                rsqrt(act_norm, work[:, TN + 1024:TN + 1024 + n], outb.get("sumsq", l, which)[:, 0:n], 1.0 / D, "rms",
                      ("rms", l, which), ("drained", "sumsq", l, which))
                if which == 3:
                    return
                eng.wait_ge(vec_cond.sem, vec_cond.at("vectors derived", l) if which == 1 else vec_cond.at("norm scale", l, "n2"))
                ws, sh = (D_WS1, 0) if which == 1 else (D_WS2, 24)
                for k in range(KT):
                    eng.wait_ge(vec_norm.sem, vec_norm.at("x scaled", l, which, k))
                    o = TN + 1536 + 512 * (k % 2)
                    parts = [s for s in segs if s[1] >= t0]
                    for i, (sg, u0, u1) in enumerate(parts):
                        last = i == len(parts) - 1
                        act(hT[:, k, u0:u1], work[:, o + u0 - t0:o + u1 - t0], ACT.Identity,
                                     bias=mod[:, sh + k, sg:sg + 1], scale=dcol(ws + 2 * k + sg)).then_inc(act_norm.sem, act_norm.step(("h tile", l, which, k) if last else None))
                        eng.wait_ge(act_norm.sem, act_norm.n)
                act_norm.also(("h", l, which))

            rows = []

            def modulation(*place):
                for what in ADA_AT.get(place, ()):
                    if what is not None:
                        q = rows_at(what)
                        eng.wait_ge(mid_filled.sem, mid_filled.at("ada", *what))
                        if len(rows) > 1:
                            eng.wait_ge(out_filled.sem, out_filled.at("ada columns", *rows[-2]))
                        rows.append(what)
                        act(work[q, ROWS2:ROWS2 + BW], mid.get("ada", *what)[q, :], ACT.Copy).then_inc(
                            act_cond.sem, act_cond.step(("drained", "ada", *what)))
                        eng.wait_ge(act_cond.sem, act_cond.n)

            eng.wait_ge(loaded_vectors.sem, loaded_vectors.at("vectors"))
            act(dcol(D_CS, 16), par[:, L * NPL + 8:L * NPL + 24], ACT.Silu).then_inc(act_cond.sem, act_cond.step(("cond silu",)))
            eng.wait_ge(act_cond.sem, act_cond.n)
            eng.wait_ge(vec_cond.sem, vec_cond.at("lb centred"))
            act(dcol(D_TMP + 8, 16), dcol(D_TMP + 8, 16), ACT.Exp).then_inc(act_cond.sem, act_cond.step(("lb exp",)))
            eng.wait_ge(act_cond.sem, act_cond.n)
            eng.wait_ge(loaded_constants.sem, loaded_constants.at("constants"))
            for l in range(L):
                lo, w, m0 = first_query(l)
                act(dcol(D_LG, 8), pcol(l, "dec", 0, 8), ACT.Exp).then_inc(act_cond.sem, act_cond.step(("ret decay exp", l)))
                eng.wait_ge(act_cond.sem, act_cond.n)
                modulation("start", l)
                norm(l, 1)

                modulation("norm1", l)
                eng.dma_start(xscr, work[:, X:X + KT * N]).then_inc(x_saved.sem, x_saved.step(("x saved", l), 16))
                eng.wait_ge(vec_norm.sem, vec_norm.at("x scaled", l, 1, 7))
                eng.dma_start(wk(RT_CS, 1024), rcon[:, 0:1024]).then_inc(loaded_ret_constants.sem, loaded_ret_constants.step(None, 16))
                eng.dma_start(wk(RT_LAG, 2304), rcon[:, 1024:NRC]).then_inc(loaded_ret_constants.sem, loaded_ret_constants.step(("ret constants", l), 16))

                for what, c in ret_order:
                    qk = RT_QK + 1024 * (c % 2)
                    if what == "P":
                        for i, n in enumerate(("rq", "rk")):
                            eng.wait_ge(big_filled.sem, big_filled.at(n, l, c))
                            t0 = lo if n == "rq" else 0
                            act(wk(qk + 512 * i)[:, t0:N], big.get(n, l, c)[:, 0:N - t0], ACT.Copy).then_inc(act_ret.sem, act_ret.step(("drained", n, l, c)))
                            eng.wait_ge(act_ret.sem, act_ret.n)
                        if c == 0:
                            eng.wait_ge(loaded_ret_constants.sem, loaded_ret_constants.at("ret constants", l))
                            lg = lambda dd, h: dcol(D_LG + 4 * dd + h)
                            for h in range(4):
                                S, E = RT_STRIP + 768 * h, RT_A + 768 * h
                                act(wk(S, 384), wk(RT_LAG, 384), ACT.Exp, scale=lg(0, h)).then_inc(act_ret.sem, act_ret.step())
                                eng.wait_ge(act_ret.sem, act_ret.n)
                                act(wk(E, 384), wk(RT_LAG + 384, 384), ACT.Exp, scale=lg(1, h)).then_inc(act_ret.sem, act_ret.step())
                                eng.wait_ge(act_ret.sem, act_ret.n)
                                act(wk(S + 384, 384), wk(RT_LAG + 1536, 384), ACT.Exp, scale=lg(0, h)).then_inc(act_ret.sem, act_ret.step())
                                eng.wait_ge(act_ret.sem, act_ret.n)
                                act(wk(E + 384, 384), wk(RT_LAG + 1920, 384), ACT.Exp, scale=lg(1, h)).then_inc(act_ret.sem, act_ret.step(("strip exps", l, h)))
                                eng.wait_ge(act_ret.sem, act_ret.n)
                            modulation("strips", l)
                        eng.wait_ge(big_filled.sem, big_filled.at("rv", l, c))
                        act(wk(RT_V + 512 * (c % 2)), big.get("rv", l, c), ACT.Copy).then_inc(act_ret.sem, act_ret.step(("drained", "rv", l, c)))
                        eng.wait_ge(act_ret.sem, act_ret.n)
                        eng.wait_ge(big_filled.sem, big_filled.at("rg", l, c))
                        act(wk(Y[YR] + 512 * c)[:, lo:N], big.get("rg", l, c)[:, 0:w], ACT.Silu).then_inc(act_ret.sem, act_ret.step(("drained", "rg", l, c)))
                        eng.wait_ge(act_ret.sem, act_ret.n)
                    if what == "N":
                        eng.wait_ge(big_filled.sem, big_filled.at("rN", l, c))
                        rsqrt(act_ret, wk(RT_O + 1024)[:, lo:N], big.get("rN", l, c)[:, 0:w], 1.0 / P, "rms", ("ret rms", l, c), ("drained", "rN", l, c))

                eng.wait_ge(vec_ret.sem, vec_ret.at("ret y", l, 3))
                eng.dma_start(wk(RW_W, 2304), wsm[l]).then_inc(loaded_small_weights.sem, loaded_small_weights.step(("small weights", l), 16))

                def raw(i, ps, key):
                    if i != 12:
                        eng.wait_ge(vec_rwkv.sem, vec_rwkv.at("mixed", l, last_mixed[0]))
                    if wants_context(l, i):
                        act(wk(RW_SCR + 1, NC), ps[:, 0:NC], ACT.Copy).then_inc(act_rwkv.sem, act_rwkv.step())
                        eng.wait_ge(act_rwkv.sem, act_rwkv.n)
                        ps = ps[:, NC:N]
                    grid = wk(RW_SCR + 258, 396).rearrange("p (r t) -> p r t", t=66)[:, 1:5, 1:65]
                    act(grid, ps[:, 0:NC].rearrange("p (r t) -> p r t", t=GRID), ACT.Copy).then_inc(act_rwkv.sem, act_rwkv.step(key))
                    eng.wait_ge(act_rwkv.sem, act_rwkv.n)
                    act_rwkv.also(("raw", l, i))
                    last_mixed[0] = i

                last_mixed = [None]
                eng.wait_ge(pool_rwkv.sem, pool_rwkv.at("pads rwkv", l, -1))
                for j in range(3):
                    eng.wait_ge(big_filled.sem, big_filled.at("small", l, j))
                    raw(12 + j, big.get("small", l, j), ("drained", "small", l, j))
                if l > 0:
                    eng.wait_ge(big_filled.sem, big_filled.at("vd", l))
                    act(work[0:32, RW_VD:RW_VD + N], big.get("vd", l)[0:32, :], ACT.Copy).then_inc(act_rwkv.sem, act_rwkv.step(("drained", "vd", l)))
                    eng.wait_ge(act_rwkv.sem, act_rwkv.n)
                eng.wait_ge(vec_rwkv.sem, vec_rwkv.at("mixed", l, 12))
                act(wk(RW_SMALL), wk(RW_SMALL), ACT.Tanh).then_inc(act_rwkv.sem, act_rwkv.step())
                eng.wait_ge(act_rwkv.sem, act_rwkv.n)
                eng.wait_ge(vec_rwkv.sem, vec_rwkv.at("mixed", l, 14))
                act(wk(RW_SMALL + 1024)[:, lo:N], wk(RW_SMALL + 1024)[:, lo:N], ACT.Sigmoid).then_inc(act_rwkv.sem, act_rwkv.step(("small ready", l)))
                eng.wait_ge(act_rwkv.sem, act_rwkv.n)
                modulation("small", l)
                for c in range(NT):
                    if c > 0:
                        eng.wait_ge(pool_rwkv.sem, pool_rwkv.at("pads rwkv", l, c - 1))

                    def low_rank(d):
                        B = RW_D[d]
                        eng.wait_ge(big_filled.sem, big_filled.at("zw", l, c, d))
                        act(wk(B + WW), big.get("zw", l, c, d), ACT.Sigmoid, bias=pcol(l, "w0", 4 * d + c)).then_inc(act_rwkv.sem, act_rwkv.step(("drained", "zw", l, c, d)))
                        eng.wait_ge(act_rwkv.sem, act_rwkv.n)
                        act_rwkv.also(("decay sigmoid", l, c, d))
                        eng.wait_ge(big_filled.sem, big_filled.at("za", l, c, d))
                        act(wk(B + BT), big.get("za", l, c, d), ACT.Sigmoid, bias=pcol(l, "a0", 4 * d + c)).then_inc(act_rwkv.sem, act_rwkv.step(("drained", "za", l, c, d)))
                        eng.wait_ge(act_rwkv.sem, act_rwkv.n)
                        act_rwkv.also(("a sigmoid", l, c, d))

                    def project(j):
                        eng.wait_ge(big_filled.sem, big_filled.at("rkv", l, c, j))
                        raw(4 * j + c, big.get("rkv", l, c, j), ("drained", "rkv", l, c, j))

                    project(1)
                    low_rank(0)
                    low_rank(1)
                    for d in range(2):
                        B = RW_D[d]
                        eng.wait_ge(vec_rwkv.sem, vec_rwkv.at("decay sums", l, c, d))
                        act(wk(B + WW), wk(B + LT), ACT.Exp, scale=-DECAY).then_inc(act_rwkv.sem, act_rwkv.step())
                        eng.wait_ge(act_rwkv.sem, act_rwkv.n)
                        act(wk(B + ABT), wk(B + LT), ACT.Exp, scale=DECAY).then_inc(act_rwkv.sem, act_rwkv.step(("decays", l, c, d)))
                        eng.wait_ge(act_rwkv.sem, act_rwkv.n)
                    project(0)
                    eng.wait_ge(big_filled.sem, big_filled.at("kk norm", l, c))
                    rsqrt(act_rwkv, wk(RW_SQ), big.get("kk norm", l, c), 1.0, "l2", ("kk rms", l, c), ("drained", "kk norm", l, c))
                    project(2)
                    if l > 0:
                        eng.wait_ge(vec_rwkv.sem, vec_rwkv.at("mixed", l, 8 + c))
                        eng.wait_ge(big_filled.sem, big_filled.at("vgate", l, c))
                        act(wk(RW_SCR), big.get("vgate", l, c), ACT.Sigmoid, bias=pcol(l, "v0", c)).then_inc(act_rwkv.sem, act_rwkv.step(("drained", "vgate", l, c)))
                        eng.wait_ge(act_rwkv.sem, act_rwkv.n)
                        act_rwkv.also(("vgate sigmoid", l, c))
                    modulation("kk", l, c)
                    modulation("keys", l, c)
                    for d in range(2):
                        B = RW_D[d]
                        for n, dst in (("tkk", chunks(B + YK, 64, 64, 128)), ("tb", chunks(B + BTT)), ("tk", chunks(B + KTT))):
                            eng.wait_ge(mid_filled.sem, mid_filled.at(n, l, c, d))
                            act(dst, mid.get(n, l, c, d).rearrange("p (m t) -> p m t", t=64), ACT.Copy).then_inc(act_rwkv.sem, act_rwkv.step(("drained", n, l, c, d)))
                            eng.wait_ge(act_rwkv.sem, act_rwkv.n)
                    eng.wait_ge(mid_filled.sem, mid_filled.at("vT", l, c))
                    act(wk(RW_VT), mid.get("vT", l, c), ACT.Copy).then_inc(act_rwkv.sem, act_rwkv.step(("drained", "vT", l, c)))
                    eng.wait_ge(act_rwkv.sem, act_rwkv.n)
                    for d in range(2):
                        B = RW_D[d]
                        eng.wait_ge(mid_filled.sem, mid_filled.at("mv", l, c, d))
                        act(chunks(B + YK, 64, 0, 128), mid.get("mv", l, c, d).rearrange("p (m t) -> p m t", t=64),
                                     ACT.Copy).then_inc(act_rwkv.sem, act_rwkv.step(("drained", "mv", l, c, d)))
                        eng.wait_ge(act_rwkv.sem, act_rwkv.n)
                    for j in range(1, 6):
                        for d in range(2):
                            B = RW_D[d]
                            eng.wait_ge(mid_filled.sem, mid_filled.at("Z", l, c, d, j))
                            act(wk(B + MT), mid.get("Z", l, c, d, j), ACT.Copy).then_inc(act_rwkv.sem, act_rwkv.step(("drained", "Z", l, c, d, j)))
                            eng.wait_ge(act_rwkv.sem, act_rwkv.n)
                    for d in range(2):
                        B = RW_D[d]
                        eng.wait_ge(wide_filled.sem, wide_filled.at("uk", l, c, d))
                        act(wk(B + LT, 1024), wide.get("uk", l, c, d), ACT.Copy, scale=-1.0).then_inc(act_rwkv.sem, act_rwkv.step(("drained", "uk", l, c, d)))
                        eng.wait_ge(act_rwkv.sem, act_rwkv.n)
                    eng.wait_ge(big_filled.sem, big_filled.at("var", l, c))
                    rsqrt(act_rwkv, wk(RW_SCR + 1024)[:, lo:N], big.get("var", l, c)[:, 0:w], 1.0 / 64, "ln", ("rwkv rms", l, c),
                          ("drained", "var", l, c))

                eng.wait_ge(vec_rwkv.sem, vec_rwkv.at("drained", "gate", l, 3))
                for i in range(4):
                    eng.wait_ge(big_filled.sem, big_filled.at("hi", l, i))
                    act(wk(HG_V + 512 * i), big.get("hi", l, i), ACT.Copy).then_inc(act_hgrn.sem, act_hgrn.step(("drained", "hi", l, i)))
                    eng.wait_ge(act_hgrn.sem, act_hgrn.n)
                for h in range(4):
                    for dd in range(2):
                        eng.wait_ge(big_filled.sem, big_filled.at("hf", l, h, dd))
                        ps = big.get("hf", l, h, dd)
                        act(wk(HG_F + 2048 * dd + 512 * h), ps, ACT.Sigmoid).then_inc(act_hgrn.sem, act_hgrn.step())
                        eng.wait_ge(act_hgrn.sem, act_hgrn.n)
                        act(wk(HG_K + 2048 * dd + 512 * h), ps, ACT.Sigmoid, scale=-1.0).then_inc(act_hgrn.sem, act_hgrn.step(("drained", "hf", l, h, dd)))
                        eng.wait_ge(act_hgrn.sem, act_hgrn.n)
                        act_hgrn.also(("forget sigmoid", l, h, dd))
                    eng.wait_ge(big_filled.sem, big_filled.at("hf", l, h, 2))
                    if h >= 2:
                        eng.wait_ge(mid_filled.sem, mid_filled.at("hd", l, h - 2))
                    act(wk(HG_T + 512 * (h % 2))[:, lo:N], big.get("hf", l, h, 2)[:, 0:w], ACT.Silu).then_inc(act_hgrn.sem, act_hgrn.step(("drained", "hf", l, h, 2)))
                    eng.wait_ge(act_hgrn.sem, act_hgrn.n)
                    act_hgrn.also(("hq silu", l, h))
                    eng.wait_ge(big_filled.sem, big_filled.at("hf", l, h, 3))
                    act(wk(Y[YH] + 512 * h)[:, lo:N], big.get("hf", l, h, 3)[:, 0:w], ACT.Silu).then_inc(act_hgrn.sem, act_hgrn.step(("drained", "hf", l, h, 3)))
                    eng.wait_ge(act_hgrn.sem, act_hgrn.n)
                for h in range(4):
                    A = HG_A + 1536 * h
                    eng.wait_ge(mid_filled.sem, mid_filled.at("hl", l, h, 7))
                    ps = mid.get("hl", l, h, 7)
                    for i, o in enumerate((128, 512, 1152, 1280)):
                        if i < lo // P:
                            continue
                        act(wk(A + o, P), ps[:, P * i:P * i + P], ACT.Copy).then_inc(act_hgrn.sem, act_hgrn.step(("drained", "hl", l, h, 7) if i == 3 else None))
                        eng.wait_ge(act_hgrn.sem, act_hgrn.n)
                for h in range(4):
                    A = HG_A + 1536 * h
                    eng.wait_ge(mid_filled.sem, mid_filled.at("hl", l, h, 8))
                    ps = mid.get("hl", l, h, 8)
                    for i in range(2):
                        act(wk(A + 512 * i + 256, 256), ps[:, 256 * i:256 * i + 256], ACT.Copy).then_inc(act_hgrn.sem, act_hgrn.step(("drained", "hl", l, h, 8) if i else None))
                        eng.wait_ge(act_hgrn.sem, act_hgrn.n)
                for h in range(4):
                    eng.wait_ge(big_filled.sem, big_filled.at("hN", l, h))
                    rsqrt(act_hgrn, wk(HG_T + 512 + 512 * (h % 2))[:, lo:N], big.get("hN", l, h)[:, 0:w], 1.0 / P, "rms", ("hgrn rms", l, h),
                          ("drained", "hN", l, h))

                modulation("out", l)
                t0, t1 = rspan(l)
                n = t1 - t0
                eng.wait_ge(vec_hgrn.sem, vec_hgrn.at("y ready", l))
                eng.wait_ge(x_saved.sem, x_saved.at("x saved", l))
                if l == L - 1:
                    eng.dma_start(work[:, X:X + KT * N], xscr).then_inc(x_back.sem, x_back.step(("x back", l), 16))
                for f in range(KT):
                    for b in range(3):
                        i = 3 * f + b
                        eng.wait_ge(big_filled.sem, big_filled.at("ga", l, f, b))
                        if i >= 3:
                            eng.wait_ge(vec_merge.sem, vec_merge.at("drained", "br", l, (i - 3) // 3, (i - 3) % 3))
                        act(work[:, MG_T + 512 * (i % 3):MG_T + 512 * (i % 3) + n],
                                     big.get("ga", l, f, b)[:, 0:n], ACT.Sigmoid).then_inc(act_merge.sem, act_merge.step(("drained", "ga", l, f, b)))
                        eng.wait_ge(act_merge.sem, act_merge.n)
                        if b == 0 and l < L - 1 and f < KT - 1:
                            j = slot_at[("gb", l, f + 1)]
                            eng.wait_ge(weights[j % RING].sem, 16 * (j // RING + 1))
                            act(gate_whi[(f + 1) % 2][:, :], ring[:, j % RING, 0:3 * KT * P], ACT.Copy).then_inc(
                                act_merge.sem, act_merge.step(("gate weights high", l, f + 1)))
                            eng.wait_ge(act_merge.sem, act_merge.n)
                if l < L - 1:
                    eng.dma_start(work[:, X:X + KT * N], xscr).then_inc(x_back.sem, x_back.step(("x back", l), 16))
                norm(l, 2)
                modulation("norm2", l)
                for n_, (kind, _, a) in enumerate(mlp_slots(l) if l < L - 1 else ()):
                    if n_ < 15:
                        weights_high(l, n_ + 1)
                    for f in range(4 * a, 4 * a + 4) if kind == "m1" else ():
                        eng.wait_ge(vec_mlp.sem, vec_mlp.at("squared", l, f))
                        act(hidden_hi[:, f % 8, :], wk(HID_T + 512 * (f % 2)), ACT.Copy).then_inc(
                            act_mlp.sem, act_mlp.step(("hidden high", l, f)))
                        eng.wait_ge(act_mlp.sem, act_mlp.n)
                    if n_ == 1:
                        modulation("mlp", l)
                for f in range(32 if l == L - 1 else 0):
                    eng.wait_ge(big_filled.sem, big_filled.at("m1", l, f))
                    act(work[:, hid(f) + t0:hid(f) + t1], big.get("m1", l, f)[:, 0:n], ACT.Relu).then_inc(act_mlp.sem, act_mlp.step(("drained", "m1", l, f)))
                    eng.wait_ge(act_mlp.sem, act_mlp.n)
            norm(L - 1, 3)

        @block.gpsimd
        def _(eng):
            tt = nc.gpsimd.tensor_tensor
            eng.wait_ge(loaded_constants.sem, loaded_constants.at("constants"))
            for l in range(L):
                lo, w, m0 = first_query(l)
                for what, c in ret_order:
                    if what == "O":
                        eng.wait_ge(vec_ret.sem, vec_ret.at("drained", "rO", l, c))
                        if c > 0:
                            eng.wait_ge(big_filled.sem, big_filled.at("rN", l, c - 1))
                        tt(wk(RT_O + 512)[:, lo:N], wk(RT_O)[:, lo:N], wk(RT_O)[:, lo:N], ALU.mult).then_inc(pool_ret.sem, pool_ret.step(("ret squared", l, c)))
                        eng.wait_ge(pool_ret.sem, pool_ret.n)
                def pads(c):
                    nc.gpsimd.memset(wk(RW_SCR, 654), 0.0).then_inc(pool_rwkv.sem, pool_rwkv.step(("pads rwkv", l, c)))
                    eng.wait_ge(pool_rwkv.sem, pool_rwkv.n)

                def neighbours(i):
                    eng.wait_ge(act_rwkv.sem, act_rwkv.at("raw", l, i))
                    S = RW_SCR + 654
                    if wants_context(l, i):
                        tt(wk(S, NC), wk(RW_SCR, NC), wk(RW_SCR + 2, NC), ALU.add).then_inc(pool_rwkv.sem, pool_rwkv.step())
                        eng.wait_ge(pool_rwkv.sem, pool_rwkv.n)
                    grid = wk(RW_SCR + 258, 396).rearrange("p (r t) -> p r t", t=66)
                    s3 = wk(S + NC, NC).rearrange("p (r t) -> p r t", t=GRID)
                    tt(s3, grid[:, 0:4, 1:65], grid[:, 2:6, 1:65], ALU.add).then_inc(pool_rwkv.sem, pool_rwkv.step())
                    eng.wait_ge(pool_rwkv.sem, pool_rwkv.n)
                    tt(s3, s3, grid[:, 1:5, 0:64], ALU.add).then_inc(pool_rwkv.sem, pool_rwkv.step())
                    eng.wait_ge(pool_rwkv.sem, pool_rwkv.n)
                    tt(s3, s3, grid[:, 1:5, 2:66], ALU.add).then_inc(pool_rwkv.sem, pool_rwkv.step(("neighbours", l, i)))
                    eng.wait_ge(pool_rwkv.sem, pool_rwkv.n)

                eng.wait_ge(vec_ret.sem, vec_ret.at("ret y", l, 3))
                pads(-1)
                for j in range(3):
                    neighbours(12 + j)
                for c in range(NT):
                    neighbours(4 + c)
                    eng.wait_ge(vec_rwkv.sem, vec_rwkv.at("kk raw", l, c))
                    tt(wk(RW_SQ), wk(RW_KK), wk(RW_KK), ALU.mult).then_inc(pool_rwkv.sem, pool_rwkv.step(("kk squared", l, c)))
                    eng.wait_ge(pool_rwkv.sem, pool_rwkv.n)
                    neighbours(c)
                    for d in range(2):
                        B = RW_D[d]
                        eng.wait_ge(vec_rwkv.sem, vec_rwkv.at("a read", l, c, d))
                        eng.wait_ge(act_rwkv.sem, act_rwkv.at("decays", l, c, d))
                        tt(wk(B + BT), wk(B + BT), wk(B + ABT), ALU.mult).then_inc(pool_rwkv.sem, pool_rwkv.step())
                        eng.wait_ge(pool_rwkv.sem, pool_rwkv.n)
                    eng.wait_ge(vec_rwkv.sem, vec_rwkv.at("kk ready", l, c))
                    for d in range(2):
                        B = RW_D[d]
                        tt(wk(B + BT), wk(B + BT), wk(RW_KK), ALU.mult).then_inc(pool_rwkv.sem, pool_rwkv.step(("b ready", l, c, d)))
                        eng.wait_ge(pool_rwkv.sem, pool_rwkv.n)
                    neighbours(8 + c)
                    for j in range(1, 6):
                        for d in range(2):
                            B = RW_D[d]
                            if j == 1:
                                eng.wait_ge(mid_filled.sem, mid_filled.at("tk", l, c, d))
                                eng.wait_ge(vec_rwkv.sem, vec_rwkv.at("level", l, c, d, 0))
                            elif j == 2:
                                eng.wait_ge(mid_filled.sem, mid_filled.at("l1", l, c, d))
                                eng.wait_ge(vec_rwkv.sem, vec_rwkv.at("R first", l, c, d))
                            else:
                                eng.wait_ge(mid_filled.sem, mid_filled.at("Z", l, c, d, j - 2))
                            tt(chunks(B + (KTI if j % 2 else BT)), chunks(B + LT),
                                        over_chunks(kcol(K_LEV + 64 * j, 64), 64), ALU.mult).then_inc(pool_rwkv.sem, pool_rwkv.step(("level", l, c, d, j)))
                            eng.wait_ge(pool_rwkv.sem, pool_rwkv.n)
                    eng.wait_ge(vec_rwkv.sem, vec_rwkv.at("drained", "mean", l, c))
                    tt(wk(RW_SCR + 512)[:, lo:N], wk(RW_SCR)[:, lo:N], wk(RW_SCR)[:, lo:N], ALU.mult).then_inc(pool_rwkv.sem, pool_rwkv.step(("centred squared", l, c)))
                    eng.wait_ge(pool_rwkv.sem, pool_rwkv.n)
                    if c < NT - 1:
                        eng.wait_ge(vec_rwkv.sem, vec_rwkv.at("drained", "gate", l, c))
                        pads(c)
                eng.wait_ge(vec_rwkv.sem, vec_rwkv.at("drained", "gate", l, 3))
                for h in range(4):
                    nc.gpsimd.memset(wk(HG_A + 1536 * h, 1536), 0.0).then_inc(pool_hgrn.sem, pool_hgrn.step(("scores clear", l, h)))
                    eng.wait_ge(pool_hgrn.sem, pool_hgrn.n)
                for j in range(8):
                    for h in range(4):
                        eng.wait_ge(mid_filled.sem, mid_filled.at("hl", l, h, j))
                        b = 1 << j
                        for dd in range(2):
                            pair = lambda ap: ap.rearrange("p (n s b) -> p n s b", s=2, b=b)
                            side = dd
                            k = pair(wk(HG_K + 2048 * dd + 512 * h))[:, :, side, :]
                            fe = pair(wk(HG_F + 2048 * dd + 512 * h))[:, :, 1 - side, 0:1].broadcast_to([P, N // (2 * b), b])
                            tt(k, k, fe, ALU.mult).then_inc(pool_hgrn.sem, pool_hgrn.step(("hk up", l, h, j) if dd else None))
                            eng.wait_ge(pool_hgrn.sem, pool_hgrn.n)
                        eng.wait_ge(vec_hgrn.sem, vec_hgrn.at("hq up", l, h, j))
                        if j < 7:
                            for dd in range(2):
                                f = pair(wk(HG_F + 2048 * dd + 512 * h))
                                tt(f[:, :, 0, 0:1], f[:, :, 0, 0:1], f[:, :, 1, 0:1], ALU.mult).then_inc(pool_hgrn.sem, pool_hgrn.step(("F up", l, h, j) if dd else None))
                                eng.wait_ge(pool_hgrn.sem, pool_hgrn.n)
                for h in range(4):
                    eng.wait_ge(vec_hgrn.sem, vec_hgrn.at("drained", "hO", l, h))
                    if h >= 2:
                        eng.wait_ge(vec_hgrn.sem, vec_hgrn.at("hgrn y", l, h - 2))
                    o = HG_T + 1536 if h % 2 else HG_T
                    tt(wk(HG_T + 512 + 512 * (h % 2))[:, lo:N], wk(o)[:, lo:N], wk(o)[:, lo:N], ALU.mult).then_inc(pool_hgrn.sem, pool_hgrn.step(("hgrn squared", l, h)))
                    eng.wait_ge(pool_hgrn.sem, pool_hgrn.n)
                t0, t1 = rspan(l)
                for k in range(KT if l < L - 1 else 0):
                    nc.gpsimd.tensor_copy(gate_in_hi[:, k, :], hT[:, k, :]).then_inc(
                        pool_mlp.sem, pool_mlp.step(("gate input high", l, k)))
                    eng.wait_ge(pool_mlp.sem, pool_mlp.n)
                for k in range(KT if l < L - 1 else 0):
                    eng.wait_ge(act_norm.sem, act_norm.at("h tile", l, 2, k))
                    nc.gpsimd.tensor_copy(normed_hi[:, k, :], hT[:, k, :]).then_inc(
                        pool_mlp.sem, pool_mlp.step(("normed high", l, k)))
                    eng.wait_ge(pool_mlp.sem, pool_mlp.n)
                for f in range(32 if l == L - 1 else 0):
                    eng.wait_ge(act_mlp.sem, act_mlp.at("drained", "m1", l, f))
                    h_ = work[:, hid(f) + t0:hid(f) + t1]
                    tt(h_, h_, h_, ALU.mult).then_inc(pool_mlp.sem, pool_mlp.step(("hidden", l, f)))
                    eng.wait_ge(pool_mlp.sem, pool_mlp.n)

        @block.sync
        def _(eng):
            for i, (key, n) in enumerate(slots):
                if i >= RING and slots[i - RING][0][0] == "ada":
                    eng.wait_ge(mid_filled.sem, mid_filled.at(*slots[i - RING][0]))
                elif i >= RING:
                    eng.wait_ge(big_filled.sem, big_filled.at(*last_use(slots[i - RING][0])))
                eng.dma_start(ring[:, i % RING, 0:n], wts[i][:, 0:n]).then_inc(weights[i % RING].sem, weights[i % RING].step(None, 16))
            for k in range(KT):
                eng.wait_ge(vec_norm.sem, vec_norm.at("final", k))
                eng.dma_start(out[P * k:P * k + P, :], work[:, X + 512 * k + NC:X + 512 * k + N]).then_inc(stored.sem, stored.step(None, 16))
            eng.wait_ge(stored.sem, stored.n)
            eng.wait_ge(x_saved.sem, 16 * L)
    return log


def last_use(key):
    kind, l, *i = key
    return {"ret": lambda: ("rg", l, *i), "small": lambda: ("small", l, 2),
            "rw": lambda: ("rkv", l, *i, 2), "hi": lambda: ("hi", l, 3), "hf": lambda: ("hf", l, *i, 3),
            "gb": lambda: ("br", l, *i, 2), "out": lambda: ("ot", l, 4 * i[0] + 3),
            "m2q": lambda: ("m2", l, i[0] // 2, 4 * (i[0] % 2) + 3),
            "m1": lambda: ("m1", l, 4 * i[0] + 3), "m2": lambda: ("m2", l, *i)}[kind]()


def hid(f):
    return 512 * f if f < 12 else 14336 + 512 * (f - 12)


def wsm_up(work, wcol):
    return work[0:32, RW_W + 1792 + wcol.start:RW_W + 1792 + wcol.stop]


def HG_Q_of(dd, h):
    return HG_Q + 2048 * dd + 512 * h


def ident64(kc):
    return kc[:, K_ID2:K_ID2 + C].rearrange("p (a t) -> p a t", a=1).broadcast_to([P, M, C])


def scores_diag(work, h):
    A = HG_A + 1536 * h
    ctx = work[:, A:A + 1280].rearrange("p (i t) -> p i t", t=640)[:, :, 0:P]
    lat = work[:, A + 1024:A + 1024 + 768].rearrange("p (i t) -> p i t", t=384)[:, :, 0:P]
    return ctx, lat


def constants():
    k = np.zeros((P, NCONST), np.float32)
    p = np.arange(P)
    k[:, K_ID:K_ID + P] = np.eye(P)
    k[:, K_ONE:K_ONE + P] = 1
    k[:, K_BONE:K_BONE + P] = p[:, None] // 64 == p[None] // 64
    k[:, K_ROT:K_ROT + P] = 1.0 * (p[:, None] == p[None] - 64) - 1.0 * (p[:, None] == p[None] + 64)
    s, t = (p % 64)[:, None], np.arange(64)[None]
    k[:, K_STRICT:K_STRICT + 64], k[:, K_STRICT + 64:K_STRICT + 128] = s < t, s > t
    k[:, K_INCL:K_INCL + 64], k[:, K_INCL + 64:K_INCL + 128] = s <= t, s >= t
    for j in range(6):
        k[:, K_LEV + 64 * j:K_LEV + 64 * j + 64] = (s ^ t) >> j == 1
    for j in range(7):
        k[:, K_HLEV + P * j:K_HLEV + P * j + P] = (p[:, None] ^ p[None]) >> j == 1
    t = np.arange(N)
    k[:, K_SCAN:K_SCAN + N], k[:, K_SCAN + N:K_SCAN + 2 * N] = t % C != 0, t % C != C - 1
    k[:, K_EPS], k[:, K_EPS + 1], k[:, K_EPS + 2] = 1e-6, 64e-5, 1e-12
    k[:, K_ID2:K_ID2 + 64] = (p % 64)[:, None] == np.arange(64)[None]

    r = np.zeros((P, NRC), np.float32)
    half = P // 2
    inv = np.float32(10000.0) ** (-np.arange(half, dtype=np.float32) / np.float32(half))
    ang = np.arange(N, dtype=np.float32)[None] * inv[:, None]
    r[:, R_COS:R_COS + N] = np.tile(np.cos(ang), (2, 1))
    r[:, R_SIN:R_SIN + N] = np.tile(np.sin(ang), (2, 1))
    lag = np.arange(384)[None] - P - p[:, None]
    cross = lag + 2 * P
    for i, a in enumerate((np.maximum(lag, 0), np.maximum(-lag, 0), lag >= 0, lag <= 0, cross, N - cross)):
        r[:, R_LAG + 384 * i:R_LAG + 384 * i + 384] = a
    return k, r


def lay_out(inp):
    slots = schedule_slots()
    w = np.zeros((len(slots), P, SLOT), np.float32)

    def tiles(m):
        return m.reshape(m.shape[0] // P, P, m.shape[1] // P, P).transpose(1, 2, 0, 3)

    rw = np.cumsum([0, BW, BW, BW, 128, 128, 128])
    ret0 = int(rw[-1])
    hg0 = ret0 + 4 * BW
    ga0 = hg0 + 5 * BW
    for i, ((kind, l, *a), n) in enumerate(slots):
        wi = inp["w_in"][l]
        cut = lambda o: wi[:, o:o + P]
        if kind == "ada":
            m = inp["ada_w"][l][:, BW * a[0]:BW * a[0] + BW].reshape(KT, P, BW).transpose(1, 0, 2)
        elif kind == "ret":
            m = tiles(np.concatenate([cut(ret0 + BW * j + P * a[0]) for j in range(4)], 1))
        elif kind == "small":
            m = tiles(wi[:, 3 * BW:3 * BW + 3 * P])
        elif kind == "rw":
            m = tiles(np.concatenate([cut(BW * j + P * a[0]) for j in range(3)], 1))
        elif kind == "hi":
            m = wi[:, hg0 + 3 * BW:hg0 + 4 * BW].reshape(KT, P, BW).transpose(1, 0, 2)
        elif kind == "hf":
            m = tiles(np.concatenate([cut(hg0 + BW * j + P * a[0]) for j in (1, 2, 0, 4)], 1))
        elif kind == "gb":
            gates = tiles(np.concatenate([cut(ga0 + D * b + P * a[0]) for b in range(3)], 1)).reshape(P, -1)
            outs = [tiles(inp["w_branch"][l, b][:, P * a[0]:P * a[0] + P]).reshape(P, -1) for b in range(3)]
            m = np.concatenate([gates] + outs, 1)
        elif kind == "out":
            m = tiles(inp["w_out"][l][:, 4 * P * a[0]:4 * P * a[0] + 4 * P])
        elif kind == "m1":
            m = tiles(inp["mlp_w1"][l][:, 4 * P * a[0]:4 * P * a[0] + 4 * P])
        elif kind == "m2q":
            q, g = divmod(a[0], 2)
            m = tiles(inp["mlp_w2"][l][D * q:D * q + D, BW * g:BW * g + BW])
        else:
            m = tiles(inp["mlp_w2"][l][:, P * a[0]:P * a[0] + P])
        w[i, :, :n] = m.reshape(P, n)

    small = np.zeros((L, P, 2304), np.float32)
    for l in range(L):
        small[l, :, 0:512] = inp["rwkv_w_up"][l].reshape(P, BW)
        small[l, :, 512:1024] = inp["rwkv_a_up"][l].reshape(P, BW)
        small[l, :, 1024:1536] = inp["rwkv_g_up"][l]
        if l:
            small[l, :, 1536:1792] = inp["rwkv_v_down"][l - 1].reshape(KT, P, 32).transpose(1, 0, 2).reshape(P, 256)
            small[l, 0:32, 1792:2304] = inp["rwkv_v_up"][l - 1]

    vec = np.zeros((P, NPAR), np.float32)
    col = lambda a: np.asarray(a).reshape(-1, P).T
    for l in range(L):
        got = dict(mu=inp["rwkv_mu"][l], w0=inp["rwkv_w0"][l], a0=inp["rwkv_a0"][l], kk=inp["rwkv_k_k"][l],
                   ka=inp["rwkv_k_a"][l], rk=inp["rwkv_r_k"][l], lnw=inp["rwkv_lnx_w"][l], lnb=inp["rwkv_lnx_b"][l],
                   lb=inp["hgrn_lb"][l], hnw=inp["hgrn_norm_w"][l], n1=inp["norm1_w"][l], n2=inp["norm2_w"][l],
                   adab=inp["ada_b"][l])
        if l:
            got["v0"] = inp["rwkv_v0"][l - 1]
        for name, a in got.items():
            vec[:, l * NPL + COL[name]:l * NPL + COL[name] + PARTS[name]] = col(a)
        vec[:, l * NPL + COL["dec"]:l * NPL + COL["dec"] + 8] = inp["ret_decay"][l].reshape(1, 8)
    vec[:, L * NPL:L * NPL + 8] = col(inp["final_norm_w"])
    cond = np.stack([inp["c_ctx"], inp["c"][0]])
    vec[:, L * NPL + 8:] = cond.reshape(2, KT, P).transpose(2, 1, 0).reshape(P, 16)
    x = np.concatenate([inp["ctx"][0], inp["x"][0]], 0)
    x = x.T.reshape(KT, P, N).transpose(1, 0, 2).reshape(P, KT * N)
    con, rcon = constants()
    return dict(weights=w, small_weights=small, vectors=vec, constants=con, ret_constants=rcon,
                x=np.ascontiguousarray(x))


def kernel(**inputs):
    import concourse.bacc as bacc
    from concourse.bass_utils import run_bass_kernel_spmd

    inp = {k: np.asarray(v) for k, v in inputs.items()}
    arrays = lay_out(inp)

    def program(known):
        nc = bacc.Bacc("TRN2", target_bir_lowering=False, num_devices=1)
        a = {k: nc.dram_tensor(f"in_{k}", v.shape, F32, kind="ExternalInput").ap() for k, v in arrays.items()}
        xscr = nc.dram_tensor("x_scratch", (P, KT * N), F32, kind="Internal").ap()
        out = nc.dram_tensor("out", (D, N - NC), F32, kind="ExternalOutput").ap()
        marks = build_program(nc, known, a["weights"], a["small_weights"], a["vectors"], a["constants"],
                              a["ret_constants"], a["x"], xscr, out)
        return nc, marks

    _, marks = program(None)
    nc, _ = program(marks)
    r = run_bass_kernel_spmd(nc, [{f"in_{k}": v for k, v in arrays.items()}], core_ids=[0])
    return np.ascontiguousarray(r.results[0]["out"].T)[None]
```
